# Optimizing a Trainium2 kernel written in Bass

```python
import math
import jax, jax.numpy as jnp
from jax import lax
import numpy as np

D_MODEL = 1024
BATCH = 1
SEQ = 256
DEPTH = 2

CHUNK = 128
N_SGU_GROUPS = 8
SGU_WIDTH = D_MODEL
SGU_GROUP = SGU_WIDTH // N_SGU_GROUPS
DIFF_HEAD_DIM = 64
N_DIFF_HEADS = D_MODEL // (2 * DIFF_HEAD_DIM)
DIFF_QK_WIDTH = N_DIFF_HEADS * 2 * DIFF_HEAD_DIM
DIFF_V_WIDTH = N_DIFF_HEADS * 2 * DIFF_HEAD_DIM
Q_BLOCK = 128
ROPE_THETA = 10000.0
N_BRANCH = 2
IN_WIDTH = 2 * SGU_WIDTH + 2 * DIFF_QK_WIDTH + DIFF_V_WIDTH + N_BRANCH * D_MODEL
SPLITS = [SGU_WIDTH, 2 * SGU_WIDTH, 2 * SGU_WIDTH + DIFF_QK_WIDTH,
          2 * SGU_WIDTH + 2 * DIFF_QK_WIDTH,
          2 * SGU_WIDTH + 2 * DIFF_QK_WIDTH + DIFF_V_WIDTH]
D_FF = 2816
ALPHA = (2.0 * DEPTH) ** 0.25
BETA = (8.0 * DEPTH) ** -0.25
LN_EPS = 1e-5


def _lambda_init(layer):
    return 0.8 - 0.6 * math.exp(-0.3 * layer)

def _layernorm(x, g, b):
    xf = x.astype(jnp.float32)
    mu = jnp.mean(xf, axis=-1, keepdims=True)
    var = jnp.mean(jnp.square(xf - mu), axis=-1, keepdims=True)
    y = (xf - mu) * lax.rsqrt(var + LN_EPS)
    return (y * g.astype(jnp.float32) + b.astype(jnp.float32)).astype(x.dtype)

def _rmsnorm(x, g):
    xf = x.astype(jnp.float32)
    y = xf * lax.rsqrt(jnp.mean(jnp.square(xf), axis=-1, keepdims=True) + LN_EPS)
    return (y * g.astype(jnp.float32)).astype(x.dtype)

def _swiglu(x, w1, w3, w2):
    return (jax.nn.silu(x @ w1) * (x @ w3)) @ w2

def _rope(x, cos, sin):
    c = cos[None, :, None, None, :]
    s = sin[None, :, None, None, :]
    xf = x.astype(jnp.float32)
    x1, x2 = jnp.split(xf, 2, axis=-1)
    out = jnp.concatenate([x1 * c - x2 * s, x2 * c + x1 * s], axis=-1)
    return out.astype(x.dtype)

def _chunked_sgu(u, v, g, b, w_s, b_s):
    bsz, seq, _ = v.shape
    v = _layernorm(v, g, b)
    n_chunks = seq // CHUNK
    vb = v.reshape(bsz, n_chunks, CHUNK, N_SGU_GROUPS, SGU_GROUP)
    causal = jnp.tril(jnp.ones((CHUNK, CHUNK), dtype=bool))
    w = jnp.where(causal[None], w_s, jnp.zeros((), w_s.dtype))
    s = jnp.einsum('gtr,bnrgc->bntgc', w, vb) + b_s.T[None, None, :, :, None]
    return u * s.reshape(bsz, seq, SGU_WIDTH).astype(u.dtype)

def _diff_attention(q, k, v, lam):
    bsz, seq = q.shape[:2]
    n_blocks = seq // Q_BLOCK
    qb = q.reshape(bsz, n_blocks, Q_BLOCK, N_DIFF_HEADS, 2, DIFF_HEAD_DIM).swapaxes(0, 1)
    k_pos = jnp.arange(seq)
    scale = DIFF_HEAD_DIM ** -0.5
    neg = jnp.finfo(jnp.float32).min

    def one_block(args):
        q_blk, i = args
        s = jnp.einsum('bqhmd,bkhmd->bhmqk', q_blk, k).astype(jnp.float32) * scale
        q_pos = i * Q_BLOCK + jnp.arange(Q_BLOCK)
        mask = k_pos[None, :] <= q_pos[:, None]
        s = jnp.where(mask, s, neg)
        p = jax.nn.softmax(s, axis=-1)
        a = p[:, :, 0] - lam * p[:, :, 1]
        return jnp.einsum('bhqk,bkhe->bqhe', a.astype(v.dtype), v)

    out = lax.map(one_block, (qb, jnp.arange(n_blocks)))
    return out.swapaxes(0, 1).reshape(bsz, seq, N_DIFF_HEADS, 2 * DIFF_HEAD_DIM)

def _mixer(x, layer, w_in, gate_b, sgu_ln_g, sgu_ln_b, sgu_w, sgu_b, lam, diff_ln_g,
           w_branch, w_out, cos, sin):
    bsz, seq, _ = x.shape
    z = x @ w_in
    u, v, q, k, val, gates = jnp.split(z, SPLITS, axis=-1)
    u = jax.nn.gelu(u, approximate=False)
    v = jax.nn.gelu(v, approximate=False)
    h_a = _chunked_sgu(u, v, sgu_ln_g, sgu_ln_b, sgu_w, sgu_b)
    q = _rope(q.reshape(bsz, seq, N_DIFF_HEADS, 2, DIFF_HEAD_DIM), cos, sin)
    k = _rope(k.reshape(bsz, seq, N_DIFF_HEADS, 2, DIFF_HEAD_DIM), cos, sin)
    val = val.reshape(bsz, seq, N_DIFF_HEADS, 2 * DIFF_HEAD_DIM)
    lam_init = _lambda_init(layer)
    lf = lam.astype(jnp.float32)
    lam_full = (jnp.exp(jnp.sum(lf[0] * lf[1])) - jnp.exp(jnp.sum(lf[2] * lf[3]))
                + lam_init)
    o = _diff_attention(q, k, val, lam_full)
    o = _rmsnorm(o, diff_ln_g) * (1.0 - lam_init)
    h_b = o.reshape(bsz, seq, DIFF_V_WIDTH)
    g = jax.nn.sigmoid(gates.reshape(bsz, seq, N_BRANCH, D_MODEL) + gate_b)
    m = g[:, :, 0] * (h_a @ w_branch[0]) + g[:, :, 1] * (h_b @ w_branch[1])
    return m @ w_out

def first_inputs(seed: int = 0) -> dict:
    key = jax.random.key(seed)
    ks = jax.random.split(key, 20)
    f32 = jnp.float32
    nrm = lambda k, shape, s: jax.random.normal(k, shape, f32) * s
    x = jax.random.normal(ks[0], (BATCH, SEQ, D_MODEL), f32)
    w_in = nrm(ks[1], (DEPTH, D_MODEL, IN_WIDTH), D_MODEL ** -0.5)
    gate_b = nrm(ks[2], (DEPTH, N_BRANCH, D_MODEL), 0.02)
    sgu_ln_g = 1.0 + nrm(ks[3], (DEPTH, SGU_WIDTH), 0.02)
    sgu_ln_b = nrm(ks[4], (DEPTH, SGU_WIDTH), 0.02)
    sgu_w = nrm(ks[5], (DEPTH, N_SGU_GROUPS, CHUNK, CHUNK), CHUNK ** -0.5)
    sgu_b = 1.0 + nrm(ks[6], (DEPTH, N_SGU_GROUPS, CHUNK), 0.02)
    lam = nrm(ks[7], (DEPTH, 4, DIFF_HEAD_DIM), 0.1)
    diff_ln_g = 1.0 + nrm(ks[8], (DEPTH, 2 * DIFF_HEAD_DIM), 0.02)
    w_branch = jnp.concatenate([
        nrm(ks[9], (DEPTH, 1, SGU_WIDTH, D_MODEL), BETA * SGU_WIDTH ** -0.5),
        nrm(ks[10], (DEPTH, 1, DIFF_V_WIDTH, D_MODEL), BETA * DIFF_V_WIDTH ** -0.5)], axis=1)
    w_out = nrm(ks[11], (DEPTH, D_MODEL, D_MODEL), BETA * D_MODEL ** -0.5)
    ffn_w1 = nrm(ks[12], (DEPTH, 2, D_MODEL, D_FF), D_MODEL ** -0.5)
    ffn_w3 = nrm(ks[13], (DEPTH, 2, D_MODEL, D_FF), D_MODEL ** -0.5)
    ffn_w2 = nrm(ks[14], (DEPTH, 2, D_FF, D_MODEL), BETA * D_FF ** -0.5)
    ln_g = 1.0 + nrm(ks[15], (DEPTH, 3, D_MODEL), 0.02)
    ln_b = nrm(ks[16], (DEPTH, 3, D_MODEL), 0.02)
    return {"x": x, "w_in": w_in, "gate_b": gate_b, "sgu_ln_g": sgu_ln_g,
            "sgu_ln_b": sgu_ln_b, "sgu_w": sgu_w, "sgu_b": sgu_b, "lam": lam,
            "diff_ln_g": diff_ln_g, "w_branch": w_branch, "w_out": w_out,
            "ffn_w1": ffn_w1, "ffn_w3": ffn_w3, "ffn_w2": ffn_w2,
            "ln_g": ln_g, "ln_b": ln_b}

def first_block(x, w_in, gate_b, sgu_ln_g, sgu_ln_b, sgu_w, sgu_b, lam, diff_ln_g,
              w_branch, w_out, ffn_w1, ffn_w3, ffn_w2, ln_g, ln_b):
    seq = x.shape[1]
    pos = jnp.arange(seq, dtype=jnp.float32)
    inv_freq = ROPE_THETA ** (-jnp.arange(0, DIFF_HEAD_DIM, 2, dtype=jnp.float32) / DIFF_HEAD_DIM)
    ang = pos[:, None] * inv_freq[None, :]
    cos, sin = jnp.cos(ang), jnp.sin(ang)
    for l in range(DEPTH):
        h = _swiglu(x, ffn_w1[l, 0], ffn_w3[l, 0], ffn_w2[l, 0])
        x = _layernorm(ALPHA * x + 0.5 * h, ln_g[l, 0], ln_b[l, 0])
        h = _mixer(x, l, w_in[l], gate_b[l], sgu_ln_g[l], sgu_ln_b[l], sgu_w[l], sgu_b[l],
                   lam[l], diff_ln_g[l], w_branch[l], w_out[l], cos, sin)
        x = _layernorm(ALPHA * x + h, ln_g[l, 1], ln_b[l, 1])
        h = _swiglu(x, ffn_w1[l, 1], ffn_w3[l, 1], ffn_w2[l, 1])
        x = _layernorm(ALPHA * x + 0.5 * h, ln_g[l, 2], ln_b[l, 2])
    return x


CHUNK_2 = 64
HEAD_DIM = 64
NORM_EPS = 1e-6
D_RWKV = D_MODEL // 2
N_RWKV_HEADS = D_RWKV // HEAD_DIM
D_CONV = D_MODEL // 2
CONV_WIDTH = 31
LORA_DECAY = 64
LORA_ICLR = 64
LORA_GATE = 128
GN_EPS = 1e-5 * HEAD_DIM
CONV_LN_EPS = 1e-5
COLS_RWKV = 3 * D_RWKV + LORA_DECAY + LORA_ICLR + LORA_GATE
COLS_A = COLS_RWKV + 2 * D_CONV
N_FOX_HEADS = D_MODEL // HEAD_DIM
D_FOX = N_FOX_HEADS * HEAD_DIM
COLS_C = 4 * D_FOX + N_FOX_HEADS
N_A_LAYERS = (DEPTH + 1) // 2
N_C_LAYERS = DEPTH // 2


def rms_norm(x, g):
    xf = x.astype(jnp.float32)
    y = xf * lax.rsqrt(jnp.mean(xf * xf, axis=-1, keepdims=True) + NORM_EPS)
    return (y * g.astype(jnp.float32)).astype(x.dtype)

def layer_norm(x, g, b, eps):
    xf = x.astype(jnp.float32)
    mu = jnp.mean(xf, axis=-1, keepdims=True)
    xc = xf - mu
    y = xc * lax.rsqrt(jnp.mean(xc * xc, axis=-1, keepdims=True) + eps)
    return (y * g.astype(jnp.float32) + b.astype(jnp.float32)).astype(x.dtype)

def swiglu(x, w_gate, w_up, w_down):
    return (jax.nn.silu(x @ w_gate) * (x @ w_up)) @ w_down

def split_cols(t, sizes):
    out, start = [], 0
    for s in sizes:
        out.append(t[..., start:start + s])
        start += s
    return out

def rwkv7_scan(r, w, k, v, kk, a):
    b, _, h, n = r.shape

    def step(state, inp):
        r_t, w_t, k_t, v_t, kk_t, a_t = inp
        s_kk = jnp.einsum('bhvk,bhk->bhv', state, kk_t)
        state = (state * w_t[:, :, None, :]
                 - s_kk[..., None] * (kk_t * a_t)[:, :, None, :]
                 + v_t[..., None] * k_t[:, :, None, :])
        y_t = jnp.einsum('bhvk,bhk->bhv', state, r_t)
        return state, y_t

    xs = tuple(jnp.moveaxis(t, 1, 0) for t in (r, w, k, v, kk, a))
    s0 = jnp.zeros((b, h, n, n), jnp.float32)
    _, ys = lax.scan(step, s0, xs)
    return jnp.moveaxis(ys, 0, 1)

def mixer_ab(h, w_in, shift_mu, decay_up, decay_base, iclr_up, iclr_base, gate_up,
             k_k, k_a, r_k, lnx_g, lnx_b, conv_w, conv_b, conv_ln_g, conv_ln_b, w_out):
    b, t, _ = h.shape
    f32 = jnp.float32
    proj = h @ w_in
    p = proj[..., :COLS_RWKV]
    p_prev = jnp.pad(p, ((0, 0), (1, 0), (0, 0)))[:, :-1]
    p = p + shift_mu * (p_prev - p)
    r, k, v, d_w, d_a, d_g = split_cols(p, [D_RWKV, D_RWKV, D_RWKV, LORA_DECAY, LORA_ICLR, LORA_GATE])
    w_log = -jax.nn.softplus(-(decay_base + jnp.tanh(d_w) @ decay_up)) - 0.5
    decay = jnp.exp(-jnp.exp(w_log.astype(f32)))
    a = jax.nn.sigmoid(iclr_base + d_a @ iclr_up).astype(f32)
    g = jax.nn.sigmoid(d_g) @ gate_up
    r = r.astype(f32)
    k = k.astype(f32)
    v = v.astype(f32)
    kk = (k * k_k.astype(f32)).reshape(b, t, N_RWKV_HEADS, HEAD_DIM)
    kk = kk * lax.rsqrt(jnp.maximum(jnp.sum(kk * kk, axis=-1, keepdims=True), 1e-24))
    k = k * (1.0 + (a - 1.0) * k_a.astype(f32))
    hs = lambda z: z.reshape(b, t, N_RWKV_HEADS, HEAD_DIM)
    rh, kh, vh = hs(r), hs(k), hs(v)
    y = rwkv7_scan(rh, hs(decay), kh, vh, kk, hs(a))
    mu = jnp.mean(y, axis=-1, keepdims=True)
    yc = y - mu
    y = yc * lax.rsqrt(jnp.mean(yc * yc, axis=-1, keepdims=True) + GN_EPS)
    y = y.reshape(b, t, D_RWKV) * lnx_g.astype(f32) + lnx_b.astype(f32)
    bonus = jnp.sum(rh * kh * r_k.astype(f32), axis=-1, keepdims=True) * vh
    y_a = ((y + bonus.reshape(b, t, D_RWKV)) * g.astype(f32)).astype(h.dtype)
    c_val, c_gate = split_cols(proj[..., COLS_RWKV:], [D_CONV, D_CONV])
    glu = c_val * jax.nn.sigmoid(c_gate)
    conv = lax.conv_general_dilated(
        glu, conv_w[:, None, :], window_strides=(1,), padding=[(CONV_WIDTH - 1, 0)],
        dimension_numbers=('NWC', 'WIO', 'NWC'), feature_group_count=D_CONV) + conv_b
    y_b = jax.nn.silu(layer_norm(conv, conv_ln_g, conv_ln_b, CONV_LN_EPS))
    return jnp.concatenate([y_a, y_b], axis=-1) @ w_out

def mixer_c(h, w_in, forget_bias, q_norm_g, k_norm_g, w_out):
    b, t, _ = h.shape
    f32 = jnp.float32
    proj = h @ w_in
    q, k, v, gate, f_logit = split_cols(proj, [D_FOX, D_FOX, D_FOX, D_FOX, N_FOX_HEADS])
    q = rms_norm(q.reshape(b, t, N_FOX_HEADS, HEAD_DIM), q_norm_g) * (HEAD_DIM ** -0.5)
    k = rms_norm(k.reshape(b, t, N_FOX_HEADS, HEAD_DIM), k_norm_g)
    v = v.reshape(b, t, N_FOX_HEADS, HEAD_DIM)
    log_f = jax.nn.log_sigmoid((f_logit + forget_bias).astype(f32))
    cum = jnp.transpose(jnp.cumsum(log_f, axis=1), (0, 2, 1))
    outs = []
    for blk in range(t // Q_BLOCK):
        q0 = blk * Q_BLOCK
        k_end = q0 + Q_BLOCK
        s = jnp.einsum('bqhd,bkhd->bhqk', q[:, q0:k_end], k[:, :k_end],
                       preferred_element_type=f32)
        s = s + cum[:, :, q0:k_end, None] - cum[:, :, None, :k_end]
        q_pos = q0 + jnp.arange(Q_BLOCK)
        mask = q_pos[:, None] >= jnp.arange(k_end)[None, :]
        prob = jax.nn.softmax(jnp.where(mask, s, -jnp.inf), axis=-1)
        outs.append(jnp.einsum('bhqk,bkhd->bqhd', prob.astype(v.dtype), v[:, :k_end]))
    o = jnp.concatenate(outs, axis=1).reshape(b, t, D_FOX)
    o = o * jax.nn.sigmoid(gate)
    return o @ w_out

def second_inputs(seed: int = 0) -> dict:
    key = jax.random.key(seed)
    ks = list(jax.random.split(key, 40))

    def nrm(i, shape, scale):
        return scale * jax.random.normal(ks[i], shape, jnp.float32)

    def uni(i, shape, lo, hi):
        return jax.random.uniform(ks[i], shape, jnp.float32, minval=lo, maxval=hi)

    na, nc = N_A_LAYERS, N_C_LAYERS
    return {
        "x": nrm(0, (BATCH, SEQ, D_MODEL), 1.0),
        "norm_gains": 1.0 + nrm(1, (DEPTH, 6, D_MODEL), 0.02),
        "ffn_w_gate": nrm(2, (DEPTH, 2, D_MODEL, D_FF), D_MODEL ** -0.5),
        "ffn_w_up": nrm(3, (DEPTH, 2, D_MODEL, D_FF), D_MODEL ** -0.5),
        "ffn_w_down": nrm(4, (DEPTH, 2, D_FF, D_MODEL), D_FF ** -0.5),
        "a_w_in": nrm(5, (na, D_MODEL, COLS_A), D_MODEL ** -0.5),
        "a_shift_mu": uni(6, (na, COLS_RWKV), 0.0, 1.0),
        "a_decay_up": nrm(7, (na, LORA_DECAY, D_RWKV), 0.1),
        "a_decay_base": uni(8, (na, D_RWKV), -6.0, 1.0),
        "a_iclr_up": nrm(9, (na, LORA_ICLR, D_RWKV), 0.5 * LORA_ICLR ** -0.5),
        "a_iclr_base": nrm(10, (na, D_RWKV), 0.5),
        "a_gate_up": nrm(11, (na, LORA_GATE, D_RWKV), LORA_GATE ** -0.5),
        "a_k_k": 0.85 + nrm(12, (na, D_RWKV), 0.05),
        "a_k_a": 1.0 + nrm(13, (na, D_RWKV), 0.05),
        "a_r_k": nrm(14, (na, N_RWKV_HEADS, HEAD_DIM), 0.1),
        "a_lnx_g": 1.0 + nrm(15, (na, D_RWKV), 0.02),
        "a_lnx_b": nrm(16, (na, D_RWKV), 0.02),
        "b_conv_w": nrm(17, (na, CONV_WIDTH, D_CONV), CONV_WIDTH ** -0.5),
        "b_conv_b": nrm(18, (na, D_CONV), 0.02),
        "b_ln_g": 1.0 + nrm(19, (na, D_CONV), 0.02),
        "b_ln_b": nrm(20, (na, D_CONV), 0.02),
        "ab_w_out": nrm(21, (na, D_RWKV + D_CONV, D_MODEL), (D_RWKV + D_CONV) ** -0.5),
        "c_w_in": nrm(22, (nc, D_MODEL, COLS_C), D_MODEL ** -0.5),
        "c_forget_bias": 2.0 + nrm(23, (nc, N_FOX_HEADS), 0.5),
        "c_q_norm_g": 1.0 + nrm(24, (nc, HEAD_DIM), 0.02),
        "c_k_norm_g": 1.0 + nrm(25, (nc, HEAD_DIM), 0.02),
        "c_w_out": nrm(26, (nc, D_FOX, D_MODEL), D_FOX ** -0.5),
    }

def second_block(x, norm_gains, ffn_w_gate, ffn_w_up, ffn_w_down,
              a_w_in, a_shift_mu, a_decay_up, a_decay_base, a_iclr_up, a_iclr_base, a_gate_up,
              a_k_k, a_k_a, a_r_k, a_lnx_g, a_lnx_b,
              b_conv_w, b_conv_b, b_ln_g, b_ln_b, ab_w_out,
              c_w_in, c_forget_bias, c_q_norm_g, c_k_norm_g, c_w_out):
    for layer in range(DEPTH):
        g = norm_gains[layer]
        f = swiglu(rms_norm(x, g[0]), ffn_w_gate[layer, 0], ffn_w_up[layer, 0], ffn_w_down[layer, 0])
        x = x + 0.5 * rms_norm(f, g[1])
        h = rms_norm(x, g[2])
        i = layer // 2
        if layer % 2 == 0:
            m = mixer_ab(h, a_w_in[i], a_shift_mu[i], a_decay_up[i], a_decay_base[i],
                         a_iclr_up[i], a_iclr_base[i], a_gate_up[i], a_k_k[i], a_k_a[i],
                         a_r_k[i], a_lnx_g[i], a_lnx_b[i], b_conv_w[i], b_conv_b[i],
                         b_ln_g[i], b_ln_b[i], ab_w_out[i])
        else:
            m = mixer_c(h, c_w_in[i], c_forget_bias[i], c_q_norm_g[i], c_k_norm_g[i], c_w_out[i])
        x = x + rms_norm(m, g[3])
        f = swiglu(rms_norm(x, g[4]), ffn_w_gate[layer, 1], ffn_w_up[layer, 1], ffn_w_down[layer, 1])
        x = x + 0.5 * rms_norm(f, g[5])
    return x


def setup_inputs(seed=0):
    out = dict(first_inputs(seed))
    for name, value in second_inputs(seed + 1).items():
        if name != "x":
            out[name + "_2"] = value
    return out


def reference(
    x, w_in, gate_b, sgu_ln_g, sgu_ln_b, sgu_w, sgu_b, lam, diff_ln_g, w_branch, w_out, ffn_w1,
    ffn_w3, ffn_w2, ln_g, ln_b, norm_gains_2, ffn_w_gate_2, ffn_w_up_2, ffn_w_down_2, a_w_in_2,
    a_shift_mu_2, a_decay_up_2, a_decay_base_2, a_iclr_up_2, a_iclr_base_2, a_gate_up_2,
    a_k_k_2, a_k_a_2, a_r_k_2, a_lnx_g_2, a_lnx_b_2, b_conv_w_2, b_conv_b_2, b_ln_g_2, b_ln_b_2,
    ab_w_out_2, c_w_in_2, c_forget_bias_2, c_q_norm_g_2, c_k_norm_g_2, c_w_out_2,
):
    x = first_block(
        x, w_in, gate_b, sgu_ln_g, sgu_ln_b, sgu_w, sgu_b, lam, diff_ln_g, w_branch, w_out,
        ffn_w1, ffn_w3, ffn_w2, ln_g, ln_b,
    )
    return second_block(
        x, norm_gains_2, ffn_w_gate_2, ffn_w_up_2, ffn_w_down_2, a_w_in_2, a_shift_mu_2,
        a_decay_up_2, a_decay_base_2, a_iclr_up_2, a_iclr_base_2, a_gate_up_2, a_k_k_2, a_k_a_2,
        a_r_k_2, a_lnx_g_2, a_lnx_b_2, b_conv_w_2, b_conv_b_2, b_ln_g_2, b_ln_b_2, ab_w_out_2,
        c_w_in_2, c_forget_bias_2, c_q_norm_g_2, c_k_norm_g_2, c_w_out_2,
    )


_drawn_inputs = setup_inputs


def setup_inputs(seed=0):
    import zlib

    import numpy as np

    out = dict(_drawn_inputs(seed))
    spreads = {}
    factors = {'gate_b': 8.0,
     'sgu_ln_g': 8.0,
     'sgu_ln_b': 8.0,
     'sgu_b': 8.0,
     'diff_ln_g': 8.0,
     'a_lnx_g_2': 4.812,
     'a_lnx_b_2': 3.525,
     'b_ln_g_2': 3.396,
     'b_ln_b_2': 3.613,
     'c_q_norm_g_2': 7.673,
     'c_k_norm_g_2': 8.0}
    for name, (base, spread) in spreads.items():
        noise = np.random.default_rng([zlib.crc32(name.encode()), seed]).standard_normal(out[name].shape)
        drawn = base * np.exp(spread * noise) if base else spread * noise
        out[name] = __import__('jax').numpy.asarray(drawn.astype(out[name].dtype))
    for name, factor in factors.items():
        out[name] = (out[name] * factor).astype(out[name].dtype)
    return out
```

```python
import math
from contextlib import ExitStack, contextmanager

import numpy as np
import concourse.bass as bass
import concourse.mybir as mybir

P = 128
T = 256
TB = T // P
D = 1024
KT = D // P
FF = 2816
STEP = 256
STEPS = FF // STEP
DEPTH = 2
HALF = 512
SLOTS = 4
UNIT = 2048
LN_EPS = 1e-5
RMS_EPS = 1e-6
ALPHA = (2.0 * DEPTH) ** 0.25
GROUPS = 8
DHEADS = 8
HD = 64
ROPE_THETA = 10000.0
NEG = -1e30
IN1 = 7168
COL_U, COL_Q, COL_V, COL_G = 0, 2048, 4096, 5120
RH = 8
CH = 16
NCH = T // CH
LORA = 256
RW = 512
CONV = 31
GN_EPS = 1e-5 * HD
FOX = 16
DECAY = -math.exp(-0.5)

STARTED = [f"{n}{s}" for n in ("lo", "used") for s in range(SLOTS)] + [
    "gen0", "gen1", "x_ready", "s_ready", "a_ready", "o_out", "m_new", "y_out", "sq_free"]


class Counts:

    def __init__(self, engine, held):
        self.engine, self.held, self.loops = engine, held, []
        self.seen = {n: 1 for n in STARTED}

    def so_far(self, name):
        v = self.seen.get(name, 0)
        for i, per_pass in self.loops:
            if per_pass.get(name, 0):
                v = i * per_pass[name] + v
        return v

    def count(self, name, k=1):
        self.seen[name] = self.seen.get(name, 0) + k

    def next(self, name, k=1):
        self.count(name, k)
        return self.so_far(name)

    def hold(self):
        self.engine.sem_inc(self.held, 1)

    @contextmanager
    def loop(self, n, which):
        per_pass = PER_PASS.get(which, {})
        before = dict(self.seen)
        self.hold()
        with self.engine.Fori(0, n) as i:
            self.loops.append((i, per_pass))
            yield i
            self.loops.pop()
        grew = {k: v - before.get(k, 0) for k, v in self.seen.items() if v != before.get(k, 0)}
        assert grew == per_pass, (which, grew)
        for k, v in grew.items():
            self.seen[k] = before.get(k, 0) + n * v


PER_PASS = {
    "sp ffn": {"lo0": 1, "lo1": 1, "lo2": 1},
    "sp four": {"lo0": 1, "lo1": 1, "lo2": 1, "lo3": 1},
    "sp layer": {"lo0": 32, "lo1": 32, "lo2": 32, "lo3": 10},
    "pool att": {"s_ready": 4},
    "pool layer": {"var": 8, "x_ready": 6, "qk_ready": 8, "s_ready": 8, "o_var": 1, "m_ready": 1},
    "act ffn": {"ld0": 32, "used0": 1, "ld1": 32, "used1": 1, "ht_tr": 1, "ld2": 16, "used2": 1},
        "act uv": {"ld0": 16, "used0": 1, "ld1": 16, "used1": 1, "ld2": 16, "used2": 1, "gen0": 1, "gen1": 1, "ld3":
        16, "used3": 1},
        "act qk": {"ld0": 16, "used0": 1, "ld1": 16, "used1": 1, "ld2": 16, "used2": 1, "gen0": 1, "gen1": 1, "ld3":
        16, "used3": 1, "rope_tr": 4},
        "act att": {"ld0": 16, "used0": 1, "ld1": 16, "used1": 1, "ld2": 16, "used2": 1, "gen0": 1, "gen1": 1,
        "ld3": 16, "used3": 1, "smax": 4, "a_ready": 4, "a_tr": 4, "o_ready": 4, "o_out": 4},
        "act layer": {"ld0": 864, "used0": 32, "ld1": 864, "used1": 32, "tr": 24, "ht_tr": 22, "ld2": 512, "used2":
        32, "gen0": 12, "gen1": 12, "ld3": 160, "used3": 10, "lam_s": 1, "rope_tr": 8, "smax": 8, "a_ready": 8,
        "a_tr": 8, "o_ready": 8, "o_out": 8},
    "dve ffn": {"hi0": 1, "used0": 1, "hi1": 1, "used1": 1, "h_silu": 2, "ht_hi": 1, "hi2": 1, "used2": 1},
        "dve uv": {"hi0": 1, "used0": 1, "hi1": 1, "used1": 1, "hi2": 1, "used2": 1, "hi3": 1, "used3": 1, "gen0":
        1, "gen1": 1},
        "dve qk": {"hi0": 1, "used0": 1, "hi1": 1, "used1": 1, "hi2": 1, "used2": 1, "hi3": 1, "used3": 1, "dve": 2,
        "gen0": 1, "gen1": 1, "rope": 4},
        "dve att": {"hi0": 1, "used0": 1, "hi1": 1, "used1": 1, "hi2": 1, "used2": 1, "hi3": 1, "used3": 1, "dve":
        12, "gen0": 1, "gen1": 1, "s_ready": 4, "e_ready": 16},
        "dve layer": {"hi0": 32, "used0": 32, "hi1": 32, "used1": 32, "xt_hi": 24, "h_silu": 44, "ht_hi": 22, "hi2":
        32, "used2": 32, "hi3": 10, "used3": 10, "dve": 64, "gen0": 12, "gen1": 12, "gains_ld": 128, "rstd": 8,
        "x_ready": 6, "sgu_ld": 96, "rope": 8, "lam_e": 1, "sgw_tr": 2, "sgu_mm": 2, "s_ready": 8, "e_ready": 32,
        "o_sq": 1, "o_rstd": 1, "gate_on": 2},
    "pe ffn": {"lo0": 1, "lo1": 1, "h_ready": 1, "ht_ready": 1, "lo2": 1},
    "pe uv": {"lo0": 1, "lo1": 1, "gen0": 1, "gen1": 1, "lo2": 1, "lo3": 1},
    "pe qk": {"lo0": 1, "lo1": 1, "gen0": 1, "gen1": 1, "lo2": 1, "lo3": 1, "rope": 4, "qk_ready": 4},
        "pe att": {"lo0": 1, "lo1": 1, "gen0": 1, "gen1": 1, "lo2": 1, "lo3": 1, "qh_ready": 8, "a_ready": 4,
        "aT_ready": 4, "o_out": 4},
        "pe layer": {"xt_ready": 24, "lo0": 32, "lo1": 32, "h_ready": 22, "gen0": 12, "gen1": 12, "ht_ready": 22,
        "lo2": 32, "x_ready": 6, "lo3": 10, "rope": 8, "qk_ready": 8, "sgu_ld": 96, "sgw_ready": 2, "v_ready": 2,
        "ha_ready": 2, "qh_ready": 16, "a_ready": 8, "aT_ready": 8, "o_out": 8, "hb_ready": 1, "m_ready": 1},
    "pool scan": {"m_new": 1},
    "pool qk": {"fss_ready": 4},
    "pool fox": {"s_ready": 4},
    "act scan": {"rkab_tr": 1, "rT_tr": 1, "pw_mm": 3, "aT_mm": 1, "y_mm": 1},
        "act fqk": {"used0": 1, "used1": 1, "used2": 1, "used3": 1, "gen0": 1, "gen1": 1, "sq_free": 4, "ld0": 16,
        "ld1": 16, "ld2": 16, "ld3": 16, "rope_tr": 4},
    "act fox": {"used0": 1, "used1": 1, "gen0": 1, "ld0": 16, "ld1": 16, "smax": 4, "eT_tr": 4},
    "dve conv": {"dve": 1},
        "dve scan": {"m_new": 1, "gram_mm": 1, "gram_ready": 1, "inv_ready": 4, "inv_mm": 3, "tlk_mm": 1, "u_mm": 1,
        "m_mm": 1},
        "dve fqk": {"used0": 1, "used1": 1, "used2": 1, "used3": 1, "gen0": 1, "gen1": 1, "sq_free": 4, "hi0": 1,
        "hi1": 1, "hi2": 1, "hi3": 1, "dve": 2, "rope": 4, "fsq": 4, "frs_ready": 4},
        "dve fox": {"used0": 1, "used1": 1, "gen0": 1, "s_ready": 4, "o_out": 4, "hi0": 1, "hi1": 1, "e_ready": 16,
        "o_ready": 4, "rinv": 4, "eT1_tr": 4},
        "pe scan": {"m_new": 1, "y_out": 1, "rkab_ready": 1, "exp_ready": 4, "rkabT_ready": 1, "gram_ready": 1,
        "pw_ready": 3, "inv_ready": 4, "aTs_ready": 1, "tlk_ready": 1, "rT_ready": 1, "u_ready": 1},
    "pe qk2": {"lo0": 1, "lo1": 1, "lo2": 1, "lo3": 1, "gen0": 1, "gen1": 1, "rope": 4, "qk_ready": 4},
        "pe fox": {"lo0": 1, "lo1": 1, "gen0": 1, "o_out": 4, "qh_ready": 12, "aT_ready": 4, "e_ready": 16,
        "eT1_ready": 4},
}

USED = ("x", "w_in", "gate_b", "sgu_ln_g", "sgu_ln_b", "sgu_w", "sgu_b", "lam", "diff_ln_g", "w_branch", "w_out",
        "ffn_w1", "ffn_w3", "ffn_w2", "ln_g", "ln_b",
        "norm_gains_2", "ffn_w_gate_2", "ffn_w_up_2", "ffn_w_down_2", "a_w_in_2", "a_shift_mu_2",
        "a_decay_up_2", "a_decay_base_2", "a_iclr_up_2", "a_iclr_base_2", "a_gate_up_2", "a_k_k_2", "a_k_a_2",
        "a_r_k_2", "a_lnx_g_2", "a_lnx_b_2", "b_conv_w_2", "b_conv_b_2", "b_ln_g_2", "b_ln_b_2", "ab_w_out_2",
        "c_w_in_2", "c_forget_bias_2", "c_q_norm_g_2", "c_k_norm_g_2", "c_w_out_2")


def program(nc, a, out):
    f32, f32r, bf16 = mybir.dt.float32, mybir.dt.float32r, mybir.dt.bfloat16
    ACT = mybir.ActivationFunctionType
    ALU = mybir.AluOpType
    X = mybir.AxisListType.X
    ds = bass.ds
    ctx = ExitStack()
    ctx.enter_context(nc.allow_non_contiguous_dma("small parameters"))

    def sb(name, shape, dt=f32):
        return ctx.enter_context(nc.sbuf_tensor(name, shape, dt))

    wf = [sb(f"wf{s}", [P, UNIT]) for s in range(SLOTS)]
    wh = [sb(f"wh{s}", [P, UNIT], f32r) for s in range(SLOTS)]
    wl = [sb(f"wl{s}", [P, UNIT], f32r) for s in range(SLOTS)]
    xTh = sb("xTh", [P, KT, T], f32r)
    xTl = sb("xTl", [P, KT, T], f32r)
    x = sb("x", [P, TB, D])
    y = sb("y", [P, TB, D])
    hTh = sb("hTh", [P, 2, T], f32r)
    hTl = sb("hTl", [P, 2, T], f32r)
    hid = sb("hid", [P, TB, STEP])
    sil = sb("sil", [P, TB, STEP])
    gains = sb("gains", [P, 2, D])
    ident = sb("ident", [P, P])
    mhalf = sb("mhalf", [P, P + 1])
    scale = mhalf[:, P:P + 1]
    stats = sb("stats", [P, 2, 6])
    mv = sb("mv", [P, TB, 2])
    ve = sb("ve", [P, TB])
    rstd = sb("rstd", [P, TB])
    ssq = sb("ssq", [P, 4])
    arena = sb("arena", [P, 15360])
    bank = [ctx.enter_context(nc.psum_tensor(f"bank{i}", [P, HALF], f32)) for i in range(8)]

    def part(at, *shape):
        n = int(np.prod(shape))
        assert at + n <= 15360
        v = arena[:, at:at + n]
        if len(shape) == 2:
            return v.rearrange("p (a b) -> p a b", a=shape[0])
        if len(shape) == 3:
            return v.rearrange("p (a b c) -> p a b c", a=shape[0], b=shape[1])
        if len(shape) == 4:
            return v.rearrange("p (a b c d) -> p a b c d", a=shape[0], b=shape[1], c=shape[2])
        return v

    u_t = part(0, TB, D)
    v_t = part(2048, TB, D)
    uv = part(0, 2, TB, D)
    qkT = part(4096, 2, DHEADS, T)
    val = part(8192, TB, D)
    sgu_gb = part(10240, 2, D)
    sgu_w = part(12288, GROUPS, P)
    sgu_wT = part(13312, GROUPS, P)
    rope1 = hid[:, :, :].rearrange("p b n -> p (b n)")
    rope2 = sil[:, :, :].rearrange("p b n -> p (b n)")
    qh, kh = hid[:, 0, :], hid[:, 1, :]
    osq = part(4096, TB, D)
    gate = (v_t, part(10240, TB, D))
    e_t = part(12288, 2, 384)
    a_t = part(13056, 384)
    aT = part(13440, 3, P)
    att = part(13824, 64)
    oss = part(13888, 16)
    orstd = part(13904, 16)
    sgu_bT = part(14336, GROUPS)
    cs = part(14344, 2, TB, HD)
    tri = part(14600, P)
    lam_t = part(14728, 4, HD)
    lam_c = part(14984, 4)
    laminit = part(14988, DEPTH, 2)
    dgain = part(14992, P)
    negm_f, identb_f = part(15120, P), part(15248, 64)
    negm_wide, identb = negm_f.bitcast(bf16), identb_f.bitcast(bf16)
    negm = negm_wide[:, P:T]

    names = []

    def new(*ns):
        names.extend(ns)

    new("held", "const_ld", "x_ld")
    for s in range(SLOTS):
        new(f"ld{s}", f"hi{s}", f"lo{s}", f"used{s}")
    new("h_silu", "h_ready", "ht_tr", "ht_hi", "ht_ready")
    new("tr", "xt_hi", "xt_ready", "x_ready", "gen0", "gen1")
    new("var", "rstd", "gains_ld", "dve", "act", "pool")
    new("sgu_ld", "sgu_var", "sgu_rstd", "v_ready", "sgw_tr", "sgw_ready", "sgu_mm", "ha_ready")
    new("rope", "rope_tr", "qk_ready", "val_ready")
    new("s_ready", "smax", "e_ready", "a_ready", "a_tr", "aT_ready", "o_ready", "o_out", "e_free")
    new("o_var", "o_rstd", "o_sq", "hb_ready", "gate_on", "m_ready", "lam_e", "lam_s", "qh_ready", "out_st")
    new("sq", "x_new", "done", "ab_ld", "z_st", "lp_ld", "rkv_ld", "glu_ready", "cgb_ld", "kk_var", "kk_rstd")
    new("mixed", "sag_ready", "sag_st", "sag_ld", "e_done", "m_new", "rkab_ready", "exp_ready", "yr_ready")
    new("y_st", "y_ld", "c_ld", "fss_ready", "frs_ready", "cw_tr", "cw_ready", "glu_tr", "gluT_ready", "lmix")
    new("lora_ready", "lora_tr", "loraT_ready", "ups_ready", "sa_ready", "tot_ready", "pc_ready", "cum_ready")
    new("e_exp", "conv_n", "yb_ready", "rkab_tr", "rkabT_ready", "rT_tr", "rT_ready", "pw_mm", "pw_ready")
    new("aT_mm", "aTs_ready", "y_mm", "y_out", "sq_free", "fsq", "fabs", "fln", "eT_tr", "conv_done", "convT")
    new("gram_mm", "gram_ready", "inv_mm", "inv_ready", "tlk_mm", "tlk_ready", "u_mm", "u_ready", "m_mm")
    new("flog_ready", "cum_mm", "cumT_ready", "rinv", "eT1_tr", "eT1_ready")
    SEM = {n: ctx.enter_context(nc.semaphore(n)) for n in names}
    block = ctx.enter_context(nc.Block())

    def bcast_row(ap, n):
        return bass.AP(tensor=ap.tensor, offset=ap.offset, ap=[[0, P], [1, n]])


    rows_t = part(0, 9, NCH, HD)
    ROW_V, ROW_R, ROW_K, ROW_SIG, ROW_A, ROW_G, ROW_6, ROW_7, ROW_8 = range(9)
    st_rkv = part(6144, 3, TB, RW)
    st_sag = part(6144, 3, TB, RW)
    glu = part(9216, TB, RW)
    y_conv = part(9216, TB, RW)
    cgate = part(10240, TB, RW)
    conv_gb = part(10240, 2, RW)
    convw_rows = part(11264, RW)
    gluT = part(11264, 4, CONV - 1 + T)
    conv_o = part(12408, 4, T)
    sag_base = part(12408, 2, RW)
    lora = part(13432, TB, LORA)
    lora_prev = part(13944, TB, LORA)
    loraT = part(14456, 2, T)
    convw = part(14968, 4, 32)
    lora_up = hid[:, :, :].rearrange("p b n -> p (b n)")
    gate_up = sil[:, :, :].rearrange("p b n -> p (b n)")
    gflat = gains[:, :, :].rearrange("p a n -> p (a n)")
    cum_mask = gflat[:, 0:384].rearrange("p (a b) -> p a b", a=3)
    gram_mask = gflat[:, 384:1024].rearrange("p (a b) -> p a b", a=5)
    head_mask = gflat[:, 1024:1032]
    chunk_mask = gflat[:, 1032:1040]
    mu_rows = gflat[:, 1040:1232].rearrange("p (a b) -> p a b", a=3)
    row_par = gflat[:, 1232:1552].rearrange("p (a b) -> p a b", a=5)
    mu_lora = gflat[:, 1552:1808]
    small = gflat[:, 1808:1888].rearrange("p (a b) -> p a b", a=5)
    bonus = small[:, 0, :]
    pc = gflat[:, 1888:1952].rearrange("p (j c) -> p j c", j=4)
    yflat = y[:, :, :].rearrange("p b n -> p (b n)")
    a_exp, r_exp, kt_exp, bt_exp = (yflat[:, i * 512:(i + 1) * 512] for i in range(4))
    rkabT = part(13432, 512)
    gram = part(11264, 5, P)
    pw = part(11904, 5, P)
    inv = part(12544, P)
    tlk = part(12672, P)
    aT_s = part(12800, 4, P)
    rT_s = part(13944, 4, P)
    state = part(14456, 4, HD)
    sdec = part(14712, 4, HD)
    u_s = part(13312, HD)
    rkab = part(10240, 4, HD)
    y_rwkv = part(6144, TB, RW)
    fqkT = part(0, 2, 8, T)
    fval = part(4096, TB, D)
    fgate = part(6144, TB, D)
    sel = part(8192, FOX, T)
    fe_t = part(12288, 2, 384)
    feT = part(13056, 2, 3, P)
    fatt = part(13824, 32)
    cumT = part(13856, 2, T)
    fbias = part(14368, FOX)
    flog = part(14384, TB, FOX)
    fabs = part(14416, TB, FOX)
    qk_gain = part(14448, 2, HD)
    tri_c = part(14576, P)
    ones_c = part(14704, P)
    fss = part(14832, 8)
    frs = part(14840, 8)
    selh = sil
    z_rows = nc.dram_tensor("z_rows", (3, (T + 1) * RH, HD), f32, kind="Internal").ap()
    lora_rows = nc.dram_tensor("lora_rows", (T + 1, LORA), f32, kind="Internal").ap()
    sag_rows = nc.dram_tensor("sag_rows", (3, T * RH, HD), f32, kind="Internal").ap()
    y_rows = nc.dram_tensor("y_rows", (T * RH, HD), f32, kind="Internal").ap()

    def by_chunk(r):
        return r.rearrange("(c p) n -> p c n", p=P)

    def by_token(r):
        return r.rearrange("(b p h) n -> p b (h n)", b=TB, h=RH)

    def second_sp(c, sp, ffn, half_panel, load, rows):
        w1, w3, w2 = a["ffn_w_gate_2"], a["ffn_w_up_2"], a["ffn_w_down_2"]
        ffn(w1[0, 0], w3[0, 0], w2[0, 0])
        wa = a["a_w_in_2"][0]
        for s, col in ((0, 0), (1, 0), (3, 512), (2, 512), (0, 1024), (1, 1024), (2, 1536), (3, 1536), (0, 2048), (1, 2048)):
            half_panel(wa, col, s, s % 2)
        load(2, (wf[2][:, :].rearrange("p (k n) -> p k n", k=KT), rows(wa)[:, :, 2560:2816]))
        for s in range(4):
            half_panel(a["ab_w_out_2"][0], HALF * (s // 2), s, s % 2)
        ffn(w1[0, 1], w3[0, 1], w2[0, 1])
        ffn(w1[1, 0], w3[1, 0], w2[1, 0])
        wc = a["c_w_in_2"][0]
        for s in (0, 1, 3, 2):
            half_panel(wc, HALF * (s // 2), s, s % 2)
        for s in range(4):
            half_panel(wc, D + HALF * (s // 2), s, s % 2)
        for s in range(4):
            half_panel(wc, 2 * D + HALF * (s // 2), s, s % 2)
        load(0, (wf[0][:, 0:KT * FOX].rearrange("p (k n) -> p k n", k=KT), rows(wc)[:, :, 4 * D:4 * D + FOX]))
        for i in range(2):
            for h in range(2):
                half_panel(wc, 3 * D + i * HALF, h, h)
        for s in range(4):
            half_panel(a["c_w_out_2"][0], HALF * (s // 2), s, s % 2)
        ffn(w1[1, 1], w3[1, 1], w2[1, 1])
        sp.wait_ge(SEM["done"], c.next("done", TB))
        sp.dma_start(out[0].rearrange("(b p) n -> p b n", p=P), x[:, :, :]).then_inc(SEM["out_st"], 16)
        sp.wait_ge(SEM["out_st"], c.next("out_st", 16))

    def second_pool(c, pool, gains_load, power, norm):
        g2 = a["norm_gains_2"]
        copy = pool.tensor_copy

        def two_norms(l, post, pre_l, pre):
            gains_load(g2[l, post:post + 1, :], g2[pre_l, pre:pre + 1, :])
            norm()
            norm()
            pool.wait_ge(SEM["x_ready"], c.next("x_ready", TB))

        for p in range(2):
            c.count(f"gen{p}", 12 * DEPTH + 1)
        pool.wait_ge(SEM["x_ready"], c.so_far("x_ready"))
        gains_load(g2[0, 0:1, :], g2[0, 0:1, :])
        norm()
        pool.wait_ge(SEM["x_ready"], c.next("x_ready", TB))
        two_norms(0, 1, 0, 2)
        def per_row(name, at):
            t = a[name]
            return bass.AP(tensor=t.tensor, offset=t.offset + at, ap=[[0, CH], [HD, RH], [1, HD]])
        loads = [(gflat[:, 0:1040], a["c_masks"]), (mu_lora, bcast_row(a["a_shift_mu_2"][0:1, 1536:1792], LORA)),
                 (lora_up[0:64, :], a["a_decay_up_2"][0]), (lora_up[64:128, :], a["a_iclr_up_2"][0]),
                 (gate_up, a["a_gate_up_2"][0]),
                 (sag_base[:, 0, :], bcast_row(a["a_decay_base_2"], RW)), (sag_base[:, 1, :], bcast_row(a["a_iclr_base_2"], RW)),
                 (convw_rows[0:31, :], a["b_conv_w_2"][0]), (convw_rows[31:32, :], a["b_conv_b_2"])]
        for j, col in enumerate((1024, 0, 512)):
            loads.append((mu_rows[:, j, :], per_row("a_shift_mu_2", col)))
        for j, n in enumerate(("a_k_k_2", "a_k_a_2", "a_r_k_2", "a_lnx_g_2", "a_lnx_b_2")):
            loads.append((row_par[:, j, :], per_row(n, 0)))
        for dst, src in loads:
            pool.dma_start(dst, src).then_inc(SEM["ab_ld"], 16)
        pool.memset(lora_prev[0:1, :, :], 0.0).then_inc(SEM["pool"], 1)
        pool.wait_ge(SEM["pool"], c.next("pool"))
        zero = lora_prev[0:1, :, :].rearrange("p b n -> p (b n)")
        for j in range(3):
            pool.dma_start(z_rows[j, 0:RH, :].rearrange("(o h) n -> o (h n)", o=1), zero).then_inc(SEM["z_st"], 16)
        pool.dma_start(lora_rows[0:1, :], zero[:, 0:LORA]).then_inc(SEM["z_st"], 16)
        for j, p in ((1, 0), (2, 1), (0, 0)):
            pool.wait_ge(SEM[f"gen{p}"], c.next(f"gen{p}"))
            pool.dma_start(by_token(z_rows[j, RH:, :]), st_rkv[:, j, :, :]).then_inc(SEM["z_st"], 16)
        pool.wait_ge(SEM["gen1"], c.next("gen1"))
        pool.dma_start(lora_rows[1:, :].rearrange("(b p) n -> p b n", p=P), lora).then_inc(SEM["z_st"], 16)
        pool.wait_ge(SEM["z_st"], c.next("z_st", 16 * 8))
        pool.dma_start(lora_prev, lora_rows[0:T, :].rearrange("(b p) n -> p b n", p=P)).then_inc(SEM["lp_ld"], 16)
        for j in range(3):
            pool.dma_start(rows_t[:, j, :, :], by_chunk(z_rows[j, RH:, :])).then_inc(SEM["rkv_ld"], 16)
            pool.dma_start(rows_t[:, 3 + j, :, :], by_chunk(z_rows[j, 0:T * RH, :])).then_inc(SEM["rkv_ld"], 16)
        pool.wait_ge(SEM["glu_ready"], c.next("glu_ready"))
        for i, n in enumerate(("b_ln_g_2", "b_ln_b_2")):
            pool.dma_start(conv_gb[:, i, :], bcast_row(a[n], RW)).then_inc(SEM["cgb_ld"], 16)
        pool.wait_ge(SEM["mixed"], c.next("mixed"))
        pool.wait_ge(SEM["sag_ready"], c.next("sag_ready", 2))
        for j in range(3):
            pool.dma_start(by_token(sag_rows[j]), st_sag[:, j, :, :]).then_inc(SEM["sag_st"], 16)
        pool.wait_ge(SEM["sag_st"], c.next("sag_st", 48))
        for j in range(3):
            pool.dma_start(rows_t[:, 3 + j, :, :], by_chunk(sag_rows[j])).then_inc(SEM["sag_ld"], 16)
        norm()
        power(small[:, 1, :], small[:, 2, :], 16, "kk_var", "kk_rstd")
        pool.wait_ge(SEM["e_done"], c.next("e_done"))
        def expand(dst, j, i):
            src = rows_t[:, j, ds(i, 1), :].broadcast_to([P, RH, HD])
            pool.tensor_tensor(dst.rearrange("p (h n) -> p h n", h=RH), src,
                               head_mask.rearrange("p (h a) -> p h a", a=1).broadcast_to([P, RH, HD]), ALU.mult)\
                .then_inc(SEM["exp_ready"], 1)
        c.count("m_new")
        with c.loop(NCH, "pool scan") as i:
            pool.wait_ge(SEM["m_new"], c.so_far("m_new"))
            c.count("m_new")
            copy(rkab, rows_t[:, 1:5, ds(i, 1), :].rearrange("p j a n -> p j (a n)")).then_inc(SEM["rkab_ready"], 1)
            expand(r_exp, ROW_R, i)
            expand(a_exp, ROW_SIG, i)
            expand(kt_exp, ROW_6, i)
            expand(bt_exp, ROW_7, i)
        power(small[:, 1, :], small[:, 2, :], 16, "kk_var", "kk_rstd")
        pool.wait_ge(SEM["yr_ready"], c.next("yr_ready"))
        pool.dma_start(by_chunk(y_rows), rows_t[:, ROW_8, :, :]).then_inc(SEM["y_st"], 16)
        pool.wait_ge(SEM["y_st"], c.next("y_st", 16))
        pool.dma_start(y_rwkv, by_token(y_rows)).then_inc(SEM["y_ld"], 16)
        two_norms(0, 3, 0, 4)
        two_norms(0, 5, 1, 0)
        two_norms(1, 1, 1, 2)
        for dst, src in ((sel[0:FOX, :, :], a["c_sel"]), (fbias, bcast_row(a["c_forget_bias_2"], FOX)),
                         (qk_gain[:, 0, :], bcast_row(a["c_q_norm_g_2"], HD)),
                         (qk_gain[:, 1, :], bcast_row(a["c_k_norm_g_2"], HD)),
                         (tri_c, a["c_tri"]), (ones_c, a["c_ones"])):
            pool.dma_start(dst, src).then_inc(SEM["c_ld"], 16)
        with c.loop(2, "pool qk") as i:
            for r in range(4):
                power(frs, fss, 8, "fss_ready", "frs_ready")
        pool.wait_ge(SEM["qk_ready"], c.next("qk_ready", 8))
        pool.wait_ge(SEM["c_ld"], c.next("c_ld", 16 * 6))
        with c.loop(2, "pool fox") as i:
            for hp in range(4):
                pool.wait_ge(SEM["s_ready"], c.so_far("s_ready"))
                c.count("s_ready")
                head = [fqkT[:, w, ds(i * 4 + hp, 1), :].rearrange("p a t -> p (a t)") for w in range(2)]
                pool.tensor_tensor(qh, head[0], scale.broadcast_to([P, T]), ALU.mult).then_inc(SEM["qh_ready"], 1)
                copy(kh, head[1]).then_inc(SEM["qh_ready"], 1)
                copy(selh[0:FOX, :, :], sel[0:FOX, ds(i * 8 + hp * 2, 2), :]).then_inc(SEM["qh_ready"], 1)
        two_norms(1, 3, 1, 4)
        gains_load(g2[1, 5:6, :], g2[1, 5:6, :])
        norm()

    def second_act(c, act, prep, next_units, panel_evac, transposed, ffn):
        def square_sums(bank_of, name):
            act.wait_ge(SEM[name], c.so_far(name))
            for b in range(TB):
                for h in range(2):
                    act.activation(y[:, b, h * HALF:(h + 1) * HALF], bank[2 * b + h][:, :], ACT.Square,
                                   accum_out=ssq[:, 2 * b + h:2 * b + h + 1]).then_inc(SEM["sq"], 1)

        def pre():
            for b in range(TB):
                act.wait_ge(SEM["x_new"], c.next("x_new"))
                act.activation(y[:, b, :], x[:, b, :], ACT.Square, accum_out=ssq[:, 2 * b:2 * b + 1]).then_inc(SEM["sq"], 1)

        def two_norms(name):
            square_sums(None, name)
            pre()
            transposed()

        pre()
        transposed()
        ffn([])
        square_sums(None, "used2")
        for s in (0, 1, 3, 2):
            prep(s)
        pre()
        transposed()
        def evac(p, fn, then, dmas=1):
            panel_evac(p, fn)
            for s in then:
                prep(s, dmas)
        def to_stage(j):
            def fn(b, t):
                return act.activation(st_rkv[:, j, b, :], t, ACT.Copy)
            return fn
        evac(0, to_stage(1), (0, 1))
        evac(1, to_stage(2), (2, 3))
        evac(0, to_stage(0), (0, 1))
        act.wait_ge(SEM["used3"], c.so_far("used3"))
        for b in range(TB):
            act.activation(glu[:, b, 0:256], bank[2 * b + 1][:, 256:512], ACT.Copy)
            ins = act.activation(lora[:, b, :], bank[2 * b + 1][:, 0:256], ACT.Copy)
        ins.then_inc(SEM["gen1"], 1)
        c.count("gen1")
        prep(2)
        act.wait_ge(SEM["used1"], c.so_far("used1"))
        for b in range(TB):
            act.activation(glu[:, b, 256:512], bank[2 * b][:, 0:256], ACT.Copy)
            ins = act.activation(cgate[:, b, 0:256], bank[2 * b][:, 256:512], ACT.Sigmoid)
        ins.then_inc(SEM["gen0"], 1)
        c.count("gen0")
        prep(0)
        prep(1)
        act.wait_ge(SEM["used2"], c.so_far("used2"))
        for b in range(TB):
            ins = act.activation(cgate[:, b, 256:512], bank[2 * b + 1][:, 0:256], ACT.Sigmoid)
        ins.then_inc(SEM["gen1"], 1)
        c.count("gen1")
        prep(2)
        prep(3)
        act.wait_ge(SEM["cw_tr"], c.next("cw_tr"))
        act.activation(convw, bank[4][:, 0:P].rearrange("p (c j) -> p c j", c=4), ACT.Copy).then_inc(SEM["cw_ready"], 1)
        for b in range(TB):
            act.wait_ge(SEM["glu_tr"], c.next("glu_tr"))
            act.activation(gluT[:, :, CONV - 1 + b * P:CONV - 1 + (b + 1) * P],
                           bank[6 + b][:, :].rearrange("p (c t) -> p c t", c=4), ACT.Copy).then_inc(SEM["gluT_ready"], 1)
        act.wait_ge(SEM["lmix"], c.next("lmix"))
        act.activation(lora[:, :, 0:64], lora[:, :, 0:64], ACT.Tanh).then_inc(SEM["lora_ready"], 1)
        act.activation(lora[:, :, 128:256], lora[:, :, 128:256], ACT.Sigmoid).then_inc(SEM["lora_ready"], 1)
        act.wait_ge(SEM["lora_tr"], c.next("lora_tr"))
        act.activation(loraT, bank[4][:, :].rearrange("p (w t) -> p w t", w=2), ACT.Copy).then_inc(SEM["loraT_ready"], 1)
        for b in range(TB):
            act.wait_ge(SEM["ups_ready"], c.next("ups_ready"))
            act.activation(st_sag[:, 2, b, :], bank[3 * b + 2][:, :], ACT.Copy)
            act.wait_ge(SEM["sa_ready"], c.next("sa_ready"))
            act.activation(st_sag[:, 0:2, b, :], st_sag[:, 0:2, b, :], ACT.Sigmoid).then_inc(SEM["sag_ready"], 1)
        act.wait_ge(SEM["tot_ready"], c.next("tot_ready"))
        act.activation(pc, bank[7][:, 0:64].rearrange("p (j c) -> p j c", j=4), ACT.Exp, scale=DECAY).then_inc(SEM["pc_ready"], 1)
        for n, (dst, bk, sgn) in enumerate(((ROW_6, 0, 1), (ROW_7, 4, 1), (ROW_8, 2, -1), (ROW_8, 2, 1))):
            if n < 3:
                act.wait_ge(SEM["cum_ready"], c.next("cum_ready"))
            act.wait_ge(SEM["e_free"], c.next("e_free"))
            for h in range(2):
                ins = act.activation(rows_t[:, dst, 8 * h:8 * h + 8, :].rearrange("p c n -> p (c n)"), bank[bk + h][:, :],
                                     ACT.Exp, scale=sgn * DECAY)
            ins.then_inc(SEM["e_exp"], 1)
        for b in range(TB):
            act.wait_ge(SEM["conv_n"], c.next("conv_n"))
            act.activation(y_conv[:, b, :], y_conv[:, b, :], ACT.Silu).then_inc(SEM["yb_ready"], 1)
        with c.loop(NCH, "act scan") as i:
            act.wait_ge(SEM["rkab_tr"], c.next("rkab_tr"))
            act.activation(rkabT[0:64, :], bank[0][0:64, :], ACT.Copy).then_inc(SEM["rkabT_ready"], 1)
            act.wait_ge(SEM["rT_tr"], c.next("rT_tr"))
            act.activation(rT_s, bank[5][:, :].rearrange("p (j t) -> p j t", j=4), ACT.Copy).then_inc(SEM["rT_ready"], 1)
            act.wait_ge(SEM["pw_mm"], c.next("pw_mm"))
            act.activation(pw[:, 0:2, :], bank[3][:, 0:256].rearrange("p (a t) -> p a t", a=2), ACT.Copy).then_inc(SEM["pw_ready"], 1)
            act.wait_ge(SEM["pw_mm"], c.next("pw_mm"))
            act.activation(pw[:, 2:4, :], bank[4][:, 0:256].rearrange("p (a t) -> p a t", a=2), ACT.Copy).then_inc(SEM["pw_ready"], 1)
            act.wait_ge(SEM["pw_mm"], c.next("pw_mm"))
            act.activation(pw[:, 4, :], bank[3][:, 0:P], ACT.Copy).then_inc(SEM["pw_ready"], 1)
            act.wait_ge(SEM["aT_mm"], c.next("aT_mm"))
            act.activation(aT_s, bank[6][:, :].rearrange("p (j t) -> p j t", j=4), ACT.Copy).then_inc(SEM["aTs_ready"], 1)
            act.wait_ge(SEM["y_mm"], c.next("y_mm"))
            act.activation(rows_t[:, ROW_8, ds(i, 1), :].rearrange("p a n -> p (a n)"), bank[7][:, 0:HD], ACT.Copy)\
               .then_inc(SEM["y_out"], 1)
        transposed()
        next_units(0, 2)
        for p in range(2):
            c.count(f"gen{p}")
        two_norms("used3")
        ffn([])
        square_sums(None, "used2")
        prep(0, 2)
        prep(1, 2)
        pre()
        transposed()
        ffn([])
        square_sums(None, "used2")
        for s in (0, 1, 3, 2):
            prep(s)
        pre()
        transposed()
        with c.loop(2, "act fqk") as i:
            for p in range(2):
                act.wait_ge(SEM[f"used{2 * p + 1}"], c.so_far(f"used{2 * p + 1}"))
                for b in range(TB):
                    act.wait_ge(SEM["sq_free"], c.so_far("sq_free"))
                    c.count("sq_free")
                    act.activation(rope2, bank[2 * b + p][:, :], ACT.Square).then_inc(SEM["fsq"], 1)
                c.count(f"gen{p}")
                next_units(p)
            for r in range(4):
                act.wait_ge(SEM["rope_tr"], c.next("rope_tr"))
                act.activation(fqkT[:, ds(i, 1), 4 * (r // 2):4 * (r // 2) + 4, (r % 2) * P:(r % 2 + 1) * P],
                               bank[6 + r % 2][:, :].rearrange("p (a h t) -> p a h t", a=1, h=4), ACT.Copy)\
                   .then_inc(SEM["qk_ready"], 1)
        panel_evac(0, lambda b, t: act.activation(fval[:, b, 0:HALF], t, ACT.Copy))
        prep(0)
        panel_evac(1, lambda b, t: act.activation(fval[:, b, HALF:D], t, ACT.Copy))
        c.count("gen0")
        prep(0)
        prep(1)
        act.wait_ge(SEM["fabs"], c.next("fabs"))
        act.activation(fabs, fabs, ACT.Exp, scale=-1.0).then_inc(SEM["act"], 1)
        act.wait_ge(SEM["act"], c.next("act"))
        act.activation(fabs, fabs, ACT.Ln, bias=1.0).then_inc(SEM["fln"], 1)
        with c.loop(2, "act fox") as i:
            for hp in range(4):
                act.wait_ge(SEM["smax"], c.next("smax"))
                for j in range(4):
                    at = slice(0, P) if j < 2 else slice(P, P + T)
                    act.activation(fe_t[:, j % 2, at], bank[4 + j % 2][:, at], ACT.Exp, bias=fatt[:, j:j + 1],
                                   accum_out=fatt[:, 4 + j:5 + j]).then_inc(SEM["e_ready"], 1)
                act.wait_ge(SEM["eT_tr"], c.next("eT_tr"))
                act.activation(feT[:, 0, :, :], bank[6][:, 0:384].rearrange("p (k t) -> p k t", k=3), ACT.Copy)\
                   .then_inc(SEM["aT_ready"], 1)
                if hp == 3:
                    act.wait_ge(SEM["used1"], c.so_far("used1"))
                    for b in range(TB):
                        ins = act.activation(fgate[:, b, ds(i * HALF, HALF)], bank[2 * b][:, :], ACT.Copy)
                    ins.then_inc(SEM["gen0"], 1)
                    c.count("gen0")
                    prep(0)
                    prep(1)
        prep(2)
        prep(3)
        act.wait_ge(SEM["gen0"], c.so_far("gen0"))
        act.activation(fgate, fgate, ACT.Sigmoid).then_inc(SEM["gate_on"], 1)
        transposed()
        next_units(0, 2)
        for p in range(2):
            c.count(f"gen{p}")
        two_norms("used3")
        ffn([])
        square_sums(None, "used2")

    def second_dve(c, dve, low, next_units, transposed, ffn, moments):
        def var_of(b, parts):
            dve.wait_ge(SEM["sq"], c.next("sq", parts))
            if parts == 2:
                dve.tensor_tensor(ssq[:, 2 * b:2 * b + 1], ssq[:, 2 * b:2 * b + 1], ssq[:, 2 * b + 1:2 * b + 2], ALU.add)\
                   .then_inc(SEM["dve"], 1)
                dve.wait_ge(SEM["dve"], c.next("dve"))
            dve.tensor_scalar(ve[:, b:b + 1], ssq[:, 2 * b:2 * b + 1], 1.0 / D, RMS_EPS, ALU.mult, ALU.add)\
               .then_inc(SEM["var"], 1)

        def post(factor, to):
            for b in range(TB):
                var_of(b, 2)
            dve.wait_ge(SEM["gains_ld"], c.next("gains_ld", 32))
            for b in range(TB):
                dve.wait_ge(SEM["rstd"], c.next("rstd"))
                dve.tensor_scalar(rstd[:, b:b + 1], rstd[:, b:b + 1], factor, None, ALU.mult).then_inc(SEM["dve"], 1)
                dve.wait_ge(SEM["dve"], c.next("dve"))
                for h in range(2):
                    at = slice(h * HALF, (h + 1) * HALF)
                    ins = dve.scalar_tensor_tensor(y[:, b, at], bank[2 * b + h][:, :], rstd[:, b:b + 1], gains[:, 0, at],
                                                   ALU.mult, ALU.mult)
                    if b == TB - 1:
                        ins.then_inc(SEM[f"gen{h}"], 1)
                        dve.wait_ge(SEM[f"gen{h}"], c.next(f"gen{h}"))
                    else:
                        ins.then_inc(SEM["dve"], 1)
                        dve.wait_ge(SEM["dve"], c.next("dve"))
                dve.tensor_tensor(x[:, b, :], x[:, b, :], y[:, b, :], ALU.add).then_inc(SEM[to], 1)

        def pre():
            for b in range(TB):
                var_of(b, 1)
            for b in range(TB):
                dve.wait_ge(SEM["rstd"], c.next("rstd"))
                dve.scalar_tensor_tensor(y[:, b, :], x[:, b, :], rstd[:, b:b + 1], gains[:, 1, :], ALU.mult, ALU.mult)\
                   .then_inc(SEM["x_ready"], 1)
                c.count("x_ready")

        def two_norms(factor):
            post(factor, "x_new")
            pre()
            transposed()

        c.count("o_out", 8 * DEPTH)
        c.count("o_ready", 8 * DEPTH)
        dve.wait_ge(SEM["gains_ld"], c.next("gains_ld", 32))
        for b in range(TB):
            dve.tensor_scalar(ve[:, b:b + 1], mv[:, b, 1:2], 1.0, None, ALU.mult).then_inc(SEM["x_new"], 1)
        pre()
        transposed()
        ffn(1.0)
        post(0.5, "x_new")
        for s in (0, 1, 3, 2):
            low(s)
        pre()
        transposed()
        for p, then in ((0, (0, 1)), (1, (2, 3)), (0, (0, 1)), (1, (2,)), (0, (0, 1)), (1, (2, 3))):
            c.count(f"gen{p}")
            for s in then:
                low(s)
        dve.wait_ge(SEM["gen0"], c.so_far("gen0"))
        dve.wait_ge(SEM["gen1"], c.so_far("gen1"))
        dve.tensor_tensor(glu, glu, cgate, ALU.mult).then_inc(SEM["glu_ready"], 1)
        dve.wait_ge(SEM["ab_ld"], c.next("ab_ld", 16 * 17))
        dve.wait_ge(SEM["lp_ld"], c.next("lp_ld", 16))
        dve.tensor_tensor(lora_prev, lora_prev, lora, ALU.subtract).then_inc(SEM["dve"], 1)
        dve.wait_ge(SEM["dve"], c.next("dve"))
        dve.tensor_tensor(lora_prev, lora_prev, mu_lora.rearrange("p (a n) -> p a n", a=1).broadcast_to([P, TB, LORA]), ALU.mult)\
           .then_inc(SEM["dve"], 1)
        dve.wait_ge(SEM["dve"], c.next("dve"))
        dve.tensor_tensor(lora, lora, lora_prev, ALU.add).then_inc(SEM["lmix"], 1)
        dve.wait_ge(SEM["rkv_ld"], c.next("rkv_ld", 16 * 6))
        dve.tensor_tensor(rows_t[:, 3:6, :, :], rows_t[:, 3:6, :, :], rows_t[:, 0:3, :, :], ALU.subtract)\
           .then_inc(SEM["dve"], 1)
        dve.wait_ge(SEM["dve"], c.next("dve"))
        for j in range(3):
            ins = dve.tensor_tensor(rows_t[:, 3 + j, :, :], rows_t[:, 3 + j, :, :],
                                    mu_rows[:, j:j + 1, :].broadcast_to([P, NCH, HD]), ALU.mult)
        ins.then_inc(SEM["dve"], 1)
        dve.wait_ge(SEM["dve"], c.next("dve"))
        dve.tensor_tensor(rows_t[:, 0:3, :, :], rows_t[:, 0:3, :, :], rows_t[:, 3:6, :, :], ALU.add).then_inc(SEM["mixed"], 1)
        dve.wait_ge(SEM["mixed"], c.next("mixed"))
        for b in range(TB):
            dve.wait_ge(SEM["ups_ready"], c.next("ups_ready"))
            for j in range(2):
                ins = dve.tensor_tensor(st_sag[:, j, b, :], bank[3 * b + j][:, :], sag_base[:, j, :], ALU.add)
            ins.then_inc(SEM["sa_ready"], 1)
        def par(j):
            return row_par[:, j:j + 1, :].broadcast_to([P, NCH, HD])
        def per_chunk(t):
            return t.rearrange("p (c a) -> p c a", a=1).broadcast_to([P, NCH, HD])
        V, R_, K_, SIG, A_, G_, T6, T7, T8 = (rows_t[:, j, :, :] for j in range(9))
        dve.wait_ge(SEM["cw_ready"], c.next("cw_ready"))
        dve.memset(gluT[:, :, 0:CONV - 1], 0.0).then_inc(SEM["dve"], 1)
        dve.wait_ge(SEM["dve"], c.next("dve"))
        dve.wait_ge(SEM["gluT_ready"], c.next("gluT_ready", TB))
        for ct in range(4):
            dve.tensor_scalar(conv_o[:, ct, :], gluT[:, ct, 0:T], convw[:, ct, 0:1], convw[:, ct, CONV:CONV + 1], ALU.mult, ALU.add)\
               .then_inc(SEM["dve"], 1)
            dve.wait_ge(SEM["dve"], c.next("dve"))
            with c.loop(CONV - 1, "dve conv") as j:
                dve.scalar_tensor_tensor(conv_o[:, ct, :], gluT[:, ct, ds(j + 1, T)], convw[:, ct, ds(j + 1, 1)],
                                         conv_o[:, ct, :], ALU.mult, ALU.add).then_inc(SEM["dve"], 1)
                dve.wait_ge(SEM["dve"], c.next("dve"))
        dve.memset(small[:, 3, :], 0.0).then_inc(SEM["conv_done"], 1)
        dve.wait_ge(SEM["cgb_ld"], c.next("cgb_ld", 32))
        for b in range(TB):
            dve.wait_ge(SEM["convT"], c.next("convT"))
            dve.bn_stats(stats[:, 0, :], bank[6 + b][:, :]).then_inc(SEM["dve"], 1)
            dve.wait_ge(SEM["dve"], c.next("dve"))
            c.hold()
            dve.bn_aggr(mv[:, b, :], stats[:, 0, :]).then_inc(SEM["dve"], 1)
            dve.wait_ge(SEM["dve"], c.next("dve"))
            dve.tensor_scalar(ve[:, b:b + 1], mv[:, b, 1:2], LN_EPS, None, ALU.add).then_inc(SEM["var"], 1)
            dve.scalar_tensor_tensor(y_conv[:, b, :], bank[6 + b][:, :], mv[:, b, 0:1], conv_gb[:, 0, :], ALU.subtract, ALU.mult)\
               .then_inc(SEM["dve"], 1)
            dve.wait_ge(SEM["dve"], c.next("dve"))
            dve.wait_ge(SEM["rstd"], c.next("rstd"))
            dve.scalar_tensor_tensor(y_conv[:, b, :], y_conv[:, b, :], rstd[:, b:b + 1], conv_gb[:, 1, :], ALU.mult, ALU.add)\
               .then_inc(SEM["conv_n"], 1)
        dve.wait_ge(SEM["sag_ld"], c.next("sag_ld", 48))
        dve.wait_ge(SEM["pc_ready"], c.next("pc_ready"))
        dve.tensor_tensor(T8, K_, par(0), ALU.mult).then_inc(SEM["dve"], 1)
        dve.wait_ge(SEM["dve"], c.next("dve"))
        dve.tensor_tensor(T7, T8, T8, ALU.mult).then_inc(SEM["dve"], 1)
        dve.wait_ge(SEM["dve"], c.next("dve"))
        dve.tensor_reduce(small[:, 2, :], T7, X, ALU.add).then_inc(SEM["dve"], 1)
        dve.wait_ge(SEM["dve"], c.next("dve"))
        dve.tensor_scalar(small[:, 2, :], small[:, 2, :], 1e-24, None, ALU.max).then_inc(SEM["kk_var"], 1)
        dve.scalar_tensor_tensor(T7, A_, -1.0, par(1), ALU.add, ALU.mult).then_inc(SEM["dve"], 1)
        dve.wait_ge(SEM["dve"], c.next("dve"))
        dve.scalar_tensor_tensor(K_, T7, 1.0, K_, ALU.add, ALU.mult).then_inc(SEM["dve"], 1)
        dve.wait_ge(SEM["dve"], c.next("dve"))
        dve.tensor_tensor(T7, R_, K_, ALU.mult).then_inc(SEM["dve"], 1)
        dve.wait_ge(SEM["dve"], c.next("dve"))
        dve.tensor_tensor(T7, T7, par(2), ALU.mult).then_inc(SEM["dve"], 1)
        dve.wait_ge(SEM["dve"], c.next("dve"))
        dve.tensor_reduce(bonus, T7, X, ALU.add).then_inc(SEM["dve"], 1)
        dve.wait_ge(SEM["dve"], c.next("dve"))
        dve.wait_ge(SEM["kk_rstd"], c.next("kk_rstd"))
        dve.tensor_tensor(T8, T8, per_chunk(small[:, 1, :]), ALU.mult).then_inc(SEM["dve"], 1)
        dve.wait_ge(SEM["dve"], c.next("dve"))
        dve.tensor_tensor(A_, T8, A_, ALU.mult).then_inc(SEM["e_free"], 1)
        dve.wait_ge(SEM["e_free"], c.next("e_free"))
        dve.wait_ge(SEM["e_exp"], c.next("e_exp"))
        dve.wait_ge(SEM["cum_ready"], c.next("cum_ready", 3))
        dve.tensor_tensor(SIG, T8, T6, ALU.mult).then_inc(SEM["e_free"], 1)
        dve.wait_ge(SEM["e_free"], c.next("e_free"))
        dve.wait_ge(SEM["e_exp"], c.next("e_exp"))
        dve.tensor_tensor(T6, K_, T7, ALU.mult)
        dve.scalar_tensor_tensor(T7, A_, -1.0, T7, ALU.mult, ALU.mult).then_inc(SEM["e_free"], 1)
        dve.wait_ge(SEM["e_free"], c.next("e_free"))
        dve.wait_ge(SEM["e_exp"], c.next("e_exp"))
        dve.tensor_tensor(K_, K_, T8, ALU.mult)
        dve.tensor_tensor(A_, A_, T8, ALU.mult).then_inc(SEM["e_free"], 1)
        dve.wait_ge(SEM["e_free"], c.next("e_free"))
        dve.wait_ge(SEM["e_exp"], c.next("e_exp"))
        dve.tensor_tensor(R_, R_, T8, ALU.mult).then_inc(SEM["e_done"], 1)
        dve.memset(state, 0.0).then_inc(SEM["m_new"], 1)
        c.count("m_new")
        with c.loop(NCH, "dve scan") as i:
            dve.wait_ge(SEM["gram_mm"], c.next("gram_mm"))
            dve.tensor_tensor(gram[:, 0:4, :], bank[1][:, :].rearrange("p (a t) -> p a t", a=4), gram_mask[:, 0:4, :], ALU.mult)
            dve.tensor_tensor(gram[:, 4, :], bank[2][:, 0:P], gram_mask[:, 4, :], ALU.mult).then_inc(SEM["gram_ready"], 1)
            dve.wait_ge(SEM["gram_ready"], c.next("gram_ready"))
            dve.tensor_tensor(inv, gram[:, 1, :], ident[:, :], ALU.add).then_inc(SEM["inv_ready"], 1)
            dve.wait_ge(SEM["inv_ready"], c.next("inv_ready"))
            for bk, at in ((4, slice(256, 384)), (3, slice(P, 256)), (4, slice(0, P))):
                dve.wait_ge(SEM["inv_mm"], c.next("inv_mm"))
                dve.tensor_tensor(inv, inv, bank[bk][:, at], ALU.add).then_inc(SEM["inv_ready"], 1)
                dve.wait_ge(SEM["inv_ready"], c.next("inv_ready"))
            dve.wait_ge(SEM["tlk_mm"], c.next("tlk_mm"))
            dve.tensor_copy(tlk, bank[2][:, 0:P]).then_inc(SEM["tlk_ready"], 1)
            dve.tensor_tensor(sdec, state, pc[:, :, ds(i, 1)].broadcast_to([P, 4, HD]), ALU.mult)
            dve.wait_ge(SEM["u_mm"], c.next("u_mm"))
            dve.tensor_copy(u_s, bank[1][:, 0:HD]).then_inc(SEM["u_ready"], 1)
            dve.wait_ge(SEM["m_mm"], c.next("m_mm"))
            dve.tensor_tensor(state, sdec, bank[0][:, 0:256].rearrange("p (j n) -> p j n", j=4), ALU.add).then_inc(SEM["m_new"], 1)
            dve.wait_ge(SEM["m_new"], c.next("m_new"))
        dve.wait_ge(SEM["y_out"], c.next("y_out", NCH))
        dve.tensor_reduce(small[:, 2, :], T8, X, ALU.add).then_inc(SEM["dve"], 1)
        dve.wait_ge(SEM["dve"], c.next("dve"))
        dve.tensor_scalar(small[:, 2, :], small[:, 2, :], 1.0 / HD, None, ALU.mult).then_inc(SEM["dve"], 1)
        dve.wait_ge(SEM["dve"], c.next("dve"))
        dve.tensor_tensor(T8, T8, per_chunk(small[:, 2, :]), ALU.subtract).then_inc(SEM["dve"], 1)
        dve.wait_ge(SEM["dve"], c.next("dve"))
        dve.tensor_tensor(T7, T8, T8, ALU.mult).then_inc(SEM["dve"], 1)
        dve.wait_ge(SEM["dve"], c.next("dve"))
        dve.tensor_reduce(small[:, 2, :], T7, X, ALU.add).then_inc(SEM["dve"], 1)
        dve.wait_ge(SEM["dve"], c.next("dve"))
        dve.tensor_scalar(small[:, 2, :], small[:, 2, :], 1.0 / HD, GN_EPS, ALU.mult, ALU.add).then_inc(SEM["kk_var"], 1)
        dve.tensor_tensor(T8, T8, par(3), ALU.mult).then_inc(SEM["dve"], 1)
        dve.wait_ge(SEM["dve"], c.next("dve"))
        dve.tensor_tensor(T7, V, per_chunk(bonus), ALU.mult).then_inc(SEM["dve"], 1)
        dve.wait_ge(SEM["dve"], c.next("dve"))
        dve.tensor_tensor(T7, T7, par(4), ALU.add).then_inc(SEM["dve"], 1)
        dve.wait_ge(SEM["dve"], c.next("dve"))
        dve.wait_ge(SEM["kk_rstd"], c.next("kk_rstd"))
        dve.tensor_tensor(T8, T8, per_chunk(small[:, 1, :]), ALU.mult).then_inc(SEM["dve"], 1)
        dve.wait_ge(SEM["dve"], c.next("dve"))
        dve.tensor_tensor(T8, T8, T7, ALU.add).then_inc(SEM["dve"], 1)
        dve.wait_ge(SEM["dve"], c.next("dve"))
        dve.tensor_tensor(T8, T8, G_, ALU.mult).then_inc(SEM["yr_ready"], 1)
        transposed()
        next_units(0)
        two_norms(1.0)
        ffn(1.0)
        post(0.5, "x_new")
        low(0)
        low(1)
        pre()
        transposed()
        ffn(1.0)
        post(0.5, "x_new")
        for s in (0, 1, 3, 2):
            low(s)
        pre()
        transposed()
        dve.wait_ge(SEM["c_ld"], c.next("c_ld", 16 * 6))
        with c.loop(2, "dve fqk") as i:
            for p in range(2):
                dve.wait_ge(SEM[f"used{2 * p + 1}"], c.so_far(f"used{2 * p + 1}"))
                for b in range(TB):
                    dve.wait_ge(SEM["fsq"], c.next("fsq"))
                    dve.tensor_reduce(fss, rope2.rearrange("p (h d) -> p h d", d=HD), X, ALU.add).then_inc(SEM["sq_free"], 1)
                    dve.wait_ge(SEM["sq_free"], c.next("sq_free"))
                    dve.tensor_scalar(fss, fss, 1.0 / HD, RMS_EPS, ALU.mult, ALU.add).then_inc(SEM["fss_ready"], 1)
                    dve.wait_ge(SEM["frs_ready"], c.next("frs_ready"))
                    t = rope1.rearrange("p (h d) -> p h d", d=HD)
                    ins = dve.tensor_tensor(t, bank[2 * b + p][:, :].rearrange("p (h d) -> p h d", d=HD),
                                            frs.rearrange("p (h a) -> p h a", a=1).broadcast_to([P, 8, HD]), ALU.mult)
                    if b == TB - 1:
                        ins.then_inc(SEM[f"gen{p}"], 1)
                        dve.wait_ge(SEM[f"gen{p}"], c.next(f"gen{p}"))
                    else:
                        ins.then_inc(SEM["dve"], 1)
                        dve.wait_ge(SEM["dve"], c.next("dve"))
                    dve.tensor_tensor(y[:, b, p * HALF:(p + 1) * HALF].rearrange("p (h d) -> p h d", d=HD), t,
                                      qk_gain[:, ds(i, 1), :].broadcast_to([P, 8, HD]), ALU.mult).then_inc(SEM["rope"], 1)
                    dve.wait_ge(SEM["rope"], c.next("rope"))
                next_units(p)
        c.count("gen0")
        low(0)
        c.count("gen1")
        dve.wait_ge(SEM["used0"], c.so_far("used0"))
        for b in range(TB):
            ins = dve.tensor_tensor(flog[:, b, :], bank[2 * b][:, 0:FOX], fbias, ALU.add)
        ins.then_inc(SEM["gen0"], 1)
        dve.wait_ge(SEM["gen0"], c.next("gen0"))
        dve.scalar_tensor_tensor(fabs, flog, -1.0, flog, ALU.mult, ALU.max).then_inc(SEM["fabs"], 1)
        low(0)
        low(1)
        dve.wait_ge(SEM["fln"], c.next("fln"))
        dve.scalar_tensor_tensor(flog, flog, 0.0, fabs, ALU.min, ALU.subtract).then_inc(SEM["flog_ready"], 1)
        dve.wait_ge(SEM["cum_mm"], c.next("cum_mm"))
        dve.tensor_copy(cumT[0:FOX, 0, :], bank[1][0:FOX, 0:T])
        dve.tensor_scalar(cumT[0:FOX, 1, :], bank[1][0:FOX, 0:T], -1.0, None, ALU.mult).then_inc(SEM["cumT_ready"], 1)
        with c.loop(2, "dve fox") as i:
            for hp in range(4):
                dve.wait_ge(SEM["s_ready"], c.next("s_ready"))
                for j in range(4):
                    at = slice(0, P) if j < 2 else slice(P, P + T)
                    ins = dve.tensor_reduce(fatt[:, j:j + 1], bank[4 + j % 2][:, at], X, ALU.max, negate=True)
                ins.then_inc(SEM["smax"], 1)
                dve.wait_ge(SEM["e_ready"], c.next("e_ready", 4))
                dve.reciprocal(fatt[:, 8:12], fatt[:, 4:8]).then_inc(SEM["rinv"], 1)
                dve.wait_ge(SEM["rinv"], c.next("rinv"))
                dve.wait_ge(SEM["eT1_tr"], c.next("eT1_tr"))
                dve.tensor_copy(feT[:, 1, :, :], bank[1][:, 0:384].rearrange("p (k t) -> p k t", k=3)).then_inc(SEM["eT1_ready"], 1)
                dve.wait_ge(SEM["o_ready"], c.next("o_ready"))
                dve.tensor_tensor(y[:, :, ds(i * 512 + hp * P, P)].rearrange("p b (m e) -> p b m e", m=2),
                                  bank[7][:, 0:T].rearrange("p (b m e) -> p b m e", b=TB, m=2),
                                  fatt[:, 8:12].rearrange("p (b m a) -> p b m a", b=TB, a=1).broadcast_to([P, TB, 2, HD]),
                                  ALU.mult)\
                   .then_inc(SEM["o_out"], 1)
                c.count("o_out")
                if hp == 3:
                    c.count("gen0")
                    low(0)
                    low(1)
        low(2)
        low(3)
        dve.wait_ge(SEM["gate_on"], c.next("gate_on"))
        dve.wait_ge(SEM["o_out"], c.so_far("o_out"))
        dve.tensor_tensor(y[:, :, :], y[:, :, :], fgate, ALU.mult).then_inc(SEM["hb_ready"], 1)
        transposed()
        next_units(0)
        two_norms(1.0)
        ffn(1.0)
        post(0.5, "done")

    def second_pe(c, pe, three, panel, panel_unit, up_unit, transposes, ffn):
        c.count("e_ready", 4 * 8 * DEPTH)
        transposes(y, "x_ready", True)
        ffn()
        transposes(y, "x_ready", True)
        for p in (0, 1, 0, 1, 0):
            panel(p)
        pe.wait_ge(SEM["ab_ld"], c.next("ab_ld", 16 * 17))
        pe.wait_ge(SEM["gen1"], c.so_far("gen1"))
        c.count("gen1")
        pe.wait_ge(SEM["lo2"], c.next("lo2"))
        for k in range(KT):
            for b in range(TB):
                t = slice(b * P, (b + 1) * P)
                r = slice(k * 256, (k + 1) * 256)
                ins = three(bank[2 * b + 1][:, 0:256], xTh[:, k, t], xTl[:, k, t], wh[2][:, r], wl[2][:, r], k == 0, k == KT - 1)
        ins.then_inc(SEM["used2"], 1)
        for ct in range(4):
            ins = pe.transpose(bank[4][:, ct * 32:(ct + 1) * 32], convw_rows[0:32, ct * P:(ct + 1) * P], ident[0:32, 0:32])
        ins.then_inc(SEM["cw_tr"], 1)
        pe.wait_ge(SEM["glu_ready"], c.next("glu_ready"))
        for b in range(TB):
            for ct in range(4):
                ins = pe.transpose(bank[6 + b][:, ct * P:(ct + 1) * P], glu[:, b, ct * P:(ct + 1) * P], ident[:, :])
            ins.then_inc(SEM["glu_tr"], 1)
        pe.wait_ge(SEM["cw_ready"], c.next("cw_ready"))
        pe.wait_ge(SEM["lora_ready"], c.next("lora_ready", 2))
        for w in range(2):
            for b in range(TB):
                ins = pe.transpose(bank[4][:, w * T + b * P:w * T + (b + 1) * P], lora[:, b, w * P:(w + 1) * P], ident[:, :])
        ins.then_inc(SEM["lora_tr"], 1)
        pe.wait_ge(SEM["loraT_ready"], c.next("loraT_ready"))
        pe.wait_ge(SEM["gen0"], c.so_far("gen0"))
        pe.wait_ge(SEM["gen1"], c.so_far("gen1"))
        for b in range(TB):
            t = slice(b * P, (b + 1) * P)
            pe.matmul(bank[3 * b][:, :], loraT[0:64, 0, t], lora_up[0:64, :], start=True, stop=True)
            pe.matmul(bank[3 * b + 1][:, :], loraT[64:128, 0, t], lora_up[64:128, :], start=True, stop=True)
            pe.matmul(bank[3 * b + 2][:, :], loraT[:, 1, t], gate_up, start=True, stop=True).then_inc(SEM["ups_ready"], 1)
        pe.wait_ge(SEM["sag_ready"], c.next("sag_ready", 2))
        pe.wait_ge(SEM["gluT_ready"], c.next("gluT_ready", 2))
        for j in range(4):
            for b in range(TB):
                ins = pe.matmul(bank[7][:, j * NCH + b * 8:j * NCH + (b + 1) * 8], st_sag[:, 0, b, j * P:(j + 1) * P],
                                chunk_mask, start=True, stop=True)
        ins.then_inc(SEM["tot_ready"], 1)
        pe.wait_ge(SEM["pc_ready"], c.next("pc_ready"))
        pe.wait_ge(SEM["conv_done"], c.next("conv_done"))
        for b in range(TB):
            for ct in range(4):
                ins = pe.transpose(bank[6 + b][:, ct * P:(ct + 1) * P], conv_o[:, ct, b * P:(b + 1) * P], ident[:, :])
            ins.then_inc(SEM["convT"], 1)
        pe.wait_ge(SEM["sag_ld"], c.next("sag_ld", 48))
        for m, bk in ((0, 0), (2, 4), (1, 2)):
            for h in range(2):
                ins = pe.matmul(bank[bk + h][:, :], cum_mask[:, m, :],
                                rows_t[:, ROW_SIG, 8 * h:8 * h + 8, :].rearrange("p c n -> p (c n)"), start=True, stop=True)
            ins.then_inc(SEM["cum_ready"], 1)
        pe.wait_ge(SEM["e_done"], c.next("e_done"))
        pe.wait_ge(SEM["conv_n"], c.next("conv_n", 2))
        c.count("m_new")
        with c.loop(NCH, "pe scan") as i:
            v_c = rows_t[:, ROW_V, ds(i, 1), :].rearrange("p a n -> p (a n)")
            pe.wait_ge(SEM["rkab_ready"], c.next("rkab_ready"))
            pe.wait_ge(SEM["m_new"], c.so_far("m_new"))
            c.count("m_new")
            c.hold()
            for j in range(4):
                ins = pe.transpose(bank[0][0:64, j * P:(j + 1) * P], rkab[:, j, :], ident[:, :])
            ins.then_inc(SEM["rkab_tr"], 1)
            pe.wait_ge(SEM["exp_ready"], c.next("exp_ready", 4))
            for j in range(4):
                ins = pe.transpose(bank[5][:, j * P:(j + 1) * P], r_exp[:, j * P:(j + 1) * P], ident[:, :])
            ins.then_inc(SEM["rT_tr"], 1)
            pe.wait_ge(SEM["rkabT_ready"], c.next("rkabT_ready"))
            rT, kT, aT_, bT = (rkabT[0:64, j * P:(j + 1) * P] for j in range(4))
            pe.matmul(bank[1][:, 0:P], bT, rT, start=True, stop=True)
            pe.matmul(bank[1][:, P:256], bT, aT_, start=True, stop=True)
            pe.matmul(bank[1][:, 256:384], aT_, kT, start=True, stop=True)
            pe.matmul(bank[1][:, 384:512], aT_, bT, start=True, stop=True)
            pe.matmul(bank[2][:, 0:P], kT, rT, start=True, stop=True).then_inc(SEM["gram_mm"], 1)
            pe.wait_ge(SEM["gram_ready"], c.next("gram_ready"))
            x1, x1t = gram[:, 1, :], gram[:, 3, :]
            pe.matmul(bank[3][:, 0:P], x1t, x1, start=True, stop=True)
            pe.matmul(bank[3][:, P:256], x1, x1t, start=True, stop=True).then_inc(SEM["pw_mm"], 1)
            pe.wait_ge(SEM["pw_ready"], c.next("pw_ready"))
            pe.wait_ge(SEM["inv_ready"], c.next("inv_ready"))
            pe.matmul(bank[4][:, 0:P], pw[:, 1, :], pw[:, 0, :], start=True, stop=True)
            pe.matmul(bank[4][:, P:256], pw[:, 0, :], pw[:, 1, :], start=True, stop=True).then_inc(SEM["pw_mm"], 1)
            pe.wait_ge(SEM["pw_ready"], c.next("pw_ready"))
            pe.matmul(bank[4][:, 256:384], pw[:, 1, :], inv, start=True, stop=True).then_inc(SEM["inv_mm"], 1)
            pe.matmul(bank[3][:, 0:P], pw[:, 2, :], pw[:, 3, :], start=True, stop=True).then_inc(SEM["pw_mm"], 1)
            pe.wait_ge(SEM["pw_ready"], c.next("pw_ready"))
            pe.wait_ge(SEM["inv_ready"], c.next("inv_ready"))
            pe.matmul(bank[3][:, P:256], pw[:, 3, :], inv, start=True, stop=True).then_inc(SEM["inv_mm"], 1)
            pe.wait_ge(SEM["inv_ready"], c.next("inv_ready"))
            pe.matmul(bank[4][:, 0:P], pw[:, 4, :], inv, start=True, stop=True).then_inc(SEM["inv_mm"], 1)
            pe.wait_ge(SEM["inv_ready"], c.next("inv_ready"))
            for j in range(4):
                ins = pe.matmul(bank[6][:, j * P:(j + 1) * P], a_exp[:, j * P:(j + 1) * P], inv, start=True, stop=True)
            ins.then_inc(SEM["aT_mm"], 1)
            pe.matmul(bank[2][:, 0:P], gram[:, 2, :], inv, start=True, stop=True).then_inc(SEM["tlk_mm"], 1)
            pe.wait_ge(SEM["aTs_ready"], c.next("aTs_ready"))
            pe.wait_ge(SEM["tlk_ready"], c.next("tlk_ready"))
            for j in range(4):
                pe.matmul(bank[1][:, 0:HD], aT_s[:, j, :], state[:, j, :], start=(j == 0), stop=False)
            pe.matmul(bank[1][:, 0:HD], tlk, v_c, start=False, stop=True).then_inc(SEM["u_mm"], 1)
            pe.wait_ge(SEM["rT_ready"], c.next("rT_ready"))
            pe.wait_ge(SEM["y_out"], c.so_far("y_out"))
            c.count("y_out")
            for j in range(4):
                pe.matmul(bank[7][:, 0:HD], rT_s[:, j, :], state[:, j, :], start=(j == 0), stop=False)
            pe.matmul(bank[7][:, 0:HD], gram[:, 4, :], v_c, start=False, stop=False)
            pe.wait_ge(SEM["u_ready"], c.next("u_ready"))
            pe.matmul(bank[7][:, 0:HD], gram[:, 0, :], u_s, start=False, stop=True).then_inc(SEM["y_mm"], 1)
            for j in range(4):
                o = bank[0][:, j * HD:(j + 1) * HD]
                pe.matmul(o, kt_exp[:, j * P:(j + 1) * P], v_c, start=True, stop=False)
                ins = pe.matmul(o, bt_exp[:, j * P:(j + 1) * P], u_s, start=False, stop=True)
            ins.then_inc(SEM["m_mm"], 1)
        pe.wait_ge(SEM["yb_ready"], c.next("yb_ready", 2))
        pe.wait_ge(SEM["y_ld"], c.next("y_ld", 16))
        transposes(lambda b, k: (y_rwkv if k < 4 else y_conv)[:, b, (k % 4) * P:(k % 4 + 1) * P], None, False)
        panel(0)
        panel(1)
        transposes(y, "x_ready", True)
        ffn()
        transposes(y, "x_ready", True)
        ffn()
        transposes(y, "x_ready", True)
        with c.loop(2, "pe qk2"):
            panel(0)
            panel(1)
            for r in range(4):
                pe.wait_ge(SEM["rope"], c.next("rope"))
                if r >= 2:
                    pe.wait_ge(SEM["qk_ready"], c.next("qk_ready"))
                for q in range(4):
                    ins = pe.transpose(bank[6 + r % 2][:, q * P:(q + 1) * P],
                                       y[:, r % 2, (r // 2) * HALF + q * P:(r // 2) * HALF + (q + 1) * P], ident[:, :])
                ins.then_inc(SEM["rope_tr"], 1)
            pe.wait_ge(SEM["qk_ready"], c.next("qk_ready", 2))
        panel(0)
        panel(1)
        pe.wait_ge(SEM["c_ld"], c.next("c_ld", 16 * 6))
        pe.wait_ge(SEM["gen0"], c.so_far("gen0"))
        c.count("gen0")
        pe.wait_ge(SEM["lo0"], c.next("lo0"))
        for k in range(KT):
            for b in range(TB):
                t = slice(b * P, (b + 1) * P)
                r = slice(k * FOX, (k + 1) * FOX)
                ins = three(bank[2 * b][:, 0:FOX], xTh[:, k, t], xTl[:, k, t], wh[0][:, r], wl[0][:, r], k == 0, k == KT - 1)
        ins.then_inc(SEM["used0"], 1)
        pe.wait_ge(SEM["gen1"], c.so_far("gen1"))
        pe.wait_ge(SEM["flog_ready"], c.next("flog_ready"))
        pe.matmul(bank[1][0:FOX, 0:P], flog[:, 0, :], tri_c, start=True, stop=True)
        pe.matmul(bank[1][0:FOX, P:T], flog[:, 0, :], ones_c, start=True, stop=False)
        pe.matmul(bank[1][0:FOX, P:T], flog[:, 1, :], tri_c, start=False, stop=True).then_inc(SEM["cum_mm"], 1)
        pe.wait_ge(SEM["cumT_ready"], c.next("cumT_ready"))
        with c.loop(2, "pe fox") as i:
            for hp in range(4):
                pe.wait_ge(SEM["qh_ready"], c.next("qh_ready", 3))
                for m in range(2):
                    f = slice(m * HD, (m + 1) * HD)
                    for at, q, n in ((0, slice(0, P), P), (P, slice(P, T), T)):
                        o = bank[4 + m][:, at:at + n]
                        pe.matmul(o, identb, negm_wide[:, T - n:T], start=True, stop=False)
                        pe.matmul(o, selh[0:FOX, m, 0:P], cumT[0:FOX, 1, 0:n], start=False, stop=False)
                        pe.matmul(o, cumT[0:FOX, 0, q], selh[0:FOX, m, 0:n], start=False, stop=False)
                        ins = pe.matmul(o, qh[f, q], kh[f, 0:n], start=False, stop=True)
                ins.then_inc(SEM["s_ready"], 1)
                if hp in (1, 2):
                    panel_unit(0, hp - 1)
                pe.wait_ge(SEM["e_ready"], c.next("e_ready", 4))
                pe.wait_ge(SEM["o_out"], c.so_far("o_out"))
                c.count("o_out")
                for m, bk in ((0, 6), (1, 1)):
                    for k in range(3):
                        ins = pe.transpose(bank[bk][:, k * P:(k + 1) * P], fe_t[:, m, k * P:(k + 1) * P], ident[:, :])
                    ins.then_inc(SEM["eT_tr" if m == 0 else "eT1_tr"], 1)
                pe.wait_ge(SEM["aT_ready"], c.next("aT_ready"))
                pe.wait_ge(SEM["eT1_ready"], c.next("eT1_ready"))
                for b in range(TB):
                    for m in range(2):
                        o = bank[7][:, (2 * b + m) * HD:(2 * b + m + 1) * HD]
                        for k in range(b + 1):
                            ins = pe.matmul(o, feT[:, m, b + k, :], fval[:, k, ds(i * 512 + hp * P + m * HD, HD)],
                                            start=(k == 0), stop=(k == b))
                ins.then_inc(SEM["o_ready"], 1)
        transposes(y, "hb_ready", False)
        panel(0)
        panel(1)
        transposes(y, "x_ready", True)
        ffn()


    @block.sync
    def _(sp):
        c = Counts(sp, SEM["held"])

        def load(s, *pieces):
            sp.wait_ge(SEM[f"lo{s}"], c.so_far(f"lo{s}"))
            c.count(f"lo{s}")
            for dst, src in pieces:
                sp.dma_start(dst, src).then_inc(SEM[f"ld{s}"], 16)

        def rows(w):
            return w.rearrange("(k p) n -> p k n", p=P)

        def up(w1, w3, j):
            for s in range(2):
                dst = wf[s][:, :].rearrange("p (k n) -> p k n", k=4)
                load(s, *((dst[:, :, m * STEP:(m + 1) * STEP],
                           rows(w)[:, 4 * s:4 * s + 4, ds(j * STEP, STEP)]) for m, w in enumerate((w1, w3))))

        def down(w2, j):
            load(2, (wf[2][:, :].rearrange("p (k n) -> p k n", k=2), rows(w2[ds(j * STEP, STEP), :])))

        def half_panel(w, col, s, h):
            load(s, (wf[s][:, :].rearrange("p (k n) -> p k n", k=4), rows(w)[:, 4 * h:4 * h + 4, ds(col, HALF)]))

        def ffn(w1, w3, w2):
            up(w1, w3, 0)
            with c.loop(STEPS - 1, "sp ffn") as j:
                up(w1, w3, j + 1)
                down(w2, j)
            down(w2, STEPS - 1)

        def two_panels(w, col):
            for s in range(4):
                half_panel(w, col + HALF * (s // 2), s, s % 2)

        def two_panels_after_ffn(w, col):
            for s in (0, 1, 3, 2):
                half_panel(w, col + HALF * (s // 2), s, s % 2)

        def layer_of(name, l):
            w = a[name][ds(l, 1)]
            return w.rearrange("a f k n -> (a f) k n") if len(w.shape) == 4 else w.rearrange("a k n -> (a k) n")

        for n in STARTED:
            sp.sem_inc(SEM[n], 1)
        sp.dma_start(x[:, :, :], a["x"][0].rearrange("(b p) n -> p b n", p=P)).then_inc(SEM["x_ld"], 16)
        with c.loop(DEPTH, "sp layer") as l:
            w1, w3, w2 = (layer_of(n, l) for n in ("ffn_w1", "ffn_w3", "ffn_w2"))
            w_in, w_br, w_out = (layer_of(n, l) for n in ("w_in", "w_branch", "w_out"))
            ffn(w1[0], w3[0], w2[0])
            two_panels_after_ffn(w_in, 0)
            two_panels(w_in, D)
            with c.loop(2, "sp four") as i:
                two_panels(w_in, i * D + 2 * D)
            two_panels(w_in, 4 * D)
            with c.loop(2, "sp four") as i:
                two_panels(w_in, i * D + 5 * D)
            two_panels(w_br[0], 0)
            two_panels(w_br[1], 0)
            two_panels(w_out, 0)
            ffn(w1[1], w3[1], w2[1])
        second_sp(c, sp, ffn, half_panel, load, rows)

    @block.gpsimd
    def _(pool):
        c = Counts(pool, SEM["held"])

        def gains_load(*rows_):
            for i, r in enumerate(rows_):
                pool.dma_start(gains[:, i, :], bcast_row(r, D)).then_inc(SEM["gains_ld"], 16)

        def power(dst, src, n, got, to):
            pool.wait_ge(SEM[got], c.next(got))
            pool.tensor_tensor(dst, src, mhalf[:, 0:n], ALU.pow).then_inc(SEM[to], 1)

        def norm():
            for b in range(TB):
                power(rstd[:, b:b + 1], ve[:, b:b + 1], 1, "var", "rstd")

        def of_layer(name, l):
            return a[name][ds(l, 1)].rearrange("a k n -> (a k) n")

        def ln_rows(l, i):
            gains_load(of_layer("ln_g", l)[i:i + 1, :], of_layer("ln_b", l)[i:i + 1, :])

        constants = ((ident[:, :], a["c_ident"]), (mhalf[:, :], a["c_mhalf"]), (cs, a["c_rope"]),
                     (tri, a["c_tri"]), (laminit, a["c_laminit"]), (negm_f, a["c_negm"]), (identb_f, a["c_identb"]))
        for dst, src in constants:
            pool.dma_start(dst, src).then_inc(SEM["const_ld"], 16)
        pool.wait_ge(SEM["const_ld"], c.next("const_ld", 16 * 7))

        with c.loop(DEPTH, "pool layer") as l:
            pool.wait_ge(SEM["x_ready"], c.so_far("x_ready"))
            ln_rows(l, 0)
            norm()
            pool.wait_ge(SEM["x_ready"], c.next("x_ready", TB))
            gb = of_layer("gate_b", l)
            gains_load(gb[0:1, :], gb[1:2, :])
            for dst, src in ((sgu_gb[:, 0, :], bcast_row(a["sgu_ln_g"][ds(l, 1), :], D)),
                             (sgu_gb[:, 1, :], bcast_row(a["sgu_ln_b"][ds(l, 1), :], D)),
                             (sgu_w, a["sgu_w"][ds(l, 1)].rearrange("a g t r -> t (a g) r")),
                             (sgu_bT, a["sgu_b"][ds(l, 1)].rearrange("a g t -> t (a g)")),
                             (part(14728, 256), bcast_row(a["lam"][ds(l, 1)].rearrange("a k n -> a (k n)"), 256)),
                             (dgain, bcast_row(a["diff_ln_g"][ds(l, 1), :], P))):
                pool.dma_start(dst, src).then_inc(SEM["sgu_ld"], 16)
            for b in range(TB):
                power(rstd[:, b:b + 1], ve[:, b:b + 1], 1, "var", "rstd")
            pool.wait_ge(SEM["qk_ready"], c.next("qk_ready", 8))
            with c.loop(2, "pool att") as i:
                for hh in range(4):
                    pool.wait_ge(SEM["s_ready"], c.so_far("s_ready"))
                    c.count("s_ready")
                    head = [qkT[:, w, ds(i * 4 + hh, 1), :].rearrange("p a t -> p (a t)") for w in range(2)]
                    pool.tensor_tensor(qh, head[0], scale.broadcast_to([P, T]), ALU.mult).then_inc(SEM["qh_ready"], 1)
                    pool.tensor_copy(kh, head[1]).then_inc(SEM["qh_ready"], 1)
            power(orstd, oss, 16, "o_var", "o_rstd")
            pool.wait_ge(SEM["m_ready"], c.next("m_ready"))
            ln_rows(l, 1)
            norm()
            pool.wait_ge(SEM["x_ready"], c.next("x_ready", TB))
            ln_rows(l, 2)
            norm()
            c.count("x_ready", TB)
        second_pool(c, pool, gains_load, power, norm)

    @block.scalar
    def _(act):
        c = Counts(act, SEM["held"])

        def prep(s, dmas=1):
            act.wait_ge(SEM[f"ld{s}"], c.next(f"ld{s}", 16 * dmas))
            act.wait_ge(SEM[f"used{s}"], c.so_far(f"used{s}"))
            c.count(f"used{s}")
            act.activation(wh[s][:, :], wf[s][:, :], ACT.Copy).then_inc(SEM[f"hi{s}"], 1)

        def transposed():
            for r in range(4):
                act.wait_ge(SEM["tr"], c.next("tr"))
                act.activation(xTh[:, 4 * (r % 2):4 * (r % 2) + 4, (r // 2) * P:(r // 2 + 1) * P],
                               bank[6 + r % 2][:, :].rearrange("p (k t) -> p k t", k=4), ACT.Copy)\
                   .then_inc(SEM["xt_hi"], 1)

        def ffn_step(last):
            act.wait_ge(SEM["used1"], c.so_far("used1"))
            for b in range(TB):
                act.activation(sil[:, b, :], bank[4 + b][:, 0:STEP], ACT.Silu).then_inc(SEM["h_silu"], 1)
            if not last:
                prep(0, 2)
                prep(1, 2)
            act.wait_ge(SEM["ht_tr"], c.next("ht_tr"))
            act.activation(hTh[:, :, :], bank[6][:, :].rearrange("p (k t) -> p k t", k=2), ACT.Copy)\
               .then_inc(SEM["ht_hi"], 1)
            prep(2)

        def ffn(then):
            with c.loop(STEPS - 1, "act ffn"):
                ffn_step(False)
            ffn_step(True)
            for p in range(2):
                c.count(f"gen{p}")
            for s, dmas in then:
                prep(s, dmas)

        def panel_evac(p, fn):
            act.wait_ge(SEM[f"used{2 * p + 1}"], c.so_far(f"used{2 * p + 1}"))
            for b in range(TB):
                ins = fn(b, bank[2 * b + p][:, :])
            ins.then_inc(SEM[f"gen{p}"], 1)
            c.count(f"gen{p}")

        def next_units(p, dmas=1):
            prep(2 * p, dmas)
            prep(2 * p + 1, dmas)

        act.wait_ge(SEM["const_ld"], c.next("const_ld", 16 * 7))
        prep(0, 2)
        prep(1, 2)
        act.wait_ge(SEM["x_ld"], c.next("x_ld", 16))
        transposed()

        with c.loop(DEPTH, "act layer") as l:
            ffn([(0, 1), (1, 1), (3, 1), (2, 1)])
            transposed()
            with c.loop(2, "act uv") as i:
                for p in range(2):
                    panel_evac(p, lambda b, t: act.activation(
                        uv[:, ds(i, 1), b, p * HALF:(p + 1) * HALF], t.rearrange("p (a n) -> p a n", a=1), ACT.Gelu))
                    next_units(p)
            act.wait_ge(SEM["lam_s"], c.next("lam_s"))
            act.activation(lam_c[:, 0:2], lam_c[:, 0:2], ACT.Exp).then_inc(SEM["lam_e"], 1)
            with c.loop(2, "act qk") as i:
                for p in range(2):
                    c.count(f"gen{p}")
                    next_units(p)
                for r in range(4):
                    act.wait_ge(SEM["rope_tr"], c.next("rope_tr"))
                    act.activation(qkT[:, ds(i, 1), 4 * (r // 2):4 * (r // 2) + 4, (r % 2) * P:(r % 2 + 1) * P],
                                   bank[6 + r % 2][:, :].rearrange("p (a h t) -> p a h t", a=1, h=4), ACT.Copy)\
                       .then_inc(SEM["qk_ready"], 1)
            for p in range(2):
                panel_evac(p, lambda b, t: act.activation(val[:, b, p * HALF:(p + 1) * HALF], t, ACT.Copy))
                next_units(p)
            with c.loop(2, "act att") as i:
                for hh in range(4):
                    act.wait_ge(SEM["smax"], c.next("smax"))
                    act.wait_ge(SEM["a_ready"], c.so_far("a_ready"))
                    c.count("a_ready")
                    for j in range(4):
                        at = slice(0, P) if j < 2 else slice(P, P + T)
                        act.activation(e_t[:, j % 2, at], bank[4 + j % 2][:, at], ACT.Exp, bias=att[:, j:j + 1], accum_out=att[:, 4 + j:5 + j])\
                           .then_inc(SEM["e_ready"], 1)
                    act.wait_ge(SEM["a_tr"], c.next("a_tr"))
                    act.activation(aT, bank[6][:, 0:384].rearrange("p (k t) -> p k t", k=3), ACT.Copy)\
                       .then_inc(SEM["aT_ready"], 1)
                    act.wait_ge(SEM["o_ready"], c.next("o_ready"))
                    act.activation(y[:, :, ds(i * 512 + hh * P, P)],
                                   bank[7][:, 0:T].rearrange("p (b e) -> p b e", b=TB), ACT.Copy)\
                       .then_inc(SEM["o_out"], 1)
                    c.count("o_out")
                    if hh % 2:
                        c.count(f"gen{hh // 2}")
                        next_units(hh // 2)
            transposed()
            act.wait_ge(SEM["o_out"], c.so_far("o_out"))
            act.activation(osq, y[:, :, :], ACT.Square).then_inc(SEM["o_sq"], 1)
            act.wait_ge(SEM["gen0"], c.so_far("gen0"))
            act.wait_ge(SEM["gen1"], c.so_far("gen1"))
            for g in gate:
                act.activation(g, g, ACT.Sigmoid).then_inc(SEM["gate_on"], 1)
            for br in range(2):
                for p in range(2):
                    c.count(f"gen{p}")
                    next_units(p)
                transposed()
            next_units(0, 2)
            for p in range(2):
                c.count(f"gen{p}")
            transposed()
            ffn([(0, 2), (1, 2)])
            transposed()
        second_act(c, act, prep, next_units, panel_evac, transposed, ffn)

    @block.vector
    def _(dve):
        c = Counts(dve, SEM["held"])


        def low(s):
            dve.wait_ge(SEM[f"hi{s}"], c.next(f"hi{s}"))
            c.count(f"used{s}")
            dve.tensor_tensor(wl[s][:, :], wf[s][:, :], wh[s][:, :].bitcast(f32), ALU.subtract).then_inc(SEM[f"lo{s}"], 1)

        def next_units(p):
            low(2 * p)
            low(2 * p + 1)

        def transposed():
            for r in range(4):
                dve.wait_ge(SEM["xt_hi"], c.next("xt_hi"))
                at = slice(4 * (r % 2), 4 * (r % 2) + 4), slice((r // 2) * P, (r // 2 + 1) * P)
                dve.tensor_tensor(xTl[:, at[0], at[1]], bank[6 + r % 2][:, :].rearrange("p (k t) -> p k t", k=4),
                                  xTh[:, at[0], at[1]].bitcast(f32), ALU.subtract).then_inc(SEM["xt_ready"], 1)

        def ffn_step(last, half):
            for b in range(TB):
                dve.wait_ge(SEM["h_silu"], c.next("h_silu"))
                ins = dve.scalar_tensor_tensor(hid[:, b, :], sil[:, b, :], half, bank[4 + b][:, STEP:2 * STEP],
                                               ALU.mult, ALU.mult)
            ins.then_inc(SEM["h_ready"], 1)
            if not last:
                low(0)
                low(1)
            dve.wait_ge(SEM["ht_hi"], c.next("ht_hi"))
            dve.tensor_tensor(hTl[:, :, :], bank[6][:, :].rearrange("p (k t) -> p k t", k=2),
                              hTh[:, :, :].bitcast(f32), ALU.subtract).then_inc(SEM["ht_ready"], 1)
            low(2)

        def ffn(half):
            with c.loop(STEPS - 1, "dve ffn"):
                ffn_step(False, half)
            ffn_step(True, half)

        def moments(src, b):
            for h in range(2):
                ins = dve.bn_stats(stats[:, h, :], src[:, b, h * HALF:(h + 1) * HALF])
            ins.then_inc(SEM["dve"], 1)
            dve.wait_ge(SEM["dve"], c.next("dve"))
            c.hold()
            dve.bn_aggr(mv[:, b, :], stats[:, :, :].rearrange("p a b -> p (a b)")).then_inc(SEM["dve"], 1)
            dve.wait_ge(SEM["dve"], c.next("dve"))
            dve.tensor_scalar(ve[:, b:b + 1], mv[:, b, 1:2], LN_EPS, None, ALU.add).then_inc(SEM["var"], 1)

        def normalise(dst, src, gb, b, to):
            dve.scalar_tensor_tensor(src[:, b, :], src[:, b, :], mv[:, b, 0:1], gb[:, 0, :], ALU.subtract, ALU.mult)\
               .then_inc(SEM["dve"], 1)
            dve.wait_ge(SEM["dve"], c.next("dve"))
            dve.wait_ge(SEM["rstd"], c.next("rstd"))
            dve.scalar_tensor_tensor(dst[:, b, :], src[:, b, :], rstd[:, b:b + 1], gb[:, 1, :], ALU.mult, ALU.add)\
               .then_inc(SEM[to], 1)

        def post_norm(complete):
            dve.wait_ge(SEM[complete], c.so_far(complete))
            for b in range(TB):
                for h in range(2):
                    ins = dve.scalar_tensor_tensor(y[:, b, h * HALF:(h + 1) * HALF], x[:, b, h * HALF:(h + 1) * HALF],
                                                   ALPHA, bank[2 * b + h][:, :], ALU.mult, ALU.add)
                    if b == TB - 1:
                        ins.then_inc(SEM[f"gen{h}"], 1)
                        dve.wait_ge(SEM[f"gen{h}"], c.next(f"gen{h}"))
                    else:
                        ins.then_inc(SEM["dve"], 1)
                        dve.wait_ge(SEM["dve"], c.next("dve"))
                moments(y, b)
            dve.wait_ge(SEM["gains_ld"], c.next("gains_ld", 32))
            for b in range(TB):
                normalise(x, y, gains, b, "x_ready")
                c.count("x_ready")

        dve.wait_ge(SEM["const_ld"], c.next("const_ld", 16 * 7))
        low(0)
        low(1)
        transposed()

        with c.loop(DEPTH, "dve layer") as l:
            ffn(0.5)
            low(0)
            low(1)
            low(3)
            post_norm("used2")
            low(2)
            transposed()
            with c.loop(2, "dve uv"):
                for p in range(2):
                    c.count(f"gen{p}")
                    next_units(p)
            dve.wait_ge(SEM["gen0"], c.so_far("gen0"))
            dve.wait_ge(SEM["gen1"], c.so_far("gen1"))
            dve.wait_ge(SEM["sgu_ld"], c.next("sgu_ld", 16 * 6))
            for b in range(TB):
                moments(v_t, b)
            for b in range(TB):
                normalise(v_t, v_t, sgu_gb, b, "v_ready")
            lam4 = part(14728, 2, 2, HD)
            dve.tensor_tensor(lam4[:, :, 0, :], lam4[:, :, 0, :], lam4[:, :, 1, :], ALU.mult).then_inc(SEM["dve"], 1)
            dve.wait_ge(SEM["dve"], c.next("dve"))
            dve.tensor_reduce(lam_c[:, 0:2], lam4[:, :, 0, :], X, ALU.add).then_inc(SEM["lam_s"], 1)
            with c.loop(2, "dve qk") as i:
                for p in range(2):
                    dve.wait_ge(SEM[f"used{2 * p + 1}"], c.so_far(f"used{2 * p + 1}"))
                    for b in range(TB):
                        src = bank[2 * b + p][:, :].rearrange("p (h m d) -> p h m d", m=2, d=HD // 2)
                        r2 = rope2.rearrange("p (h m d) -> p h m d", m=2, d=HD // 2)
                        cos = cs[:, 0:1, b, :].broadcast_to([P, 8, HD])
                        sin = cs[:, 1:2, b, :].rearrange("p a (m d) -> p a m d", m=2)
                        dve.tensor_tensor(rope1.rearrange("p (h d) -> p h d", d=HD), src.rearrange("p h m d -> p h (m d)"),
                                          cos, ALU.mult)
                        for m in range(2):
                            ins = dve.tensor_tensor(r2[:, :, m, :], src[:, :, 1 - m, :],
                                                    sin[:, :, m, :].broadcast_to([P, 8, HD // 2]), ALU.mult)
                        if b == TB - 1:
                            ins.then_inc(SEM[f"gen{p}"], 1)
                            dve.wait_ge(SEM[f"gen{p}"], c.next(f"gen{p}"))
                        else:
                            ins.then_inc(SEM["dve"], 1)
                            dve.wait_ge(SEM["dve"], c.next("dve"))
                        dve.tensor_tensor(y[:, b, p * HALF:(p + 1) * HALF], rope1, rope2, ALU.add).then_inc(SEM["rope"], 1)
                        dve.wait_ge(SEM["rope"], c.next("rope"))
                    next_units(p)
            dve.wait_ge(SEM["lam_e"], c.next("lam_e"))
            dve.tensor_tensor(lam_c[:, 2:3], lam_c[:, 1:2], lam_c[:, 0:1], ALU.subtract).then_inc(SEM["dve"], 1)
            dve.wait_ge(SEM["dve"], c.next("dve"))
            dve.tensor_tensor(lam_c[:, 2:3], lam_c[:, 2:3], laminit[:, ds(l, 1), 0], ALU.subtract)\
               .then_inc(SEM["dve"], 1)
            dve.wait_ge(SEM["dve"], c.next("dve"))
            for r in range(2):
                dve.wait_ge(SEM["sgw_tr"], c.next("sgw_tr"))
                dve.tensor_tensor(sgu_wT[:, 4 * r:4 * r + 4, :], bank[6 + r][:, :].rearrange("p (g t) -> p g t", g=4),
                                  tri[:, :].rearrange("p (a t) -> p a t", a=1).broadcast_to([P, 4, P]), ALU.mult)\
                   .then_inc(SEM["sgw_ready"], 1)
            for b in range(TB):
                dve.wait_ge(SEM["sgu_mm"], c.next("sgu_mm"))
                for g in range(GROUPS):
                    at = slice(g * P, (g + 1) * P)
                    ins = dve.scalar_tensor_tensor(u_t[:, b, at], bank[4 + 2 * b + g // 4][:, (g % 4) * P:(g % 4 + 1) * P],
                                                   sgu_bT[:, g:g + 1], u_t[:, b, at], ALU.add, ALU.mult)
                ins.then_inc(SEM["ha_ready"], 1)
            for p in range(2):
                c.count(f"gen{p}")
                next_units(p)
            dve.wait_ge(SEM["gains_ld"], c.next("gains_ld", 32))
            with c.loop(2, "dve att") as i:
                for hh in range(4):
                    dve.wait_ge(SEM["s_ready"], c.next("s_ready"))
                    for j in range(4):
                        at = slice(0, P) if j < 2 else slice(P, P + T)
                        ins = dve.tensor_reduce(att[:, j:j + 1], bank[4 + j % 2][:, at], X, ALU.max, negate=True)
                    ins.then_inc(SEM["smax"], 1)
                    dve.wait_ge(SEM["e_ready"], c.next("e_ready", 4))
                    dve.reciprocal(att[:, 8:12], att[:, 4:8]).then_inc(SEM["dve"], 1)
                    dve.wait_ge(SEM["dve"], c.next("dve"))
                    dve.tensor_scalar(att[:, 9:12:2], att[:, 9:12:2], lam_c[:, 2:3], None, ALU.mult)\
                       .then_inc(SEM["dve"], 1)
                    dve.wait_ge(SEM["dve"], c.next("dve"))
                    dve.tensor_scalar(e_t[:, 1, 0:P], e_t[:, 1, 0:P], att[:, 9:10], None, ALU.mult)
                    dve.tensor_scalar(e_t[:, 1, P:P + T], e_t[:, 1, P:P + T], att[:, 11:12], None, ALU.mult)\
                       .then_inc(SEM["dve"], 1)
                    dve.wait_ge(SEM["dve"], c.next("dve"))
                    dve.scalar_tensor_tensor(a_t[:, 0:P], e_t[:, 0, 0:P], att[:, 8:9], e_t[:, 1, 0:P], ALU.mult, ALU.add)
                    dve.scalar_tensor_tensor(a_t[:, P:P + T], e_t[:, 0, P:P + T], att[:, 10:11], e_t[:, 1, P:P + T],
                                             ALU.mult, ALU.add).then_inc(SEM["a_ready"], 1)
                    if hh % 2:
                        p = hh // 2
                        dve.wait_ge(SEM[f"used{2 * p + 1}"], c.so_far(f"used{2 * p + 1}"))
                        for b in range(TB):
                            ins = dve.tensor_tensor(arena[:, ds(i * 8192 + 2048 + b * D + p * HALF, HALF)],
                                                    bank[2 * b + p][:, :],
                                                    gains[:, ds(i, 1), p * HALF:(p + 1) * HALF].rearrange("p a n -> p (a n)"),
                                                    ALU.add)
                        ins.then_inc(SEM[f"gen{p}"], 1)
                        c.count(f"gen{p}")
                        next_units(p)
            transposed()
            dve.wait_ge(SEM["o_sq"], c.next("o_sq"))
            dve.tensor_reduce(oss, part(4096, 16, P), X, ALU.add).then_inc(SEM["dve"], 1)
            dve.wait_ge(SEM["dve"], c.next("dve"))
            dve.tensor_scalar(oss, oss, 1.0 / P, LN_EPS, ALU.mult, ALU.add).then_inc(SEM["o_var"], 1)
            dve.wait_ge(SEM["o_rstd"], c.next("o_rstd"))
            dve.tensor_scalar(orstd, orstd, laminit[:, ds(l, 1), 1], None, ALU.mult).then_inc(SEM["dve"], 1)
            dve.wait_ge(SEM["dve"], c.next("dve"))
            yh = y[:, :, :].rearrange("p b (h e) -> p (b h) e", e=P)
            dve.tensor_tensor(yh, yh, orstd.rearrange("p (h a) -> p h a", a=1).broadcast_to([P, 16, P]), ALU.mult)\
               .then_inc(SEM["dve"], 1)
            dve.wait_ge(SEM["dve"], c.next("dve"))
            dve.tensor_tensor(yh, yh, dgain.rearrange("p (a e) -> p a e", a=1).broadcast_to([P, 16, P]), ALU.mult)\
               .then_inc(SEM["hb_ready"], 1)
            dve.wait_ge(SEM["gate_on"], c.next("gate_on", 2))
            for br in range(2):
                for p in range(2):
                    dve.wait_ge(SEM[f"used{2 * p + 1}"], c.so_far(f"used{2 * p + 1}"))
                    for b in range(TB):
                        g = gate[br][:, b, p * HALF:(p + 1) * HALF]
                        ins = dve.tensor_tensor(g, g, bank[2 * b + p][:, :], ALU.mult)
                    ins.then_inc(SEM[f"gen{p}"], 1)
                    dve.wait_ge(SEM[f"gen{p}"], c.next(f"gen{p}"))
                    next_units(p)
                if br:
                    dve.tensor_tensor(gate[0], gate[0], gate[1], ALU.add).then_inc(SEM["m_ready"], 1)
                transposed()
            next_units(0)
            post_norm("used3")
            transposed()
            ffn(0.5)
            next_units(0)
            post_norm("used2")
            transposed()
        second_dve(c, dve, low, next_units, transposed, ffn, moments)

    @block.tensor
    def _(pe):
        c = Counts(pe, SEM["held"])

        def three(o, lh, ll, rh, rl, start, stop):
            pe.matmul(o, lh, rh, start=start, stop=False)
            pe.matmul(o, lh, rl, start=False, stop=False)
            return pe.matmul(o, ll, rh, start=False, stop=stop)

        def up_unit(s, h, out0):
            pe.wait_ge(SEM[f"lo{s}"], c.next(f"lo{s}"))
            for q in range(4):
                k = 4 * h + q
                r = slice(q * HALF, (q + 1) * HALF)
                for b in range(TB):
                    t = slice(b * P, (b + 1) * P)
                    ins = three(out0(b), xTh[:, k, t], xTl[:, k, t], wh[s][:, r], wl[s][:, r], k == 0, k == KT - 1)
            ins.then_inc(SEM[f"used{s}"], 1)

        def panel_unit(p, h):
            if h == 0:
                pe.wait_ge(SEM[f"gen{p}"], c.so_far(f"gen{p}"))
                c.count(f"gen{p}")
            up_unit(2 * p + h, h, lambda b: bank[2 * b + p][:, :])

        def panel(p):
            panel_unit(p, 0)
            panel_unit(p, 1)

        def up():
            for h in range(2):
                up_unit(h, h, lambda b: bank[4 + b][:, :])

        def down(first, last):
            if first:
                for p in range(2):
                    pe.wait_ge(SEM[f"gen{p}"], c.so_far(f"gen{p}"))
                    c.count(f"gen{p}")
            pe.wait_ge(SEM["ht_ready"], c.next("ht_ready"))
            pe.wait_ge(SEM["lo2"], c.next("lo2"))
            for k in range(2):
                for n in range(2):
                    r = slice(k * D + n * HALF, k * D + (n + 1) * HALF)
                    for b in range(TB):
                        t = slice(b * P, (b + 1) * P)
                        ins = three(bank[2 * b + n][:, :], hTh[:, k, t], hTl[:, k, t], wh[2][:, r], wl[2][:, r],
                                    first and k == 0, last and k == 1)
            ins.then_inc(SEM["used2"], 1)

        def hidden():
            pe.wait_ge(SEM["h_ready"], c.next("h_ready"))
            for k in range(2):
                for b in range(TB):
                    ins = pe.transpose(bank[6][:, k * T + b * P:k * T + (b + 1) * P], hid[:, b, k * P:(k + 1) * P], ident[:, :])
            ins.then_inc(SEM["ht_tr"], 1)

        def ffn():
            up()
            hidden()
            up()
            down(True, False)
            hidden()
            with c.loop(STEPS - 2, "pe ffn"):
                up()
                down(False, False)
                hidden()
            down(False, True)

        def transposes(src, ready, each):
            for r in range(4):
                b = r // 2
                if ready and (r == 0 or (each and r == 2)):
                    pe.wait_ge(SEM[ready], c.next(ready))
                if r >= 2:
                    pe.wait_ge(SEM["xt_ready"], c.next("xt_ready"))
                for q in range(4):
                    k = 4 * (r % 2) + q
                    ins = pe.transpose(bank[6 + r % 2][:, q * P:(q + 1) * P],
                                       src(b, k) if callable(src) else src[:, b, k * P:(k + 1) * P], ident[:, :])
                ins.then_inc(SEM["tr"], 1)
            pe.wait_ge(SEM["xt_ready"], c.next("xt_ready", 2))

        pe.wait_ge(SEM["const_ld"], c.next("const_ld", 16 * 7))
        pe.wait_ge(SEM["x_ld"], c.next("x_ld", 16))
        transposes(x, None, False)

        with c.loop(DEPTH, "pe layer") as l:
            ffn()
            transposes(x, "x_ready", True)
            with c.loop(2, "pe uv"):
                panel(0)
                panel(1)
            with c.loop(2, "pe qk"):
                panel(0)
                panel(1)
                for r in range(4):
                    pe.wait_ge(SEM["rope"], c.next("rope"))
                    if r >= 2:
                        pe.wait_ge(SEM["qk_ready"], c.next("qk_ready"))
                    for q in range(4):
                        ins = pe.transpose(bank[6 + r % 2][:, q * P:(q + 1) * P],
                                           y[:, r % 2, (r // 2) * HALF + q * P:(r // 2) * HALF + (q + 1) * P], ident[:, :])
                    ins.then_inc(SEM["rope_tr"], 1)
                pe.wait_ge(SEM["qk_ready"], c.next("qk_ready", 2))
            pe.wait_ge(SEM["sgu_ld"], c.next("sgu_ld", 16 * 6))
            for r in range(2):
                for q in range(4):
                    ins = pe.transpose(bank[6 + r][:, q * P:(q + 1) * P], sgu_w[:, 4 * r + q, :], ident[:, :])
                ins.then_inc(SEM["sgw_tr"], 1)
            pe.wait_ge(SEM["sgw_ready"], c.next("sgw_ready", 2))
            for b in range(TB):
                pe.wait_ge(SEM["v_ready"], c.next("v_ready"))
                for g in range(GROUPS):
                    ins = pe.matmul(bank[4 + 2 * b + g // 4][:, (g % 4) * P:(g % 4 + 1) * P], sgu_wT[:, g, :],
                                    v_t[:, b, g * P:(g + 1) * P], start=True, stop=True)
                ins.then_inc(SEM["sgu_mm"], 1)
            panel(0)
            panel(1)
            pe.wait_ge(SEM["ha_ready"], c.next("ha_ready", 2))
            pe.wait_ge(SEM["gen0"], c.so_far("gen0"))
            pe.wait_ge(SEM["gen1"], c.so_far("gen1"))
            with c.loop(2, "pe att") as i:
                for hh in range(4):
                    pe.wait_ge(SEM["qh_ready"], c.next("qh_ready", 2))
                    for m in range(2):
                        f = slice(m * HD, (m + 1) * HD)
                        pe.matmul(bank[4 + m][:, 0:P], qh[f, 0:P], kh[f, 0:P], start=True, stop=False)
                        pe.matmul(bank[4 + m][:, 0:P], identb, negm, start=False, stop=True)
                        pe.matmul(bank[4 + m][:, P:P + T], qh[f, P:T], kh[f, 0:T], start=True, stop=False)
                        ins = pe.matmul(bank[4 + m][:, T:P + T], identb, negm, start=False, stop=True)
                    ins.then_inc(SEM["s_ready"], 1)
                    panel_unit(hh // 2, hh % 2)
                    pe.wait_ge(SEM["a_ready"], c.next("a_ready"))
                    for k in range(3):
                        ins = pe.transpose(bank[6][:, k * P:(k + 1) * P], a_t[:, k * P:(k + 1) * P], ident[:, :])
                    ins.then_inc(SEM["a_tr"], 1)
                    pe.wait_ge(SEM["aT_ready"], c.next("aT_ready"))
                    pe.wait_ge(SEM["o_out"], c.so_far("o_out"))
                    c.count("o_out")
                    ve_ = [val[:, b, ds(i * 512 + hh * P, P)] for b in range(TB)]
                    pe.matmul(bank[7][:, 0:P], aT[:, 0, :], ve_[0], start=True, stop=True)
                    pe.matmul(bank[7][:, P:T], aT[:, 1, :], ve_[0], start=True, stop=False)
                    pe.matmul(bank[7][:, P:T], aT[:, 2, :], ve_[1], start=False, stop=True).then_inc(SEM["o_ready"], 1)
            pe.wait_ge(SEM["o_out"], c.so_far("o_out"))
            transposes(u_t, None, False)
            panel(0)
            panel(1)
            transposes(y, "hb_ready", False)
            panel(0)
            panel(1)
            transposes(gate[0], "m_ready", False)
            panel(0)
            panel(1)
            transposes(x, "x_ready", True)
            ffn()
            transposes(x, "x_ready", True)
        second_pe(c, pe, three, panel, panel_unit, up_unit, transposes, ffn)
    ctx.close()


def constants():
    f = np.float32

    def bf16(t):
        return (t.astype(f).view(np.uint32) >> 16).astype(np.uint16).view(f)

    pos = np.arange(T, dtype=f)
    inv = (f(ROPE_THETA) ** (-np.arange(0, HD, 2, dtype=f) / f(HD))).astype(f)
    ang = pos[:, None] * inv[None, :]
    cos, sin = np.cos(ang).astype(f), np.sin(ang).astype(f)
    rope = np.stack([np.concatenate([cos, cos], 1), np.concatenate([-sin, sin], 1)])
    r = np.arange(P)
    lam = np.array([0.8 - 0.6 * math.exp(-0.3 * l) for l in range(DEPTH)])
    tok, head = r // RH, r % RH
    same = head[:, None] == head[None, :]
    s_lt, s_le, s_gt = ((op(tok[:, None], tok[None, :]) & same).astype(f) for op in (np.less, np.less_equal, np.greater))
    masks = [s_lt, s_le, s_gt, -s_le, -s_lt, s_gt, -s_gt, s_le,
             (head[:, None] == np.arange(RH)[None, :]).astype(f), (r[:, None] // CH == np.arange(RH)[None, :]).astype(f)]
    return {
        "c_masks": np.concatenate(masks, 1),
        "c_sel": np.broadcast_to(np.eye(FOX, dtype=f)[:, :, None], (FOX, FOX, T)).copy(),
        "c_ones": np.ones((P, P), f),
        "c_ident": np.eye(P, dtype=f),
        "c_mhalf": np.concatenate([np.full((P, P), -0.5, f), np.full((P, 1), HD ** -0.5, f)], 1),
        "c_rope": np.ascontiguousarray(rope.reshape(2, TB, P, HD).transpose(2, 0, 1, 3)),
        "c_tri": (r[:, None] <= r[None, :]).astype(f),
        "c_laminit": np.ascontiguousarray(np.broadcast_to(np.stack([lam, 1 - lam], 1).astype(f), (P, DEPTH, 2))),
        "c_negm": bf16(np.concatenate([np.zeros((P, P)), np.where(r[None, :] <= r[:, None], 0, NEG)], 1)),
        "c_identb": bf16(np.eye(P)),
    }


def kernel(**inputs):
    import concourse.bacc as bacc
    from concourse.bass_utils import run_bass_kernel_spmd

    nc = bacc.Bacc("TRN2", target_bir_lowering=False, num_devices=1)
    arrays = {n: np.ascontiguousarray(v) for n, v in inputs.items() if n in USED}
    arrays.update(constants())
    f32 = mybir.dt.float32
    a = {n: nc.dram_tensor(f"in_{n}", v.shape, f32, kind="ExternalInput").ap() for n, v in arrays.items()}
    out = nc.dram_tensor("out", (1, T, D), f32, kind="ExternalOutput").ap()
    program(nc, a, out)
    got = run_bass_kernel_spmd(nc, [{f"in_{n}": v for n, v in arrays.items()}], core_ids=[0])
    return got.results[0]["out"]
```

```python
import math
from contextlib import ExitStack, contextmanager

import numpy as np
import concourse.bass as bass
import concourse.mybir as mybir

P = 128
T = 256
TB = T // P
D = 1024
KT = D // P
FF = 2816
STEP = 256
STEPS = FF // STEP
DEPTH = 2
HALF = 512
SLOTS = 4
UNIT = 2048
LN_EPS = 1e-5
RMS_EPS = 1e-6
ALPHA = (2.0 * DEPTH) ** 0.25
GROUPS = 8
DHEADS = 8
HD = 64
ROPE_THETA = 10000.0
NEG = -1e30
IN1 = 7168
COL_U, COL_Q, COL_V, COL_G = 0, 2048, 4096, 5120
RH = 8
CH = 16
NCH = T // CH
LORA = 256
RW = 512
CONV = 31
GN_EPS = 1e-5 * HD
FOX = 16
DECAY = -math.exp(-0.5)

STARTED = [f"{n}{s}" for n in ("lo", "used") for s in range(SLOTS)] + [
    "gen0", "gen1", "x_ready", "s_ready0", "s_ready1", "a_ready", "a_tr", "o_out", "y_out", "sq_free"]


class Counts:

    def __init__(self, engine, held):
        self.engine, self.held, self.loops = engine, held, []
        self.seen = {n: 1 for n in STARTED} | {"x_ready": 1 + TB}

    def so_far(self, name):
        v = self.seen.get(name, 0)
        for i, per_pass in self.loops:
            if per_pass.get(name, 0):
                v = i * per_pass[name] + v
        return v

    def count(self, name, k=1):
        self.seen[name] = self.seen.get(name, 0) + k

    def next(self, name, k=1):
        self.count(name, k)
        return self.so_far(name)

    def hold(self):
        self.engine.sem_inc(self.held, 1)

    @contextmanager
    def loop(self, n, which):
        per_pass = PER_PASS.get(which, {})
        before = dict(self.seen)
        self.hold()
        with self.engine.Fori(0, n) as i:
            self.loops.append((i, per_pass))
            yield i
            self.loops.pop()
        grew = {k: v - before.get(k, 0) for k, v in self.seen.items() if v != before.get(k, 0)}
        assert grew == per_pass, (which, grew)
        for k, v in grew.items():
            self.seen[k] = before.get(k, 0) + n * v


PER_PASS = {
    "sp ffn": {"lo0": 1, "lo1": 1, "lo2": 1},
    "sp four": {"lo0": 1, "lo1": 1, "lo2": 1, "lo3": 1},
    "sp layer": {"lo0": 32, "lo1": 32, "lo2": 30, "lo3": 12},
    "pool att": {"s_ready0": 2, "s_ready1": 2},
    "pool layer": {"x_ready": 6, "s_ready0": 4, "s_ready1": 4, "var": 8, "qk_ready": 8, "o_var": 1, "m_ready": 2},
    "act ffn": {"ld0": 32, "used0": 1, "ld1": 32, "used1": 1, "ht_tr": 1, "ld2": 16, "used2": 1},
        "act uv": {"ld0": 16, "used0": 1, "ld1": 16, "used1": 1, "ld2": 16, "used2": 1, "gen0": 1, "gen1": 1, "ld3":
        16, "used3": 1},
        "act qk": {"ld0": 16, "used0": 1, "ld1": 16, "used1": 1, "ld2": 16, "used2": 1, "gen0": 1, "gen1": 1, "ld3":
        16, "used3": 1, "rope_tr": 4},
        "act att": {"used0": 1, "used1": 1, "used2": 1, "used3": 1, "gen0": 2, "a_ready": 4, "a_tr": 4, "o_out": 4,
        "ld0": 16, "ld1": 16, "ld2": 16, "ld3": 16, "smax": 4, "o_ready": 4},
        "act layer": {"used0": 32, "used1": 32, "used2": 30, "used3": 12, "gen0": 14, "gen1": 10, "a_ready": 8,
        "a_tr": 8, "o_out": 8, "ld0": 864, "ld1": 864, "tr": 24, "ht_tr": 22, "ld2": 480, "ld3": 192, "lam_s": 1,
        "rope_tr": 8, "smax": 8, "o_ready": 8},
    "dve ffn": {"hi0": 1, "used0": 1, "hi1": 1, "used1": 1, "h_silu": 2, "ht_hi": 1, "hi2": 1, "used2": 1},
        "dve uv": {"hi0": 1, "used0": 1, "hi1": 1, "used1": 1, "hi2": 1, "used2": 1, "hi3": 1, "used3": 1, "gen0":
        1, "gen1": 1},
        "dve qk": {"hi0": 1, "used0": 1, "hi1": 1, "used1": 1, "hi2": 1, "used2": 1, "hi3": 1, "used3": 1, "dve": 2,
        "gen0": 1, "gen1": 1, "rope": 4},
        "dve att": {"used0": 1, "used1": 1, "used2": 1, "used3": 1, "gen0": 2, "s_ready0": 2, "s_ready1": 2, "a_tr":
        4, "hi0": 1, "hi1": 1, "hi2": 1, "hi3": 1, "dve": 12, "e_ready": 16},
        "dve layer": {"used0": 32, "used1": 32, "used2": 30, "used3": 12, "gen0": 14, "gen1": 10, "x_ready": 6,
        "s_ready0": 4, "s_ready1": 4, "a_tr": 8, "hi0": 32, "hi1": 32, "xt_hi": 24, "h_silu": 44, "ht_hi": 22,
        "hi2": 30, "hi3": 12, "half": 3, "dve": 65, "gains_ld": 128, "rstd": 8, "sgu_ld": 96, "rope": 8, "lam_e": 1,
        "sgw_tr": 2, "sgu_mm": 2, "e_ready": 32, "o_sq": 1, "o_rstd": 1, "gate_on": 2},
    "pe ffn": {"lo0": 1, "lo1": 1, "h_ready": 1, "ht_ready": 1, "lo2": 1},
    "pe uv": {"lo0": 1, "lo1": 1, "gen0": 1, "gen1": 1, "lo2": 1, "lo3": 1},
    "pe qk": {"lo0": 1, "lo1": 1, "gen0": 1, "gen1": 1, "lo2": 1, "lo3": 1, "rope": 4, "qk_ready": 4},
        "pe att": {"lo0": 1, "lo1": 1, "lo2": 1, "lo3": 1, "gen0": 2, "a_ready": 4, "o_out": 4, "qh_ready": 4,
        "aT_ready": 4},
        "pe layer": {"lo0": 32, "lo1": 32, "lo2": 30, "lo3": 12, "gen0": 14, "gen1": 10, "x_ready": 6, "a_ready": 8,
        "o_out": 8, "xt_ready": 24, "h_ready": 22, "ht_ready": 22, "rope": 8, "qk_ready": 8, "sgu_ld": 96,
        "sgw_ready": 2, "v_ready": 2, "ha_ready": 2, "qh_ready": 8, "aT_ready": 8, "hb_ready": 2, "m_ready": 2},
    "pool scan": {"rows_tr0": 1, "rows_tr1": 1, "m_mm": 2},
    "pool qk": {"fss_ready": 4},
    "pool fox": {"s_ready0": 2, "s_ready1": 2},
    "act scan": {"rows_tr0": 1, "rows_tr1": 1, "pw_mm0": 3, "pw_mm1": 3, "y_mm": 2},
        "act fqk": {"used0": 1, "used1": 1, "used2": 1, "used3": 1, "gen0": 1, "gen1": 1, "sq_free": 4, "ld0": 16,
        "ld1": 16, "ld2": 16, "ld3": 16, "rope_tr": 4},
    "act fox": {"used0": 1, "used1": 1, "gen0": 1, "ld0": 16, "ld1": 16, "smax": 4, "eT_tr": 4},
    "dve conv": {"dve": 1},
        "dve scan": {"dve": 8, "m_new": 2, "rowsT_ready0": 1, "rowsT_ready1": 1, "gram_mm0": 1, "gram_ready0": 1,
        "inv_ready0": 4, "gram_mm1": 1, "gram_ready1": 1, "inv_ready1": 4, "inv_mm0": 3, "inv_mm1": 3, "w_mm": 2,
        "kv_mm": 2, "u_mm": 2, "m_mm": 2, "y_mm": 2},
        "dve fqk": {"used0": 1, "used1": 1, "used2": 1, "used3": 1, "gen0": 1, "gen1": 1, "sq_free": 4, "hi0": 1,
        "hi1": 1, "hi2": 1, "hi3": 1, "dve": 2, "rope": 4, "fsq": 4, "frs_ready": 4},
        "dve fox": {"used0": 1, "used1": 1, "gen0": 1, "s_ready0": 2, "s_ready1": 2, "o_out": 4, "hi0": 1, "hi1": 1,
        "e_ready": 16, "o_ready": 4, "eT1_tr": 4, "rinv": 4},
        "pe scan": {"y_out": 2, "rkab_ready0": 1, "rkab_ready1": 1, "rowsT_ready0": 1, "rowsT_ready1": 1,
        "gram_ready0": 1, "gram_ready1": 1, "pw_ready0": 3, "inv_ready0": 4, "pw_ready1": 3, "inv_ready1": 4,
        "ra_ready0": 1, "m_new": 2, "exp_ready0": 1, "w_ready": 2, "u_ready": 2, "ra_ready1": 1, "exp_ready1": 1},
    "pe qk2": {"lo0": 1, "lo1": 1, "lo2": 1, "lo3": 1, "gen0": 1, "gen1": 1, "rope": 4, "qk_ready": 4},
        "pe fox": {"lo0": 1, "lo1": 1, "gen0": 1, "o_out": 4, "qh_ready": 4, "aT_ready": 4, "e_ready": 16,
        "eT1_ready": 4},
}

USED = ("x", "w_in", "gate_b", "sgu_ln_g", "sgu_ln_b", "sgu_w", "sgu_b", "lam", "diff_ln_g", "w_branch", "w_out",
        "ffn_w1", "ffn_w3", "ffn_w2", "ln_g", "ln_b",
        "norm_gains_2", "ffn_w_gate_2", "ffn_w_up_2", "ffn_w_down_2", "a_w_in_2", "a_shift_mu_2",
        "a_decay_up_2", "a_decay_base_2", "a_iclr_up_2", "a_iclr_base_2", "a_gate_up_2", "a_k_k_2", "a_k_a_2",
        "a_r_k_2", "a_lnx_g_2", "a_lnx_b_2", "b_conv_w_2", "b_conv_b_2", "b_ln_g_2", "b_ln_b_2", "ab_w_out_2",
        "c_w_in_2", "c_forget_bias_2", "c_q_norm_g_2", "c_k_norm_g_2", "c_w_out_2")


def program(nc, a, out):
    f32, f32r, bf16 = mybir.dt.float32, mybir.dt.float32r, mybir.dt.bfloat16
    ACT = mybir.ActivationFunctionType
    ALU = mybir.AluOpType
    X = mybir.AxisListType.X
    ds = bass.ds
    ctx = ExitStack()
    ctx.enter_context(nc.allow_non_contiguous_dma("small parameters"))

    def sb(name, shape, dt=f32):
        return ctx.enter_context(nc.sbuf_tensor(name, shape, dt))

    wf = [sb(f"wf{s}", [P, UNIT]) for s in range(SLOTS)]
    wh = [sb(f"wh{s}", [P, UNIT], f32r) for s in range(SLOTS)]
    wl = [sb(f"wl{s}", [P, UNIT], f32r) for s in range(SLOTS)]
    xTh = sb("xTh", [P, KT, T], f32r)
    xTl = sb("xTl", [P, KT, T], f32r)
    x = sb("x", [P, TB, D])
    y = sb("y", [P, TB, D])
    hTh = sb("hTh", [P, 2, T], f32r)
    hTl = sb("hTl", [P, 2, T], f32r)
    hid = sb("hid", [P, TB, STEP])
    sil = sb("sil", [P, TB, STEP])
    gains = sb("gains", [P, 2, D])
    ident = sb("ident", [P, P])
    mhalf = sb("mhalf", [P, P + 1])
    scale = mhalf[:, P:P + 1]
    stats = sb("stats", [P, 2, 6])
    mv = sb("mv", [P, TB, 2])
    ve = sb("ve", [P, TB])
    rstd = sb("rstd", [P, TB])
    ssq = sb("ssq", [P, 4])
    arena = sb("arena", [P, 15360])
    bank = [ctx.enter_context(nc.psum_tensor(f"bank{i}", [P, HALF], f32)) for i in range(8)]

    def part(at, *shape):
        n = int(np.prod(shape))
        assert at + n <= 15360
        v = arena[:, at:at + n]
        if len(shape) == 2:
            return v.rearrange("p (a b) -> p a b", a=shape[0])
        if len(shape) == 3:
            return v.rearrange("p (a b c) -> p a b c", a=shape[0], b=shape[1])
        if len(shape) == 4:
            return v.rearrange("p (a b c d) -> p a b c d", a=shape[0], b=shape[1], c=shape[2])
        return v

    u_t = part(0, TB, D)
    v_t = part(2048, TB, D)
    uv = part(0, 2, TB, D)
    qkT = part(4096, 2, DHEADS, T)
    val = part(8192, TB, D)
    sgu_gb = part(10240, 2, D)
    sgu_w = part(12288, GROUPS, P)
    sgu_wT = part(13312, GROUPS, P)
    rope1 = hid[:, :, :].rearrange("p b n -> p (b n)")
    rope2 = sil[:, :, :].rearrange("p b n -> p (b n)")
    qh, kh = ([t[:, w, :] for t in (hid, sil)] for w in range(2))
    score_banks = ((4, 5), (1, 3))
    osq = part(4096, TB, D)
    gate = (v_t, part(10240, TB, D))
    e_t = part(12288, 2, 384)
    a_t = part(13056, 384)
    aT = part(13440, 3, P)
    att = part(13824, 64)
    oss = part(13888, 16)
    orstd = part(13904, 16)
    sgu_bT = part(14336, GROUPS)
    cs = part(14344, 2, TB, HD)
    tri = part(14600, P)
    lam_t = part(14728, 4, HD)
    lam_c = part(14984, 4)
    laminit = part(14988, DEPTH, 2)
    dgain = part(14992, P)
    negm_f, identb_f = part(15120, P), part(15248, 64)
    negm_wide, identb = negm_f.bitcast(bf16), identb_f.bitcast(bf16)
    negm = negm_wide[:, P:T]

    names = []

    def new(*ns):
        names.extend(ns)

    new("held", "const_ld", "x_ld", "half", "pre_var", "pre_rstd")
    for s in range(SLOTS):
        new(f"ld{s}", f"hi{s}", f"lo{s}", f"used{s}")
    new("h_silu", "h_ready", "ht_tr", "ht_hi", "ht_ready")
    new("tr", "xt_hi", "xt_ready", "x_ready", "gen0", "gen1")
    new("var", "rstd", "gains_ld", "dve", "act", "pool")
    new("sgu_ld", "sgu_var", "sgu_rstd", "v_ready", "sgw_tr", "sgw_ready", "sgu_mm", "ha_ready")
    new("rope", "rope_tr", "qk_ready", "val_ready")
    new("s_ready0", "s_ready1", "smax", "e_ready", "a_ready", "a_tr", "aT_ready", "o_ready", "o_out", "e_free")
    new("o_var", "o_rstd", "o_sq", "hb_ready", "gate_on", "m_ready", "lam_e", "lam_s", "qh_ready", "out_st")
    new("sq", "x_new", "done", "ab_ld", "z_st", "lp_ld", "rkv_ld", "glu_ready", "cgb_ld", "kk_var", "kk_rstd")
    new("mixed", "sag_ready", "sag_st", "sag_ld", "e_done", "m_new", "yr_ready", "y_st", "y_ld", "c_ld", "fss_ready")
    new("frs_ready", "cw_tr", "cw_ready", "glu_tr", "gluT_ready", "lmix", "lora_ready", "lora_tr", "loraT_ready")
    new("ups_ready", "sa_ready", "tot_ready", "pc_ready", "cum_ready", "e_exp", "conv_n", "yb_ready", "y_mm")
    new("y_out", "sq_free", "fsq", "fabs", "fln", "eT_tr", "convT", "u_mm", "u_ready", "m_mm", "flog_ready")
    new("cum_mm", "cumT_ready", "rinv", "eT1_tr", "eT1_ready", "w_mm", "w_ready", "kv_mm")
    for q in range(2):
        new(*(f"{n}{q}" for n in ("rkab_ready", "exp_ready", "rows_tr", "rowsT_ready", "ra_ready", "gram_mm", "gram_ready",
                                  "pw_mm", "pw_ready", "inv_mm", "inv_ready")))
    SEM = {n: ctx.enter_context(nc.semaphore(n)) for n in names}
    block = ctx.enter_context(nc.Block())

    def bcast_row(ap, n):
        return bass.AP(tensor=ap.tensor, offset=ap.offset, ap=[[0, P], [1, n]])


    rows_t = part(0, 9, NCH, HD)
    ROW_V, ROW_R, ROW_K, ROW_SIG, ROW_A, ROW_G, ROW_6, ROW_7, ROW_8 = range(9)
    st_rkv = part(6144, 3, TB, RW)
    st_sag = part(6144, 3, TB, RW)
    glu = part(9216, TB, RW)
    y_conv = part(9216, TB, RW)
    cgate = part(10240, TB, RW)
    conv_gb = part(10240, 2, RW)
    convw_rows = part(11264, RW)
    gluT = part(11264, 4, CONV - 1 + T)
    conv_o = part(12408, 4, T)
    sag_base = part(12408, 2, RW)
    lora = part(13432, TB, LORA)
    lora_prev = part(13944, TB, LORA)
    loraT = part(14456, 2, T)
    convw = part(14968, 4, 32)
    lora_up = hid[:, :, :].rearrange("p b n -> p (b n)")
    gate_up = sil[:, :, :].rearrange("p b n -> p (b n)")
    gflat = gains[:, :, :].rearrange("p a n -> p (a n)")
    cum_mask = gflat[:, 0:384].rearrange("p (a b) -> p a b", a=3)
    gram_mask = gflat[:, 384:1024].rearrange("p (a b) -> p a b", a=5)
    head_mask = gflat[:, 1024:1032]
    chunk_mask = gflat[:, 1032:1040]
    mu_rows = gflat[:, 1040:1232].rearrange("p (a b) -> p a b", a=3)
    row_par = gflat[:, 1232:1552].rearrange("p (a b) -> p a b", a=5)
    mu_lora = gflat[:, 1552:1808]
    small = gflat[:, 1808:1888].rearrange("p (a b) -> p a b", a=5)
    bonus = small[:, 0, :]
    pc = gflat[:, 1888:1952].rearrange("p (j c) -> p j c", j=4)
    yflat = y[:, :, :].rearrange("p b n -> p (b n)")
    kt_exp, bt_exp = ([yflat[:, (2 * q + i) * 512:(2 * q + i + 1) * 512] for q in range(2)] for i in range(2))
    xflat, lflat = wf[3], wf[2]
    ra_exp = [xflat[:, q * D:(q + 1) * D].rearrange("p (w j t) -> p w j t", w=2, j=4) for q in range(2)]
    gram = [lflat[:, q * 640:(q + 1) * 640].rearrange("p (a t) -> p a t", a=5) for q in range(2)]
    pw = [(lflat[:, 1280:1920] if q == 0 else part(13432, 640)).rearrange("p (a t) -> p a t", a=5) for q in range(2)]
    inv = [lflat[:, 1920:2048], part(14072, P)]
    rowsT = [part(14200 + q * 384, 3, P) for q in range(2)]
    rkab = [part(9216 + q * 384, 3, P) for q in range(2)]
    state = part(9984, 4, HD)
    hflat = hid[:, :, :].rearrange("p b n -> p (b n)")
    sdec = hflat[:, 0:256].rearrange("p (j n) -> p j n", j=4)
    w_s, u_s = hflat[:, 256:320], hflat[:, 320:384]
    pair_mask = gate_up.rearrange("p (j t) -> p j t", j=4)
    y_rwkv = part(6144, TB, RW)
    fqkT = part(0, 2, 8, T)
    fval = part(4096, TB, D)
    fgate = part(6144, TB, D)
    sel = part(8192, FOX, P)
    fe_t = part(12288, 2, 384)
    feT = part(13056, 2, 3, P)
    fatt = [part(13824 + 16 * q, 16) for q in range(2)]
    cumh, cuml = hTh[0:FOX, 0, :], hTl[0:FOX, 0, :]
    fbias = part(14368, FOX)
    flog = part(14384, TB, FOX)
    fabs = part(14416, TB, FOX)
    qk_gain = part(14448, 2, HD)
    tri_c = part(14576, P)
    ones_c = part(14704, P)
    fss = part(14832, 8)
    frs = part(14840, 8)
    selh = [t[0:FOX, 1, :] for t in (hTh, hTl)]
    z_rows = nc.dram_tensor("z_rows", (3, (T + 1) * RH, HD), f32, kind="Internal").ap()
    lora_rows = nc.dram_tensor("lora_rows", (T + 1, LORA), f32, kind="Internal").ap()
    sag_rows = nc.dram_tensor("sag_rows", (3, T * RH, HD), f32, kind="Internal").ap()
    y_rows = nc.dram_tensor("y_rows", (T * RH, HD), f32, kind="Internal").ap()

    def by_chunk(r):
        return r.rearrange("(c p) n -> p c n", p=P)

    def by_token(r):
        return r.rearrange("(b p h) n -> p b (h n)", b=TB, h=RH)

    def second_sp(c, sp, ffn, half_panel, load, rows):
        w1, w3, w2 = a["ffn_w_gate_2"], a["ffn_w_up_2"], a["ffn_w_down_2"]
        ffn(w1[0, 0], w3[0, 0], w2[0, 0])
        wa = a["a_w_in_2"][0]
        for s, col in ((0, 0), (1, 0), (2, 512), (3, 512), (0, 1024), (1, 1024), (2, 1536), (3, 1536), (0, 2048), (1, 2048)):
            half_panel(wa, col, s, s % 2)
        load(2, (wf[2][:, :].rearrange("p (k n) -> p k n", k=KT), rows(wa)[:, :, 2560:2816]))
        for s in range(4):
            half_panel(a["ab_w_out_2"][0], HALF * (s // 2), s, s % 2)
        ffn(w1[0, 1], w3[0, 1], w2[0, 1])
        ffn(w1[1, 0], w3[1, 0], w2[1, 0])
        wc = a["c_w_in_2"][0]
        for s in range(4):
            half_panel(wc, HALF * (s // 2), s, s % 2)
        for s in range(4):
            half_panel(wc, D + HALF * (s // 2), s, s % 2)
        for s in range(4):
            half_panel(wc, 2 * D + HALF * (s // 2), s, s % 2)
        load(0, (wf[0][:, 0:KT * FOX].rearrange("p (k n) -> p k n", k=KT), rows(wc)[:, :, 4 * D:4 * D + FOX]))
        for i in range(2):
            for h in range(2):
                half_panel(wc, 3 * D + i * HALF, h, h)
        for s in range(4):
            half_panel(a["c_w_out_2"][0], HALF * (s // 2), s, s % 2)
        ffn(w1[1, 1], w3[1, 1], w2[1, 1])
        sp.wait_ge(SEM["done"], c.next("done", TB))
        sp.dma_start(out[0].rearrange("(b p) n -> p b n", p=P), x[:, :, :]).then_inc(SEM["out_st"], 16)
        sp.wait_ge(SEM["out_st"], c.next("out_st", 16))

    def second_pool(c, pool, gains_load, power, norm, pre_norm):
        g2 = a["norm_gains_2"]
        copy = pool.tensor_copy

        def two_norms(l, post, pre_l, pre):
            gains_load(g2[l, post:post + 1, :], g2[pre_l, pre:pre + 1, :])
            norm()
            pre_norm()
            pool.wait_ge(SEM["x_ready"], c.next("x_ready", TB))

        for p in range(2):
            c.count(f"gen{p}", (14, 10)[p] * DEPTH + 1)
        pool.wait_ge(SEM["x_ready"], c.so_far("x_ready"))
        gains_load(g2[0, 0:1, :], g2[0, 0:1, :])
        pre_norm()
        pool.wait_ge(SEM["x_ready"], c.next("x_ready", TB))
        two_norms(0, 1, 0, 2)
        def per_row(name, at):
            t = a[name]
            return bass.AP(tensor=t.tensor, offset=t.offset + at, ap=[[0, CH], [HD, RH], [1, HD]])
        loads = [(gflat[:, 0:1040], a["c_masks"]), (mu_lora, bcast_row(a["a_shift_mu_2"][0:1, 1536:1792], LORA)),
                 (lora_up[0:64, :], a["a_decay_up_2"][0]), (lora_up[64:128, :], a["a_iclr_up_2"][0]),
                 (gate_up, a["a_gate_up_2"][0]),
                 (sag_base[:, 0, :], bcast_row(a["a_decay_base_2"], RW)), (sag_base[:, 1, :], bcast_row(a["a_iclr_base_2"], RW)),
                 (convw_rows[0:31, :], a["b_conv_w_2"][0]), (convw_rows[31:32, :], a["b_conv_b_2"])]
        for j, col in enumerate((1024, 0, 512)):
            loads.append((mu_rows[:, j, :], per_row("a_shift_mu_2", col)))
        for j, n in enumerate(("a_k_k_2", "a_k_a_2", "a_r_k_2", "a_lnx_g_2", "a_lnx_b_2")):
            loads.append((row_par[:, j, :], per_row(n, 0)))
        for dst, src in loads:
            pool.dma_start(dst, src).then_inc(SEM["ab_ld"], 16)
        pool.memset(lora_prev[0:1, :, :], 0.0).then_inc(SEM["pool"], 1)
        pool.wait_ge(SEM["pool"], c.next("pool"))
        zero = lora_prev[0:1, :, :].rearrange("p b n -> p (b n)")
        for j in range(3):
            pool.dma_start(z_rows[j, 0:RH, :].rearrange("(o h) n -> o (h n)", o=1), zero).then_inc(SEM["z_st"], 16)
        pool.dma_start(lora_rows[0:1, :], zero[:, 0:LORA]).then_inc(SEM["z_st"], 16)
        for j, p in ((1, 0), (2, 1), (0, 0)):
            pool.wait_ge(SEM[f"gen{p}"], c.next(f"gen{p}"))
            pool.dma_start(by_token(z_rows[j, RH:, :]), st_rkv[:, j, :, :]).then_inc(SEM["z_st"], 16)
        pool.wait_ge(SEM["gen1"], c.next("gen1"))
        pool.dma_start(lora_rows[1:, :].rearrange("(b p) n -> p b n", p=P), lora).then_inc(SEM["z_st"], 16)
        pool.wait_ge(SEM["z_st"], c.next("z_st", 16 * 8))
        pool.dma_start(lora_prev, lora_rows[0:T, :].rearrange("(b p) n -> p b n", p=P)).then_inc(SEM["lp_ld"], 16)
        for j in range(3):
            pool.dma_start(rows_t[:, j, :, :], by_chunk(z_rows[j, RH:, :])).then_inc(SEM["rkv_ld"], 16)
            pool.dma_start(rows_t[:, 3 + j, :, :], by_chunk(z_rows[j, 0:T * RH, :])).then_inc(SEM["rkv_ld"], 16)
        pool.wait_ge(SEM["glu_ready"], c.next("glu_ready"))
        for i, n in enumerate(("b_ln_g_2", "b_ln_b_2")):
            pool.dma_start(conv_gb[:, i, :], bcast_row(a[n], RW)).then_inc(SEM["cgb_ld"], 16)
        pool.wait_ge(SEM["mixed"], c.next("mixed"))
        pool.wait_ge(SEM["sag_ready"], c.next("sag_ready", 2))
        pool.dma_start(pair_mask, a["c_pairs"]).then_inc(SEM["cgb_ld"], 16)
        for j in range(3):
            pool.dma_start(by_token(sag_rows[j]), st_sag[:, j, :, :]).then_inc(SEM["sag_st"], 16)
        pool.wait_ge(SEM["sag_st"], c.next("sag_st", 48))
        for j in range(3):
            pool.dma_start(rows_t[:, 3 + j, :, :], by_chunk(sag_rows[j])).then_inc(SEM["sag_ld"], 16)
        power(small[:, 1, :], small[:, 2, :], 16, "kk_var", "kk_rstd")
        pool.wait_ge(SEM["e_done"], c.next("e_done"))
        def rows_of(n, q):
            twice = rows_t[:, ROW_R:ROW_A:2, ds(n, 1), :].broadcast_to([P, 2, 2, HD])
            copy(rkab[q][:, 0:2, :].rearrange("p w (m n) -> p w m n", m=2), twice)
            copy(rkab[q][:, 2, :].rearrange("p (w n) -> p w n", w=2),
                 rows_t[:, ROW_K:ROW_G:2, ds(n, 1), :].rearrange("p w a n -> p w (a n)")).then_inc(SEM[f"rkab_ready{q}"], 1)

        def expand(n, q):
            for dst, j in ((kt_exp[q], ROW_6), (bt_exp[q], ROW_7)):
                ins = pool.tensor_tensor(dst.rearrange("p (h n) -> p h n", h=RH),
                                         rows_t[:, j, ds(n, 1), :].broadcast_to([P, RH, HD]),
                                         head_mask.rearrange("p (h a) -> p h a", a=1).broadcast_to([P, RH, HD]), ALU.mult)
            ins.then_inc(SEM[f"exp_ready{q}"], 1)

        for q in range(2):
            rows_of(q, q)
        for q in range(2):
            expand(q, q)
        with c.loop(NCH // 2 - 1, "pool scan") as i:
            for q in range(2):
                pool.wait_ge(SEM[f"rows_tr{q}"], c.next(f"rows_tr{q}"))
                rows_of(i * 2 + 2 + q, q)
            for q in range(2):
                pool.wait_ge(SEM["m_mm"], c.next("m_mm"))
                expand(i * 2 + 2 + q, q)
        power(small[:, 1, :], small[:, 2, :], 16, "kk_var", "kk_rstd")
        pool.wait_ge(SEM["yr_ready"], c.next("yr_ready"))
        pool.dma_start(by_chunk(y_rows), rows_t[:, ROW_8, :, :]).then_inc(SEM["y_st"], 16)
        pool.wait_ge(SEM["y_st"], c.next("y_st", 16))
        pool.dma_start(y_rwkv, by_token(y_rows)).then_inc(SEM["y_ld"], 16)
        norm()
        two_norms(0, 3, 0, 4)
        two_norms(0, 5, 1, 0)
        two_norms(1, 1, 1, 2)
        for dst, src in ((sel[0:FOX, :, :], a["c_sel"]), (fbias, bcast_row(a["c_forget_bias_2"], FOX)),
                         (qk_gain[:, 0, :], bcast_row(a["c_q_norm_g_2"], HD)),
                         (qk_gain[:, 1, :], bcast_row(a["c_k_norm_g_2"], HD)),
                         (tri_c, a["c_tri"]), (ones_c, a["c_ones"])):
            pool.dma_start(dst, src).then_inc(SEM["c_ld"], 16)
        with c.loop(2, "pool qk") as i:
            for r in range(4):
                power(frs, fss, 8, "fss_ready", "frs_ready")
        pool.wait_ge(SEM["qk_ready"], c.next("qk_ready", 8))
        pool.wait_ge(SEM["c_ld"], c.next("c_ld", 16 * 6))
        with c.loop(2, "pool fox") as i:
            for hp in range(4):
                q = hp % 2
                pool.wait_ge(SEM[f"s_ready{q}"], c.so_far(f"s_ready{q}"))
                c.count(f"s_ready{q}")
                head = [fqkT[:, w, ds(i * 4 + hp, 1), :].rearrange("p a t -> p (a t)") for w in range(2)]
                pool.tensor_tensor(qh[q], head[0], scale.broadcast_to([P, T]), ALU.mult)
                copy(kh[q], head[1])
                copy(selh[q].rearrange("p (m t) -> p m t", m=2), sel[0:FOX, ds(i * 8 + hp * 2, 2), :])\
                    .then_inc(SEM["qh_ready"], 1)
        two_norms(1, 3, 1, 4)
        gains_load(g2[1, 5:6, :], g2[1, 5:6, :])
        norm()

    def second_act(c, act, prep, next_units, panel_evac, transposed, ffn):
        def square_sums():
            for b in range(TB):
                if b == 0:
                    act.wait_ge(SEM["half"], c.next("half"))
                else:
                    act.wait_ge(SEM["used3"], c.so_far("used3"))
                for h in range(2):
                    act.activation(y[:, b, h * HALF:(h + 1) * HALF], bank[2 * b + h][:, :], ACT.Square,
                                   accum_out=ssq[:, 2 * b + h:2 * b + h + 1]).then_inc(SEM["sq"], 1)

        def pre():
            for b in range(TB):
                act.wait_ge(SEM["x_new"], c.next("x_new"))
                act.activation(y[:, b, :], x[:, b, :], ACT.Square, accum_out=ssq[:, 2 * b:2 * b + 1]).then_inc(SEM["sq"], 1)
                transposed(b)

        def two_norms():
            square_sums()
            pre()

        c.count("half", 3 * DEPTH)
        pre()
        ffn([(0, 1), (1, 1), (2, 1)])
        two_norms()
        prep(3)
        def evac(p, fn, then, dmas=1):
            panel_evac(p, fn)
            for s in then:
                prep(s, dmas)
        def to_stage(j):
            def fn(b, t):
                return act.activation(st_rkv[:, j, b, :], t, ACT.Copy)
            return fn
        evac(0, to_stage(1), (0, 1))
        evac(1, to_stage(2), (2, 3))
        evac(0, to_stage(0), (0, 1))
        act.wait_ge(SEM["used3"], c.so_far("used3"))
        for b in range(TB):
            act.activation(glu[:, b, 0:256], bank[2 * b + 1][:, 256:512], ACT.Copy)
            ins = act.activation(lora[:, b, :], bank[2 * b + 1][:, 0:256], ACT.Copy)
        ins.then_inc(SEM["gen1"], 1)
        c.count("gen1")
        prep(2)
        act.wait_ge(SEM["used1"], c.so_far("used1"))
        for b in range(TB):
            act.activation(glu[:, b, 256:512], bank[2 * b][:, 0:256], ACT.Copy)
            ins = act.activation(cgate[:, b, 0:256], bank[2 * b][:, 256:512], ACT.Sigmoid)
        ins.then_inc(SEM["gen0"], 1)
        c.count("gen0")
        prep(0)
        prep(1)
        act.wait_ge(SEM["used2"], c.so_far("used2"))
        for b in range(TB):
            ins = act.activation(cgate[:, b, 256:512], bank[2 * b + 1][:, 0:256], ACT.Sigmoid)
        ins.then_inc(SEM["gen1"], 1)
        c.count("gen1")
        prep(2)
        prep(3)
        act.wait_ge(SEM["cw_tr"], c.next("cw_tr"))
        act.activation(convw, bank[4][:, 0:P].rearrange("p (c j) -> p c j", c=4), ACT.Copy).then_inc(SEM["cw_ready"], 1)
        for b in range(TB):
            act.wait_ge(SEM["glu_tr"], c.next("glu_tr"))
            act.activation(gluT[:, :, CONV - 1 + b * P:CONV - 1 + (b + 1) * P],
                           bank[6 + b][:, :].rearrange("p (c t) -> p c t", c=4), ACT.Copy).then_inc(SEM["gluT_ready"], 1)
        act.wait_ge(SEM["lmix"], c.next("lmix"))
        act.activation(lora[:, :, 0:64], lora[:, :, 0:64], ACT.Tanh).then_inc(SEM["lora_ready"], 1)
        act.activation(lora[:, :, 128:256], lora[:, :, 128:256], ACT.Sigmoid).then_inc(SEM["lora_ready"], 1)
        act.wait_ge(SEM["lora_tr"], c.next("lora_tr"))
        act.activation(loraT, bank[4][:, :].rearrange("p (w t) -> p w t", w=2), ACT.Copy).then_inc(SEM["loraT_ready"], 1)
        for b in range(TB):
            act.wait_ge(SEM["ups_ready"], c.next("ups_ready"))
            act.activation(st_sag[:, 2, b, :], bank[3 * b + 2][:, :], ACT.Copy)
            act.wait_ge(SEM["sa_ready"], c.next("sa_ready"))
            act.activation(st_sag[:, 0:2, b, :], st_sag[:, 0:2, b, :], ACT.Sigmoid).then_inc(SEM["sag_ready"], 1)
        act.wait_ge(SEM["tot_ready"], c.next("tot_ready"))
        act.activation(pc, bank[7][:, 0:64].rearrange("p (j c) -> p j c", j=4), ACT.Exp, scale=DECAY).then_inc(SEM["pc_ready"], 1)
        for n, (dst, bk, sgn) in enumerate(((ROW_6, 0, 1), (ROW_7, 4, 1), (ROW_8, 2, -1), (ROW_8, 2, 1))):
            if n < 3:
                act.wait_ge(SEM["cum_ready"], c.next("cum_ready"))
            act.wait_ge(SEM["e_free"], c.next("e_free"))
            for h in range(2):
                ins = act.activation(rows_t[:, dst, 8 * h:8 * h + 8, :].rearrange("p c n -> p (c n)"), bank[bk + h][:, :],
                                     ACT.Exp, scale=sgn * DECAY)
            ins.then_inc(SEM["e_exp"], 1)

        def copy(dst, src, to):
            act.activation(dst, src, ACT.Copy).then_inc(SEM[to], 1)

        def take_rows(q):
            act.wait_ge(SEM[f"rows_tr{q}"], c.next(f"rows_tr{q}"))
            copy(rowsT[q], bank[2 * q][:, 0:384].rearrange("p (w t) -> p w t", w=3), f"rowsT_ready{q}")

        def take_powers(q, step):
            act.wait_ge(SEM[f"pw_mm{q}"], c.next(f"pw_mm{q}"))
            dst = pw[q][:, 4, :] if step == 2 else pw[q][:, 2 * step:2 * step + 2, :]
            src = bank[2 * q + step % 2][:, 0:P if step == 2 else 2 * P]
            copy(dst, src if step == 2 else src.rearrange("p (a t) -> p a t", a=2), f"pw_ready{q}")

        def take_y(n):
            act.wait_ge(SEM["y_mm"], c.next("y_mm"))
            copy(rows_t[:, ROW_8, ds(n, 1), :].rearrange("p a n -> p (a n)"), bank[6][:, 0:HD], "y_out")

        for q in range(2):
            take_rows(q)
        for step in range(3):
            for q in range(2):
                take_powers(q, step)
        with c.loop(NCH // 2 - 1, "act scan") as i:
            take_rows(0)
            take_rows(1)
            take_y(i * 2)
            take_powers(0, 0)
            take_y(i * 2 + 1)
            take_powers(0, 1)
            take_powers(1, 0)
            take_powers(0, 2)
            take_powers(1, 1)
            take_powers(1, 2)
        for n in (NCH - 2, NCH - 1):
            take_y(n)
        for b in range(TB):
            act.wait_ge(SEM["conv_n"], c.next("conv_n"))
            act.activation(y_conv[:, b, :], y_conv[:, b, :], ACT.Silu).then_inc(SEM["yb_ready"], 1)
        transposed()
        next_units(0, 2)
        for p in range(2):
            c.count(f"gen{p}")
        two_norms()
        ffn([(0, 2), (1, 2)])
        two_norms()
        ffn([(0, 1), (1, 1), (2, 1)])
        two_norms()
        prep(3)
        with c.loop(2, "act fqk") as i:
            for p in range(2):
                act.wait_ge(SEM[f"used{2 * p + 1}"], c.so_far(f"used{2 * p + 1}"))
                for b in range(TB):
                    act.wait_ge(SEM["sq_free"], c.so_far("sq_free"))
                    c.count("sq_free")
                    act.activation(rope2, bank[2 * b + p][:, :], ACT.Square).then_inc(SEM["fsq"], 1)
                c.count(f"gen{p}")
                next_units(p)
            for r in range(4):
                act.wait_ge(SEM["rope_tr"], c.next("rope_tr"))
                act.activation(fqkT[:, ds(i, 1), 4 * (r // 2):4 * (r // 2) + 4, (r % 2) * P:(r % 2 + 1) * P],
                               bank[6 + r % 2][:, :].rearrange("p (a h t) -> p a h t", a=1, h=4), ACT.Copy)\
                   .then_inc(SEM["qk_ready"], 1)
        panel_evac(0, lambda b, t: act.activation(fval[:, b, 0:HALF], t, ACT.Copy))
        prep(0)
        panel_evac(1, lambda b, t: act.activation(fval[:, b, HALF:D], t, ACT.Copy))
        c.count("gen0")
        prep(0)
        prep(1)
        act.wait_ge(SEM["fabs"], c.next("fabs"))
        act.activation(fabs, fabs, ACT.Exp, scale=-1.0).then_inc(SEM["act"], 1)
        act.wait_ge(SEM["act"], c.next("act"))
        act.activation(fabs, fabs, ACT.Ln, bias=1.0).then_inc(SEM["fln"], 1)

        def exps(hp):
            q = hp % 2
            act.wait_ge(SEM["smax"], c.next("smax"))
            for j in range(4):
                at = slice(0, P) if j < 2 else slice(P, P + T)
                act.activation(fe_t[:, j % 2, at], bank[score_banks[q][j % 2]][:, at], ACT.Exp, bias=fatt[q][:, j:j + 1],
                               accum_out=fatt[q][:, 4 + j:5 + j]).then_inc(SEM["e_ready"], 1)

        def take_turned():
            act.wait_ge(SEM["eT_tr"], c.next("eT_tr"))
            act.activation(feT[:, 0, :, :], bank[6][:, 0:384].rearrange("p (k t) -> p k t", k=3), ACT.Copy)\
               .then_inc(SEM["aT_ready"], 1)

        with c.loop(2, "act fox") as i:
            for hp in range(4):
                exps(hp)
                if hp == 2:
                    act.wait_ge(SEM["used1"], c.so_far("used1"))
                    for b in range(TB):
                        ins = act.activation(fgate[:, b, ds(i * HALF, HALF)], bank[2 * b][:, :], ACT.Copy)
                    ins.then_inc(SEM["gen0"], 1)
                    c.count("gen0")
                    prep(0)
                if hp == 3:
                    prep(1)
                take_turned()
        act.wait_ge(SEM["gen0"], c.so_far("gen0"))
        for b in range(TB):
            act.activation(fgate[:, b, :], fgate[:, b, :], ACT.Sigmoid).then_inc(SEM["gate_on"], 1)
        transposed()
        prep(2)
        prep(3)
        next_units(0, 2)
        for p in range(2):
            c.count(f"gen{p}")
        two_norms()
        ffn([])
        square_sums()

    def second_dve(c, dve, low, next_units, transposed, ffn, moments):
        def var_of(b, factor):
            dve.wait_ge(SEM["sq"], c.next("sq", 2))
            dve.tensor_tensor(ssq[:, 2 * b:2 * b + 1], ssq[:, 2 * b:2 * b + 1], ssq[:, 2 * b + 1:2 * b + 2], ALU.add)\
               .then_inc(SEM["dve"], 1)
            dve.wait_ge(SEM["dve"], c.next("dve"))
            dve.tensor_scalar(ve[:, b:b + 1], ssq[:, 2 * b:2 * b + 1], 1.0 / (D * factor ** 2), RMS_EPS / factor ** 2,
                              ALU.mult, ALU.add).then_inc(SEM["var"], 1)

        def post(b, to):
            dve.wait_ge(SEM["rstd"], c.next("rstd"))
            for h in range(2):
                at = slice(h * HALF, (h + 1) * HALF)
                ins = dve.scalar_tensor_tensor(y[:, b, at], bank[2 * b + h][:, :], rstd[:, b:b + 1], gains[:, 0, at],
                                               ALU.mult, ALU.mult)
                if b == TB - 1:
                    ins.then_inc(SEM[f"gen{h}"], 1)
                    dve.wait_ge(SEM[f"gen{h}"], c.next(f"gen{h}"))
                else:
                    ins.then_inc(SEM["dve"], 1)
                    dve.wait_ge(SEM["dve"], c.next("dve"))
            dve.tensor_tensor(x[:, b, :], x[:, b, :], y[:, b, :], ALU.add).then_inc(SEM[to], 1)

        def pre_var(b):
            dve.wait_ge(SEM["sq"], c.next("sq"))
            dve.tensor_scalar(ve[:, b:b + 1], ssq[:, 2 * b:2 * b + 1], 1.0 / D, RMS_EPS, ALU.mult, ALU.add)\
               .then_inc(SEM["pre_var"], 1)

        def pre(b):
            dve.wait_ge(SEM["pre_rstd"], c.next("pre_rstd"))
            dve.scalar_tensor_tensor(y[:, b, :], x[:, b, :], rstd[:, b:b + 1], gains[:, 1, :], ALU.mult, ALU.mult)\
               .then_inc(SEM["x_ready"], 1)
            c.count("x_ready")

        def two_norms(factor):
            var_of(0, factor)
            dve.wait_ge(SEM["gains_ld"], c.next("gains_ld", 32))
            post(0, "x_new")
            var_of(1, factor)
            pre_var(0)
            pre(0)
            post(1, "x_new")
            transposed(0)
            pre_var(1)
            pre(1)
            transposed(1)

        c.count("o_out", 8 * DEPTH)
        c.count("o_ready", 8 * DEPTH)
        dve.wait_ge(SEM["gains_ld"], c.next("gains_ld", 32))
        for b in range(TB):
            dve.tensor_scalar(ve[:, b:b + 1], mv[:, b, 1:2], 1.0, None, ALU.mult).then_inc(SEM["x_new"], 1)
        for b in range(TB):
            pre_var(b)
            pre(b)
            transposed(b)
        ffn(1.0)
        for s in range(3):
            low(s)
        two_norms(0.5)
        low(3)
        for p, then in ((0, (0, 1)), (1, (2, 3)), (0, (0, 1)), (1, (2,)), (0, (0, 1)), (1, (2, 3))):
            c.count(f"gen{p}")
            for s in then:
                low(s)
        dve.wait_ge(SEM["gen0"], c.so_far("gen0"))
        dve.wait_ge(SEM["gen1"], c.so_far("gen1"))
        dve.tensor_tensor(glu, glu, cgate, ALU.mult).then_inc(SEM["glu_ready"], 1)
        dve.wait_ge(SEM["ab_ld"], c.next("ab_ld", 16 * 17))
        dve.wait_ge(SEM["lp_ld"], c.next("lp_ld", 16))
        dve.tensor_tensor(lora_prev, lora_prev, lora, ALU.subtract).then_inc(SEM["dve"], 1)
        dve.wait_ge(SEM["dve"], c.next("dve"))
        dve.tensor_tensor(lora_prev, lora_prev, mu_lora.rearrange("p (a n) -> p a n", a=1).broadcast_to([P, TB, LORA]), ALU.mult)\
           .then_inc(SEM["dve"], 1)
        dve.wait_ge(SEM["dve"], c.next("dve"))
        dve.tensor_tensor(lora, lora, lora_prev, ALU.add).then_inc(SEM["lmix"], 1)
        dve.wait_ge(SEM["rkv_ld"], c.next("rkv_ld", 16 * 6))
        dve.tensor_tensor(rows_t[:, 3:6, :, :], rows_t[:, 3:6, :, :], rows_t[:, 0:3, :, :], ALU.subtract)\
           .then_inc(SEM["dve"], 1)
        dve.wait_ge(SEM["dve"], c.next("dve"))
        for j in range(3):
            ins = dve.tensor_tensor(rows_t[:, 3 + j, :, :], rows_t[:, 3 + j, :, :],
                                    mu_rows[:, j:j + 1, :].broadcast_to([P, NCH, HD]), ALU.mult)
        ins.then_inc(SEM["dve"], 1)
        dve.wait_ge(SEM["dve"], c.next("dve"))
        dve.tensor_tensor(rows_t[:, 0:3, :, :], rows_t[:, 0:3, :, :], rows_t[:, 3:6, :, :], ALU.add).then_inc(SEM["mixed"], 1)
        dve.wait_ge(SEM["mixed"], c.next("mixed"))
        for b in range(TB):
            dve.wait_ge(SEM["ups_ready"], c.next("ups_ready"))
            for j in range(2):
                ins = dve.tensor_tensor(st_sag[:, j, b, :], bank[3 * b + j][:, :], sag_base[:, j, :], ALU.add)
            ins.then_inc(SEM["sa_ready"], 1)
        def par(j):
            return row_par[:, j:j + 1, :].broadcast_to([P, NCH, HD])
        def per_chunk(t):
            return t.rearrange("p (c a) -> p c a", a=1).broadcast_to([P, NCH, HD])
        V, R_, K_, SIG, A_, G_, T6, T7, T8 = (rows_t[:, j, :, :] for j in range(9))
        dve.wait_ge(SEM["cw_ready"], c.next("cw_ready"))
        dve.memset(gluT[:, :, 0:CONV - 1], 0.0).then_inc(SEM["dve"], 1)
        dve.wait_ge(SEM["dve"], c.next("dve"))
        dve.wait_ge(SEM["gluT_ready"], c.next("gluT_ready", TB))

        def tap(j, first=False):
            for ct in range(4):
                if first:
                    ins = dve.tensor_scalar(conv_o[:, ct, :], gluT[:, ct, 0:T], convw[:, ct, 0:1], convw[:, ct, CONV:CONV + 1],
                                            ALU.mult, ALU.add)
                else:
                    ins = dve.scalar_tensor_tensor(conv_o[:, ct, :], gluT[:, ct, ds(j, T)], convw[:, ct, ds(j, 1)],
                                                   conv_o[:, ct, :], ALU.mult, ALU.add)
            ins.then_inc(SEM["dve"], 1)
            dve.wait_ge(SEM["dve"], c.next("dve"))

        tap(0, True)
        tap(1)
        tap(2)
        dve.wait_ge(SEM["sag_ld"], c.next("sag_ld", 48))
        dve.wait_ge(SEM["pc_ready"], c.next("pc_ready"))
        dve.tensor_tensor(T8, K_, par(0), ALU.mult).then_inc(SEM["dve"], 1)
        dve.wait_ge(SEM["dve"], c.next("dve"))
        dve.tensor_tensor(T7, T8, T8, ALU.mult).then_inc(SEM["dve"], 1)
        dve.wait_ge(SEM["dve"], c.next("dve"))
        dve.tensor_reduce(small[:, 2, :], T7, X, ALU.add).then_inc(SEM["dve"], 1)
        dve.wait_ge(SEM["dve"], c.next("dve"))
        dve.tensor_scalar(small[:, 2, :], small[:, 2, :], 1e-24, None, ALU.max).then_inc(SEM["kk_var"], 1)
        dve.scalar_tensor_tensor(T7, A_, -1.0, par(1), ALU.add, ALU.mult).then_inc(SEM["dve"], 1)
        dve.wait_ge(SEM["dve"], c.next("dve"))
        dve.scalar_tensor_tensor(K_, T7, 1.0, K_, ALU.add, ALU.mult).then_inc(SEM["dve"], 1)
        dve.wait_ge(SEM["dve"], c.next("dve"))
        dve.tensor_tensor(T7, R_, K_, ALU.mult).then_inc(SEM["dve"], 1)
        dve.wait_ge(SEM["dve"], c.next("dve"))
        dve.tensor_tensor(T7, T7, par(2), ALU.mult).then_inc(SEM["dve"], 1)
        dve.wait_ge(SEM["dve"], c.next("dve"))
        dve.tensor_reduce(bonus, T7, X, ALU.add).then_inc(SEM["dve"], 1)
        dve.wait_ge(SEM["dve"], c.next("dve"))
        dve.wait_ge(SEM["kk_rstd"], c.next("kk_rstd"))
        dve.tensor_tensor(T8, T8, per_chunk(small[:, 1, :]), ALU.mult).then_inc(SEM["dve"], 1)
        dve.wait_ge(SEM["dve"], c.next("dve"))
        dve.tensor_tensor(A_, T8, A_, ALU.mult).then_inc(SEM["e_free"], 1)
        dve.wait_ge(SEM["e_free"], c.next("e_free"))
        dve.wait_ge(SEM["e_exp"], c.next("e_exp"))
        dve.wait_ge(SEM["cum_ready"], c.next("cum_ready", 3))
        dve.tensor_tensor(SIG, T8, T6, ALU.mult).then_inc(SEM["e_free"], 1)
        dve.wait_ge(SEM["e_free"], c.next("e_free"))
        dve.wait_ge(SEM["e_exp"], c.next("e_exp"))
        dve.tensor_tensor(T6, K_, T7, ALU.mult)
        dve.scalar_tensor_tensor(T7, A_, -1.0, T7, ALU.mult, ALU.mult).then_inc(SEM["e_free"], 1)
        dve.wait_ge(SEM["e_free"], c.next("e_free"))
        dve.wait_ge(SEM["e_exp"], c.next("e_exp"))
        dve.tensor_tensor(K_, K_, T8, ALU.mult)
        dve.tensor_tensor(A_, A_, T8, ALU.mult).then_inc(SEM["e_free"], 1)
        dve.wait_ge(SEM["e_free"], c.next("e_free"))
        dve.wait_ge(SEM["e_exp"], c.next("e_exp"))
        dve.tensor_tensor(R_, R_, T8, ALU.mult).then_inc(SEM["e_done"], 1)
        dve.memset(state, 0.0).then_inc(SEM["m_new"], 1)
        dve.wait_ge(SEM["m_new"], c.next("m_new"))

        def masks(q):
            dve.wait_ge(SEM[f"gram_mm{q}"], c.next(f"gram_mm{q}"))
            dve.tensor_tensor(gram[q][:, 0:3, :], bank[2 * q + 1][:, 0:384].rearrange("p (a t) -> p a t", a=3),
                              gram_mask[:, 0:3, :], ALU.mult)
            dve.tensor_tensor(gram[q][:, 3:5, :], bank[2 * q][:, 0:256].rearrange("p (a t) -> p a t", a=2),
                              gram_mask[:, 3:5, :], ALU.mult).then_inc(SEM[f"gram_ready{q}"], 1)
            dve.wait_ge(SEM[f"gram_ready{q}"], c.next(f"gram_ready{q}"))
            dve.tensor_tensor(inv[q], gram[q][:, 1, :], ident[:, :], ALU.add).then_inc(SEM[f"inv_ready{q}"], 1)
            c.count(f"inv_ready{q}")

        def spread(q):
            dve.wait_ge(SEM[f"rowsT_ready{q}"], c.next(f"rowsT_ready{q}"))
            dve.tensor_tensor(ra_exp[q], rowsT[q][:, 0:2, :].rearrange("p w (a t) -> p w a t", a=1).broadcast_to([P, 2, 4, P]),
                              pair_mask.rearrange("p (a j) t -> p a j t", a=1).broadcast_to([P, 2, 4, P]), ALU.mult)\
               .then_inc(SEM[f"ra_ready{q}"], 1)

        def factor(q, step):
            dve.wait_ge(SEM[f"inv_mm{q}"], c.next(f"inv_mm{q}"))
            dve.wait_ge(SEM[f"inv_ready{q}"], c.so_far(f"inv_ready{q}"))
            dve.tensor_tensor(inv[q], inv[q], bank[2 * q + min(step - 1, 1)][:, 0:P], ALU.add).then_inc(SEM[f"inv_ready{q}"], 1)
            c.count(f"inv_ready{q}")

        def take_w(n):
            dve.wait_ge(SEM["w_mm"], c.next("w_mm"))
            dve.tensor_copy(w_s, bank[4][:, 0:HD]).then_inc(SEM["w_ready"], 1)
            dve.tensor_tensor(sdec, state, pc[:, :, ds(n, 1)].broadcast_to([P, 4, HD]), ALU.mult).then_inc(SEM["dve"], 1)
            dve.wait_ge(SEM["dve"], c.next("dve"))
            dve.wait_ge(SEM["kv_mm"], c.next("kv_mm"))
            dve.tensor_tensor(sdec, sdec, bank[5][:, 0:256].rearrange("p (j n) -> p j n", j=4), ALU.add).then_inc(SEM["dve"], 1)
            dve.wait_ge(SEM["dve"], c.next("dve"))

        def take_u():
            dve.wait_ge(SEM["u_mm"], c.next("u_mm"))
            dve.tensor_copy(u_s, bank[4][:, HD:2 * HD]).then_inc(SEM["u_ready"], 1)

        def new_state():
            dve.wait_ge(SEM["m_mm"], c.next("m_mm"))
            dve.tensor_tensor(state, sdec, bank[7][:, 0:256].rearrange("p (j n) -> p j n", j=4), ALU.add)\
               .then_inc(SEM["m_new"], 1)
            dve.wait_ge(SEM["m_new"], c.next("m_new"))

        dve.wait_ge(SEM["cgb_ld"], c.next("cgb_ld", 48))
        spread(0)
        spread(1)
        masks(0)
        masks(1)
        for step in (1, 2, 3):
            for q in range(2):
                factor(q, step)
        with c.loop(NCH // 2 - 1, "dve scan") as i:
            for q in range(2):
                take_w(i * 2 + q)
                tap(i * 4 + 3 + 2 * q)
                take_u()
                new_state()
                dve.wait_ge(SEM["y_mm"], c.next("y_mm"))
                masks(q)
                spread(q)
                tap(i * 4 + 4 + 2 * q)
            factor(0, 1)
            factor(0, 2)
            factor(1, 1)
            factor(0, 3)
            factor(1, 2)
            factor(1, 3)
        for n in (NCH - 2, NCH - 1):
            take_w(n)
            if n == NCH - 1:
                dve.wait_ge(SEM["y_mm"], c.next("y_mm"))
            take_u()
            new_state()
        dve.wait_ge(SEM["y_out"], c.next("y_out", NCH))
        dve.tensor_reduce(small[:, 2, :], T8, X, ALU.add).then_inc(SEM["dve"], 1)
        dve.wait_ge(SEM["dve"], c.next("dve"))
        dve.tensor_scalar(small[:, 2, :], small[:, 2, :], 1.0 / HD, None, ALU.mult).then_inc(SEM["dve"], 1)
        dve.wait_ge(SEM["dve"], c.next("dve"))
        dve.tensor_tensor(T8, T8, per_chunk(small[:, 2, :]), ALU.subtract).then_inc(SEM["dve"], 1)
        dve.wait_ge(SEM["dve"], c.next("dve"))
        dve.tensor_tensor(T7, T8, T8, ALU.mult).then_inc(SEM["dve"], 1)
        dve.wait_ge(SEM["dve"], c.next("dve"))
        dve.tensor_reduce(small[:, 2, :], T7, X, ALU.add).then_inc(SEM["dve"], 1)
        dve.wait_ge(SEM["dve"], c.next("dve"))
        dve.tensor_scalar(small[:, 2, :], small[:, 2, :], 1.0 / HD, GN_EPS, ALU.mult, ALU.add).then_inc(SEM["kk_var"], 1)
        dve.tensor_tensor(T8, T8, par(3), ALU.mult).then_inc(SEM["dve"], 1)
        dve.wait_ge(SEM["dve"], c.next("dve"))
        dve.tensor_tensor(T7, V, per_chunk(bonus), ALU.mult).then_inc(SEM["dve"], 1)
        dve.wait_ge(SEM["dve"], c.next("dve"))
        dve.tensor_tensor(T7, T7, par(4), ALU.add).then_inc(SEM["dve"], 1)
        dve.wait_ge(SEM["dve"], c.next("dve"))
        dve.wait_ge(SEM["kk_rstd"], c.next("kk_rstd"))
        dve.tensor_tensor(T8, T8, per_chunk(small[:, 1, :]), ALU.mult).then_inc(SEM["dve"], 1)
        dve.wait_ge(SEM["dve"], c.next("dve"))
        dve.tensor_tensor(T8, T8, T7, ALU.add).then_inc(SEM["dve"], 1)
        dve.wait_ge(SEM["dve"], c.next("dve"))
        dve.tensor_tensor(T8, T8, G_, ALU.mult).then_inc(SEM["yr_ready"], 1)
        for b in range(TB):
            dve.wait_ge(SEM["convT"], c.next("convT"))
            dve.bn_stats(stats[:, 0, :], bank[b][:, :]).then_inc(SEM["dve"], 1)
            dve.wait_ge(SEM["dve"], c.next("dve"))
            c.hold()
            dve.bn_aggr(mv[:, b, :], stats[:, 0, :]).then_inc(SEM["dve"], 1)
            dve.wait_ge(SEM["dve"], c.next("dve"))
            dve.tensor_scalar(ve[:, b:b + 1], mv[:, b, 1:2], LN_EPS, None, ALU.add).then_inc(SEM["var"], 1)
            dve.scalar_tensor_tensor(y_conv[:, b, :], bank[b][:, :], mv[:, b, 0:1], conv_gb[:, 0, :], ALU.subtract, ALU.mult)\
               .then_inc(SEM["dve"], 1)
            dve.wait_ge(SEM["dve"], c.next("dve"))
        for b in range(TB):
            dve.wait_ge(SEM["rstd"], c.next("rstd"))
            dve.scalar_tensor_tensor(y_conv[:, b, :], y_conv[:, b, :], rstd[:, b:b + 1], conv_gb[:, 1, :], ALU.mult, ALU.add)\
               .then_inc(SEM["conv_n"], 1)
        transposed()
        next_units(0)
        two_norms(1.0)
        ffn(1.0)
        next_units(0)
        two_norms(0.5)
        ffn(1.0)
        for s in range(3):
            low(s)
        two_norms(0.5)
        low(3)
        dve.wait_ge(SEM["c_ld"], c.next("c_ld", 16 * 6))
        with c.loop(2, "dve fqk") as i:
            for p in range(2):
                dve.wait_ge(SEM[f"used{2 * p + 1}"], c.so_far(f"used{2 * p + 1}"))
                for b in range(TB):
                    dve.wait_ge(SEM["fsq"], c.next("fsq"))
                    dve.tensor_reduce(fss, rope2.rearrange("p (h d) -> p h d", d=HD), X, ALU.add).then_inc(SEM["sq_free"], 1)
                    dve.wait_ge(SEM["sq_free"], c.next("sq_free"))
                    dve.tensor_scalar(fss, fss, 1.0 / HD, RMS_EPS, ALU.mult, ALU.add).then_inc(SEM["fss_ready"], 1)
                    dve.wait_ge(SEM["frs_ready"], c.next("frs_ready"))
                    t = rope1.rearrange("p (h d) -> p h d", d=HD)
                    ins = dve.tensor_tensor(t, bank[2 * b + p][:, :].rearrange("p (h d) -> p h d", d=HD),
                                            frs.rearrange("p (h a) -> p h a", a=1).broadcast_to([P, 8, HD]), ALU.mult)
                    if b == TB - 1:
                        ins.then_inc(SEM[f"gen{p}"], 1)
                        dve.wait_ge(SEM[f"gen{p}"], c.next(f"gen{p}"))
                    else:
                        ins.then_inc(SEM["dve"], 1)
                        dve.wait_ge(SEM["dve"], c.next("dve"))
                    dve.tensor_tensor(y[:, b, p * HALF:(p + 1) * HALF].rearrange("p (h d) -> p h d", d=HD), t,
                                      qk_gain[:, ds(i, 1), :].broadcast_to([P, 8, HD]), ALU.mult).then_inc(SEM["rope"], 1)
                    dve.wait_ge(SEM["rope"], c.next("rope"))
                next_units(p)
        c.count("gen0")
        low(0)
        c.count("gen1")
        dve.wait_ge(SEM["used0"], c.so_far("used0"))
        for b in range(TB):
            ins = dve.tensor_tensor(flog[:, b, :], bank[2 * b][:, 0:FOX], fbias, ALU.add)
        ins.then_inc(SEM["gen0"], 1)
        dve.wait_ge(SEM["gen0"], c.next("gen0"))
        dve.scalar_tensor_tensor(fabs, flog, -1.0, flog, ALU.mult, ALU.max).then_inc(SEM["fabs"], 1)
        low(0)
        low(1)
        dve.wait_ge(SEM["fln"], c.next("fln"))
        dve.scalar_tensor_tensor(flog, flog, 0.0, fabs, ALU.min, ALU.subtract).then_inc(SEM["flog_ready"], 1)
        dve.wait_ge(SEM["cum_mm"], c.next("cum_mm"))
        dve.tensor_scalar(cumh, bank[1][0:FOX, 0:T], -1.0, None, ALU.mult).then_inc(SEM["dve"], 1)
        dve.wait_ge(SEM["dve"], c.next("dve"))
        dve.scalar_tensor_tensor(cuml, bank[1][0:FOX, 0:T], -1.0, cumh.bitcast(f32), ALU.mult, ALU.subtract)\
           .then_inc(SEM["cumT_ready"], 1)

        def maxima(hp):
            q = hp % 2
            dve.wait_ge(SEM[f"s_ready{q}"], c.next(f"s_ready{q}"))
            for j in range(4):
                at = slice(0, P) if j < 2 else slice(P, P + T)
                ins = dve.tensor_reduce(fatt[q][:, j:j + 1], bank[score_banks[q][j % 2]][:, at], X, ALU.max, negate=True)
            ins.then_inc(SEM["smax"], 1)

        def inverses(hp):
            q = hp % 2
            dve.wait_ge(SEM["e_ready"], c.next("e_ready", 4))
            dve.reciprocal(fatt[q][:, 8:12], fatt[q][:, 4:8]).then_inc(SEM["rinv"], 1)

        def take_turned():
            dve.wait_ge(SEM["eT1_tr"], c.next("eT1_tr"))
            dve.tensor_copy(feT[:, 1, :, :], bank[7][:, 0:384].rearrange("p (k t) -> p k t", k=3)).then_inc(SEM["eT1_ready"], 1)

        def take_output(i, hp):
            dve.wait_ge(SEM["rinv"], c.next("rinv"))
            dve.wait_ge(SEM["o_ready"], c.next("o_ready"))
            dve.tensor_tensor(y[:, :, ds(i * 512 + hp * P, P)].rearrange("p b (m e) -> p b m e", m=2),
                              bank[6][:, 0:T].rearrange("p (b m e) -> p b m e", b=TB, m=2),
                              fatt[hp % 2][:, 8:12].rearrange("p (b m a) -> p b m a", b=TB, a=1).broadcast_to([P, TB, 2, HD]),
                              ALU.mult).then_inc(SEM["o_out"], 1)
            c.count("o_out")

        with c.loop(2, "dve fox") as i:
            maxima(0)
            inverses(0)
            maxima(1)
            take_turned()
            inverses(1)
            take_output(i, 0)
            maxima(2)
            take_turned()
            inverses(2)
            maxima(3)
            take_output(i, 1)
            take_turned()
            c.count("gen0")
            low(0)
            inverses(3)
            take_output(i, 2)
            take_turned()
            low(1)
            take_output(i, 3)
        dve.wait_ge(SEM["o_out"], c.so_far("o_out"))
        for b in range(TB):
            dve.wait_ge(SEM["gate_on"], c.next("gate_on"))
            dve.tensor_tensor(y[:, b, :], y[:, b, :], fgate[:, b, :], ALU.mult).then_inc(SEM["hb_ready"], 1)
            transposed(b)
        low(2)
        low(3)
        next_units(0)
        two_norms(1.0)
        ffn(1.0)
        for b in range(TB):
            var_of(b, 0.5)
            if b == 0:
                dve.wait_ge(SEM["gains_ld"], c.next("gains_ld", 32))
            post(b, "done")

    def second_pe(c, pe, three, panel, panel_unit, up_unit, enter, ffn):
        c.count("e_ready", 4 * 8 * DEPTH)
        enter(y, "x_ready", False)
        ffn()
        enter(y, "x_ready", True)
        for p in (1, 0, 1, 0):
            panel(p)
        pe.wait_ge(SEM["ab_ld"], c.next("ab_ld", 16 * 17))
        pe.wait_ge(SEM["gen1"], c.so_far("gen1"))
        c.count("gen1")
        pe.wait_ge(SEM["lo2"], c.next("lo2"))
        for k in range(KT):
            for b in range(TB):
                t = slice(b * P, (b + 1) * P)
                r = slice(k * 256, (k + 1) * 256)
                ins = three(bank[2 * b + 1][:, 0:256], xTh[:, k, t], xTl[:, k, t], wh[2][:, r], wl[2][:, r], k == 0, k == KT - 1)
        ins.then_inc(SEM["used2"], 1)
        for ct in range(4):
            ins = pe.transpose(bank[4][:, ct * 32:(ct + 1) * 32], convw_rows[0:32, ct * P:(ct + 1) * P], ident[0:32, 0:32])
        ins.then_inc(SEM["cw_tr"], 1)
        pe.wait_ge(SEM["glu_ready"], c.next("glu_ready"))
        for b in range(TB):
            for ct in range(4):
                ins = pe.transpose(bank[6 + b][:, ct * P:(ct + 1) * P], glu[:, b, ct * P:(ct + 1) * P], ident[:, :])
            ins.then_inc(SEM["glu_tr"], 1)
        pe.wait_ge(SEM["cw_ready"], c.next("cw_ready"))
        pe.wait_ge(SEM["lora_ready"], c.next("lora_ready", 2))
        for w in range(2):
            for b in range(TB):
                ins = pe.transpose(bank[4][:, w * T + b * P:w * T + (b + 1) * P], lora[:, b, w * P:(w + 1) * P], ident[:, :])
        ins.then_inc(SEM["lora_tr"], 1)
        pe.wait_ge(SEM["loraT_ready"], c.next("loraT_ready"))
        pe.wait_ge(SEM["gen0"], c.so_far("gen0"))
        pe.wait_ge(SEM["gen1"], c.so_far("gen1"))
        for b in range(TB):
            t = slice(b * P, (b + 1) * P)
            pe.matmul(bank[3 * b][:, :], loraT[0:64, 0, t], lora_up[0:64, :], start=True, stop=True)
            pe.matmul(bank[3 * b + 1][:, :], loraT[64:128, 0, t], lora_up[64:128, :], start=True, stop=True)
            pe.matmul(bank[3 * b + 2][:, :], loraT[:, 1, t], gate_up, start=True, stop=True).then_inc(SEM["ups_ready"], 1)
        pe.wait_ge(SEM["sag_ready"], c.next("sag_ready", 2))
        pe.wait_ge(SEM["gluT_ready"], c.next("gluT_ready", 2))
        for j in range(4):
            for b in range(TB):
                ins = pe.matmul(bank[7][:, j * NCH + b * 8:j * NCH + (b + 1) * 8], st_sag[:, 0, b, j * P:(j + 1) * P],
                                chunk_mask, start=True, stop=True)
        ins.then_inc(SEM["tot_ready"], 1)
        pe.wait_ge(SEM["pc_ready"], c.next("pc_ready"))
        pe.wait_ge(SEM["sag_ld"], c.next("sag_ld", 48))
        for m, bk in ((0, 0), (2, 4), (1, 2)):
            for h in range(2):
                ins = pe.matmul(bank[bk + h][:, :], cum_mask[:, m, :],
                                rows_t[:, ROW_SIG, 8 * h:8 * h + 8, :].rearrange("p c n -> p (c n)"), start=True, stop=True)
            ins.then_inc(SEM["cum_ready"], 1)
        pe.wait_ge(SEM["e_done"], c.next("e_done"))

        def transpose_rows(q):
            pe.wait_ge(SEM[f"rkab_ready{q}"], c.next(f"rkab_ready{q}"))
            for w in range(3):
                ins = pe.transpose(bank[2 * q][:, w * P:(w + 1) * P], rkab[q][:, w, :], ident[:, :])
            ins.then_inc(SEM[f"rows_tr{q}"], 1)

        def grams(q):
            pe.wait_ge(SEM[f"rowsT_ready{q}"], c.next(f"rowsT_ready{q}"))
            (r0, a0, k0), (r1, a1, b1) = ([rowsT[q][h * HD:(h + 1) * HD, w, :] for w in range(3)] for h in range(2))
            g0, g1 = bank[2 * q], bank[2 * q + 1]
            for o, lhs, rhs in ((g1[:, 0:P], b1, r1), (g1[:, P:2 * P], b1, a1), (g1[:, 2 * P:3 * P], a1, b1),
                                (g0[:, 0:P], k0, r0), (g0[:, P:2 * P], k0, a0)):
                ins = pe.matmul(o, lhs, rhs, start=True, stop=True)
            ins.then_inc(SEM[f"gram_mm{q}"], 1)

        def powers(q, step):
            if step == 0:
                pe.wait_ge(SEM[f"gram_ready{q}"], c.next(f"gram_ready{q}"))
            else:
                pe.wait_ge(SEM[f"pw_ready{q}"], c.next(f"pw_ready{q}"))
                pe.wait_ge(SEM[f"inv_ready{q}"], c.next(f"inv_ready{q}"))
            o = bank[2 * q + step % 2]
            if step == 0:
                xx, xt = gram[q][:, 1, :], gram[q][:, 2, :]
            else:
                xx, xt = pw[q][:, 2 * step - 2, :], pw[q][:, 2 * step - 1, :] if step < 3 else None
            if step < 2:
                pe.matmul(o[:, 0:P], xt, xx, start=True, stop=True)
                pe.matmul(o[:, P:2 * P], xx, xt, start=True, stop=True).then_inc(SEM[f"pw_mm{q}"], 1)
            elif step == 2:
                pe.matmul(o[:, 0:P], xx, xt, start=True, stop=True).then_inc(SEM[f"pw_mm{q}"], 1)
            if step:
                pe.matmul(bank[2 * q + min(step - 1, 1)][:, 0:P], xt if step < 3 else xx, inv[q], start=True, stop=True)\
                  .then_inc(SEM[f"inv_mm{q}"], 1)

        def before_u(n, q):
            v_c = rows_t[:, ROW_V, ds(n, 1), :].rearrange("p a n -> p (a n)")
            pe.wait_ge(SEM[f"ra_ready{q}"], c.next(f"ra_ready{q}"))
            pe.wait_ge(SEM["m_new"], c.next("m_new"))
            for j in range(4):
                pe.matmul(bank[4][:, 0:HD], ra_exp[q][:, 1, j, :], state[:, j, :], start=(j == 0), stop=False)
            pe.matmul(bank[4][:, 0:HD], gram[q][:, 4, :], v_c, start=False, stop=True).then_inc(SEM["w_mm"], 1)
            pe.wait_ge(SEM["y_out"], c.so_far("y_out"))
            c.count("y_out")
            for j in range(4):
                pe.matmul(bank[6][:, 0:HD], ra_exp[q][:, 0, j, :], state[:, j, :], start=(j == 0), stop=False)
            pe.matmul(bank[6][:, 0:HD], gram[q][:, 3, :], v_c, start=False, stop=False)
            pe.wait_ge(SEM[f"exp_ready{q}"], c.next(f"exp_ready{q}"))
            for j in range(4):
                ins = pe.matmul(bank[5][:, j * HD:(j + 1) * HD], kt_exp[q][:, j * P:(j + 1) * P], v_c, start=True, stop=True)
            ins.then_inc(SEM["kv_mm"], 1)

        def u_of(q):
            pe.wait_ge(SEM["w_ready"], c.next("w_ready"))
            pe.wait_ge(SEM[f"inv_ready{q}"], c.next(f"inv_ready{q}"))
            pe.matmul(bank[4][:, HD:2 * HD], inv[q], w_s, start=True, stop=True).then_inc(SEM["u_mm"], 1)

        def after_u(q):
            pe.wait_ge(SEM["u_ready"], c.next("u_ready"))
            for j in range(4):
                ins = pe.matmul(bank[7][:, j * HD:(j + 1) * HD], bt_exp[q][:, j * P:(j + 1) * P], u_s, start=True, stop=True)
            ins.then_inc(SEM["m_mm"], 1)
            pe.matmul(bank[6][:, 0:HD], gram[q][:, 0, :], u_s, start=False, stop=True).then_inc(SEM["y_mm"], 1)

        for q in range(2):
            transpose_rows(q)
        for q in range(2):
            grams(q)
        for step in range(4):
            for q in range(2):
                powers(q, step)
        with c.loop(NCH // 2 - 1, "pe scan") as i:
            before_u(i * 2, 0)
            transpose_rows(0)
            u_of(0)
            transpose_rows(1)
            after_u(0)
            grams(0)
            before_u(i * 2 + 1, 1)
            grams(1)
            u_of(1)
            powers(0, 0)
            after_u(1)
            powers(0, 1)
            powers(1, 0)
            powers(0, 2)
            powers(1, 1)
            powers(0, 3)
            powers(1, 2)
            powers(1, 3)
        for q in range(2):
            before_u(NCH - 2 + q, q)
            u_of(q)
            after_u(q)
        for b in range(TB):
            for ct in range(4):
                ins = pe.transpose(bank[b][:, ct * P:(ct + 1) * P], conv_o[:, ct, b * P:(b + 1) * P], ident[:, :])
            ins.then_inc(SEM["convT"], 1)
        pe.wait_ge(SEM["yb_ready"], c.next("yb_ready", 2))
        pe.wait_ge(SEM["y_ld"], c.next("y_ld", 16))
        enter(lambda b, k: (y_rwkv if k < 4 else y_conv)[:, b, (k % 4) * P:(k % 4 + 1) * P], None, True)
        panel(1, True)
        enter(y, "x_ready", False)
        ffn()
        enter(y, "x_ready", False)
        ffn()
        enter(y, "x_ready", True)
        for i in range(2):
            if i:
                panel(0)
            panel(1)
            for r in range(4):
                pe.wait_ge(SEM["rope"], c.next("rope"))
                if r >= 2:
                    pe.wait_ge(SEM["qk_ready"], c.next("qk_ready"))
                for q in range(4):
                    ins = pe.transpose(bank[6 + r % 2][:, q * P:(q + 1) * P],
                                       y[:, r % 2, (r // 2) * HALF + q * P:(r // 2) * HALF + (q + 1) * P], ident[:, :])
                ins.then_inc(SEM["rope_tr"], 1)
            pe.wait_ge(SEM["qk_ready"], c.next("qk_ready", 2))
        panel(0)
        panel(1)
        pe.wait_ge(SEM["c_ld"], c.next("c_ld", 16 * 6))
        pe.wait_ge(SEM["gen0"], c.so_far("gen0"))
        c.count("gen0")
        pe.wait_ge(SEM["lo0"], c.next("lo0"))
        for k in range(KT):
            for b in range(TB):
                t = slice(b * P, (b + 1) * P)
                r = slice(k * FOX, (k + 1) * FOX)
                ins = three(bank[2 * b][:, 0:FOX], xTh[:, k, t], xTl[:, k, t], wh[0][:, r], wl[0][:, r], k == 0, k == KT - 1)
        ins.then_inc(SEM["used0"], 1)
        pe.wait_ge(SEM["gen1"], c.so_far("gen1"))
        pe.wait_ge(SEM["flog_ready"], c.next("flog_ready"))
        pe.matmul(bank[1][0:FOX, 0:P], flog[:, 0, :], tri_c, start=True, stop=True)
        pe.matmul(bank[1][0:FOX, P:T], flog[:, 0, :], ones_c, start=True, stop=False)
        pe.matmul(bank[1][0:FOX, P:T], flog[:, 1, :], tri_c, start=False, stop=True).then_inc(SEM["cum_mm"], 1)
        pe.wait_ge(SEM["cumT_ready"], c.next("cumT_ready"))

        def scores(hp):
            q = hp % 2
            pe.wait_ge(SEM["qh_ready"], c.next("qh_ready"))
            for m in range(2):
                f = slice(m * HD, (m + 1) * HD)
                pair = selh[q][:, m * P:(m + 1) * P]
                for at, t, n in ((0, slice(0, P), P), (P, slice(P, T), T)):
                    o = bank[score_banks[q][m]][:, at:at + n]
                    pe.matmul(o, identb, negm_wide[:, T - n:T], start=True, stop=False)
                    pe.matmul(o, pair, cumh[:, 0:n], start=False, stop=False)
                    pe.matmul(o, pair, cuml[:, 0:n], start=False, stop=False)
                    ins = pe.matmul(o, qh[q][f, t], kh[q][f, 0:n], start=False, stop=True)
            ins.then_inc(SEM[f"s_ready{q}"], 1)

        def turn():
            pe.wait_ge(SEM["e_ready"], c.next("e_ready", 4))
            pe.wait_ge(SEM["o_out"], c.so_far("o_out"))
            c.count("o_out")
            for m, bk, to in ((1, 7, "eT1_tr"), (0, 6, "eT_tr")):
                for j in range(3):
                    ins = pe.transpose(bank[bk][:, j * P:(j + 1) * P], fe_t[:, m, j * P:(j + 1) * P], ident[:, :])
                ins.then_inc(SEM[to], 1)

        def outputs(i, hp):
            pe.wait_ge(SEM["aT_ready"], c.next("aT_ready"))
            pe.wait_ge(SEM["eT1_ready"], c.next("eT1_ready"))
            for b in range(TB):
                for m in range(2):
                    o = bank[6][:, (2 * b + m) * HD:(2 * b + m + 1) * HD]
                    for j in range(b + 1):
                        ins = pe.matmul(o, feT[:, m, b + j, :], fval[:, j, ds(i * 512 + hp * P + m * HD, HD)],
                                        start=(j == 0), stop=(j == b))
            ins.then_inc(SEM["o_ready"], 1)

        with c.loop(2, "pe fox") as i:
            scores(0)
            panel_unit(0, 0)
            scores(1)
            turn()
            panel_unit(0, 1)
            outputs(i, 0)
            scores(2)
            turn()
            scores(3)
            outputs(i, 1)
            turn()
            outputs(i, 2)
            turn()
            outputs(i, 3)
        enter(y, "hb_ready", True)
        panel(1, True)
        enter(y, "x_ready", False)
        ffn()


    @block.sync
    def _(sp):
        c = Counts(sp, SEM["held"])

        def load(s, *pieces):
            sp.wait_ge(SEM[f"lo{s}"], c.so_far(f"lo{s}"))
            c.count(f"lo{s}")
            for dst, src in pieces:
                sp.dma_start(dst, src).then_inc(SEM[f"ld{s}"], 16)

        def rows(w):
            return w.rearrange("(k p) n -> p k n", p=P)

        def up(w1, w3, j):
            for s in range(2):
                dst = wf[s][:, :].rearrange("p (k n) -> p k n", k=4)
                load(s, *((dst[:, :, m * STEP:(m + 1) * STEP],
                           rows(w)[:, 4 * s:4 * s + 4, ds(j * STEP, STEP)]) for m, w in enumerate((w1, w3))))

        def down(w2, j, s=2):
            load(s, (wf[s][:, :].rearrange("p (k n) -> p k n", k=2), rows(w2[ds(j * STEP, STEP), :])))

        def half_panel(w, col, s, h):
            load(s, (wf[s][:, :].rearrange("p (k n) -> p k n", k=4), rows(w)[:, 4 * h:4 * h + 4, ds(col, HALF)]))

        def ffn(w1, w3, w2):
            up(w1, w3, 0)
            with c.loop(STEPS - 1, "sp ffn") as j:
                up(w1, w3, j + 1)
                down(w2, j)
            down(w2, STEPS - 1, 3)

        def two_panels(w, col):
            for s in range(4):
                half_panel(w, col + HALF * (s // 2), s, s % 2)

        def layer_of(name, l):
            w = a[name][ds(l, 1)]
            return w.rearrange("a f k n -> (a f) k n") if len(w.shape) == 4 else w.rearrange("a k n -> (a k) n")

        for n in STARTED:
            sp.sem_inc(SEM[n], 1 + TB if n == "x_ready" else 1)
        sp.dma_start(x[:, :, :], a["x"][0].rearrange("(b p) n -> p b n", p=P)).then_inc(SEM["x_ld"], 16)
        with c.loop(DEPTH, "sp layer") as l:
            w1, w3, w2 = (layer_of(n, l) for n in ("ffn_w1", "ffn_w3", "ffn_w2"))
            w_in, w_br, w_out = (layer_of(n, l) for n in ("w_in", "w_branch", "w_out"))
            ffn(w1[0], w3[0], w2[0])
            two_panels(w_in, 0)
            two_panels(w_in, D)
            with c.loop(2, "sp four") as i:
                two_panels(w_in, i * D + 2 * D)
            two_panels(w_in, 4 * D)
            with c.loop(2, "sp four") as i:
                two_panels(w_in, i * D + 5 * D)
            two_panels(w_br[0], 0)
            two_panels(w_br[1], 0)
            two_panels(w_out, 0)
            ffn(w1[1], w3[1], w2[1])
        second_sp(c, sp, ffn, half_panel, load, rows)

    @block.gpsimd
    def _(pool):
        c = Counts(pool, SEM["held"])

        def gains_load(*rows_):
            for i, r in enumerate(rows_):
                pool.dma_start(gains[:, i, :], bcast_row(r, D)).then_inc(SEM["gains_ld"], 16)

        def power(dst, src, n, got, to):
            pool.wait_ge(SEM[got], c.next(got))
            pool.tensor_tensor(dst, src, mhalf[:, 0:n], ALU.pow).then_inc(SEM[to], 1)

        def norm():
            for b in range(TB):
                power(rstd[:, b:b + 1], ve[:, b:b + 1], 1, "var", "rstd")

        def pre_norm():
            for b in range(TB):
                power(rstd[:, b:b + 1], ve[:, b:b + 1], 1, "pre_var", "pre_rstd")

        def of_layer(name, l):
            return a[name][ds(l, 1)].rearrange("a k n -> (a k) n")

        def ln_rows(l, i):
            gains_load(of_layer("ln_g", l)[i:i + 1, :], of_layer("ln_b", l)[i:i + 1, :])

        constants = ((ident[:, :], a["c_ident"]), (mhalf[:, :], a["c_mhalf"]), (cs, a["c_rope"]),
                     (tri, a["c_tri"]), (laminit, a["c_laminit"]), (negm_f, a["c_negm"]), (identb_f, a["c_identb"]))
        for dst, src in constants:
            pool.dma_start(dst, src).then_inc(SEM["const_ld"], 16)
        pool.wait_ge(SEM["const_ld"], c.next("const_ld", 16 * 7))

        with c.loop(DEPTH, "pool layer") as l:
            pool.wait_ge(SEM["x_ready"], c.so_far("x_ready"))
            ln_rows(l, 0)
            norm()
            pool.wait_ge(SEM["x_ready"], c.next("x_ready", TB))
            gb = of_layer("gate_b", l)
            gains_load(gb[0:1, :], gb[1:2, :])
            for dst, src in ((sgu_gb[:, 0, :], bcast_row(a["sgu_ln_g"][ds(l, 1), :], D)),
                             (sgu_gb[:, 1, :], bcast_row(a["sgu_ln_b"][ds(l, 1), :], D)),
                             (sgu_w, a["sgu_w"][ds(l, 1)].rearrange("a g t r -> t (a g) r")),
                             (sgu_bT, a["sgu_b"][ds(l, 1)].rearrange("a g t -> t (a g)")),
                             (part(14728, 256), bcast_row(a["lam"][ds(l, 1)].rearrange("a k n -> a (k n)"), 256)),
                             (dgain, bcast_row(a["diff_ln_g"][ds(l, 1), :], P))):
                pool.dma_start(dst, src).then_inc(SEM["sgu_ld"], 16)
            for b in range(TB):
                power(rstd[:, b:b + 1], ve[:, b:b + 1], 1, "var", "rstd")
            pool.wait_ge(SEM["qk_ready"], c.next("qk_ready", 8))
            with c.loop(2, "pool att") as i:
                for hh in range(4):
                    q = hh % 2
                    pool.wait_ge(SEM[f"s_ready{q}"], c.so_far(f"s_ready{q}"))
                    c.count(f"s_ready{q}")
                    head = [qkT[:, w, ds(i * 4 + hh, 1), :].rearrange("p a t -> p (a t)") for w in range(2)]
                    pool.tensor_tensor(qh[q], head[0], scale.broadcast_to([P, T]), ALU.mult)
                    pool.tensor_copy(kh[q], head[1]).then_inc(SEM["qh_ready"], 1)
            power(orstd, oss, 16, "o_var", "o_rstd")
            pool.wait_ge(SEM["m_ready"], c.next("m_ready", TB))
            ln_rows(l, 1)
            norm()
            pool.wait_ge(SEM["x_ready"], c.next("x_ready", TB))
            ln_rows(l, 2)
            norm()
            c.count("x_ready", TB)
        second_pool(c, pool, gains_load, power, norm, pre_norm)

    @block.scalar
    def _(act):
        c = Counts(act, SEM["held"])

        def prep(s, dmas=1):
            act.wait_ge(SEM[f"ld{s}"], c.next(f"ld{s}", 16 * dmas))
            act.wait_ge(SEM[f"used{s}"], c.so_far(f"used{s}"))
            c.count(f"used{s}")
            act.activation(wh[s][:, :], wf[s][:, :], ACT.Copy).then_inc(SEM[f"hi{s}"], 1)

        def transposed(*blocks):
            for r in (2 * b + h for b in blocks or range(TB) for h in range(2)):
                act.wait_ge(SEM["tr"], c.next("tr"))
                act.activation(xTh[:, 4 * (r % 2):4 * (r % 2) + 4, (r // 2) * P:(r // 2 + 1) * P],
                               bank[6 + r % 2][:, :].rearrange("p (k t) -> p k t", k=4), ACT.Copy)\
                   .then_inc(SEM["xt_hi"], 1)

        def ffn_step(last):
            if last:
                prep(3)
            else:
                prep(0, 2)
            act.wait_ge(SEM["used1"], c.so_far("used1"))
            for b in range(TB):
                act.activation(sil[:, b, :], bank[4 + b][:, 0:STEP], ACT.Silu).then_inc(SEM["h_silu"], 1)
            if not last:
                prep(1, 2)
            act.wait_ge(SEM["ht_tr"], c.next("ht_tr"))
            act.activation(hTh[:, :, :], bank[6][:, :].rearrange("p (k t) -> p k t", k=2), ACT.Copy)\
               .then_inc(SEM["ht_hi"], 1)
            if not last:
                prep(2)

        def ffn(then):
            with c.loop(STEPS - 1, "act ffn"):
                ffn_step(False)
            ffn_step(True)
            for p in range(2):
                c.count(f"gen{p}")
            for s, dmas in then:
                prep(s, dmas)

        def panel_evac(p, fn):
            act.wait_ge(SEM[f"used{2 * p + 1}"], c.so_far(f"used{2 * p + 1}"))
            for b in range(TB):
                ins = fn(b, bank[2 * b + p][:, :])
            ins.then_inc(SEM[f"gen{p}"], 1)
            c.count(f"gen{p}")

        def next_units(p, dmas=1):
            prep(2 * p, dmas)
            prep(2 * p + 1, dmas)

        act.wait_ge(SEM["const_ld"], c.next("const_ld", 16 * 7))
        prep(0, 2)
        prep(1, 2)
        act.wait_ge(SEM["x_ld"], c.next("x_ld", 16))

        with c.loop(DEPTH, "act layer") as l:
            transposed()
            ffn([(0, 1), (1, 1), (2, 1)])
            transposed()
            prep(3)
            with c.loop(2, "act uv") as i:
                for p in range(2):
                    panel_evac(p, lambda b, t: act.activation(
                        uv[:, ds(i, 1), b, p * HALF:(p + 1) * HALF], t.rearrange("p (a n) -> p a n", a=1), ACT.Gelu))
                    next_units(p)
            act.wait_ge(SEM["lam_s"], c.next("lam_s"))
            act.activation(lam_c[:, 0:2], lam_c[:, 0:2], ACT.Exp).then_inc(SEM["lam_e"], 1)
            with c.loop(2, "act qk") as i:
                for p in range(2):
                    c.count(f"gen{p}")
                    next_units(p)
                for r in range(4):
                    act.wait_ge(SEM["rope_tr"], c.next("rope_tr"))
                    act.activation(qkT[:, ds(i, 1), 4 * (r // 2):4 * (r // 2) + 4, (r % 2) * P:(r % 2 + 1) * P],
                                   bank[6 + r % 2][:, :].rearrange("p (a h t) -> p a h t", a=1, h=4), ACT.Copy)\
                       .then_inc(SEM["qk_ready"], 1)
            for p in range(2):
                panel_evac(p, lambda b, t: act.activation(val[:, b, p * HALF:(p + 1) * HALF], t, ACT.Copy))
                next_units(p)
            def exps(hh):
                act.wait_ge(SEM["smax"], c.next("smax"))
                act.wait_ge(SEM["a_ready"], c.so_far("a_ready"))
                c.count("a_ready")
                for j in range(4):
                    at = slice(0, P) if j < 2 else slice(P, P + T)
                    act.activation(e_t[:, j % 2, at], bank[score_banks[hh % 2][j % 2]][:, at], ACT.Exp, bias=att[:, j:j + 1],
                                   accum_out=att[:, 4 + j:5 + j]).then_inc(SEM["e_ready"], 1)

            def take_turned():
                act.wait_ge(SEM["a_tr"], c.next("a_tr"))
                act.activation(aT, bank[6][:, 0:384].rearrange("p (k t) -> p k t", k=3), ACT.Copy).then_inc(SEM["aT_ready"], 1)

            def take_output(i, hh):
                act.wait_ge(SEM["o_ready"], c.next("o_ready"))
                act.activation(y[:, :, ds(i * 512 + hh * P, P)], bank[7][:, 0:T].rearrange("p (b e) -> p b e", b=TB), ACT.Copy)\
                   .then_inc(SEM["o_out"], 1)
                c.count("o_out")

            with c.loop(2, "act att") as i:
                for hh in range(4):
                    exps(hh)
                    if hh:
                        take_output(i, hh - 1)
                    if hh == 1:
                        c.count("gen0")
                        next_units(0)
                    take_turned()
                c.count("gen0")
                next_units(1)
                take_output(i, 3)
            transposed()
            act.wait_ge(SEM["o_out"], c.so_far("o_out"))
            act.activation(osq, y[:, :, :], ACT.Square).then_inc(SEM["o_sq"], 1)
            act.wait_ge(SEM["gen0"], c.so_far("gen0"))
            act.wait_ge(SEM["gen1"], c.so_far("gen1"))
            for g in gate:
                act.activation(g, g, ACT.Sigmoid).then_inc(SEM["gate_on"], 1)
            for br in range(2):
                for p in range(2):
                    c.count(f"gen{p}")
                next_units(0)
                transposed()
                next_units(1)
            next_units(0, 2)
            for p in range(2):
                c.count(f"gen{p}")
            transposed()
            ffn([(0, 2), (1, 2)])
        second_act(c, act, prep, next_units, panel_evac, transposed, ffn)

    @block.vector
    def _(dve):
        c = Counts(dve, SEM["held"])


        def low(s):
            dve.wait_ge(SEM[f"hi{s}"], c.next(f"hi{s}"))
            c.count(f"used{s}")
            dve.tensor_tensor(wl[s][:, :], wf[s][:, :], wh[s][:, :].bitcast(f32), ALU.subtract).then_inc(SEM[f"lo{s}"], 1)

        def next_units(p):
            low(2 * p)
            low(2 * p + 1)

        def transposed(*blocks):
            for r in (2 * b + h for b in blocks or range(TB) for h in range(2)):
                dve.wait_ge(SEM["xt_hi"], c.next("xt_hi"))
                at = slice(4 * (r % 2), 4 * (r % 2) + 4), slice((r // 2) * P, (r // 2 + 1) * P)
                dve.tensor_tensor(xTl[:, at[0], at[1]], bank[6 + r % 2][:, :].rearrange("p (k t) -> p k t", k=4),
                                  xTh[:, at[0], at[1]].bitcast(f32), ALU.subtract).then_inc(SEM["xt_ready"], 1)

        def ffn_step(last, half):
            low(3 if last else 0)
            for b in range(TB):
                dve.wait_ge(SEM["h_silu"], c.next("h_silu"))
                ins = dve.scalar_tensor_tensor(hid[:, b, :], sil[:, b, :], half, bank[4 + b][:, STEP:2 * STEP],
                                               ALU.mult, ALU.mult)
            ins.then_inc(SEM["h_ready"], 1)
            if not last:
                low(1)
            dve.wait_ge(SEM["ht_hi"], c.next("ht_hi"))
            dve.tensor_tensor(hTl[:, :, :], bank[6][:, :].rearrange("p (k t) -> p k t", k=2),
                              hTh[:, :, :].bitcast(f32), ALU.subtract).then_inc(SEM["ht_ready"], 1)
            if not last:
                low(2)

        def ffn(half):
            with c.loop(STEPS - 1, "dve ffn"):
                ffn_step(False, half)
            ffn_step(True, half)

        def moments(src, b):
            for h in range(2):
                ins = dve.bn_stats(stats[:, h, :], src[:, b, h * HALF:(h + 1) * HALF])
            ins.then_inc(SEM["dve"], 1)
            dve.wait_ge(SEM["dve"], c.next("dve"))
            c.hold()
            dve.bn_aggr(mv[:, b, :], stats[:, :, :].rearrange("p a b -> p (a b)")).then_inc(SEM["dve"], 1)
            dve.wait_ge(SEM["dve"], c.next("dve"))
            dve.tensor_scalar(ve[:, b:b + 1], mv[:, b, 1:2], LN_EPS, None, ALU.add).then_inc(SEM["var"], 1)

        def normalise(dst, src, gb, b, to):
            dve.scalar_tensor_tensor(src[:, b, :], src[:, b, :], mv[:, b, 0:1], gb[:, 0, :], ALU.subtract, ALU.mult)\
               .then_inc(SEM["dve"], 1)
            dve.wait_ge(SEM["dve"], c.next("dve"))
            dve.wait_ge(SEM["rstd"], c.next("rstd"))
            dve.scalar_tensor_tensor(dst[:, b, :], src[:, b, :], rstd[:, b:b + 1], gb[:, 1, :], ALU.mult, ALU.add)\
               .then_inc(SEM[to], 1)

        def post_norm(and_transposed=True):
            for b in range(TB):
                if b == 0:
                    dve.wait_ge(SEM["half"], c.next("half"))
                else:
                    dve.wait_ge(SEM["used3"], c.so_far("used3"))
                for h in range(2):
                    ins = dve.scalar_tensor_tensor(y[:, b, h * HALF:(h + 1) * HALF], x[:, b, h * HALF:(h + 1) * HALF],
                                                   ALPHA, bank[2 * b + h][:, :], ALU.mult, ALU.add)
                    if b == TB - 1:
                        ins.then_inc(SEM[f"gen{h}"], 1)
                        dve.wait_ge(SEM[f"gen{h}"], c.next(f"gen{h}"))
                    else:
                        ins.then_inc(SEM["dve"], 1)
                        dve.wait_ge(SEM["dve"], c.next("dve"))
                moments(y, b)
                if b == 0:
                    dve.wait_ge(SEM["gains_ld"], c.next("gains_ld", 32))
                normalise(x, y, gains, b, "x_ready")
                c.count("x_ready")
                if and_transposed:
                    transposed(b)

        dve.wait_ge(SEM["const_ld"], c.next("const_ld", 16 * 7))
        low(0)
        low(1)

        with c.loop(DEPTH, "dve layer") as l:
            transposed()
            ffn(0.5)
            low(0)
            low(1)
            low(2)
            post_norm()
            low(3)
            with c.loop(2, "dve uv"):
                for p in range(2):
                    c.count(f"gen{p}")
                    next_units(p)
            dve.wait_ge(SEM["gen0"], c.so_far("gen0"))
            dve.wait_ge(SEM["gen1"], c.so_far("gen1"))
            dve.wait_ge(SEM["sgu_ld"], c.next("sgu_ld", 16 * 6))
            for b in range(TB):
                moments(v_t, b)
            for b in range(TB):
                normalise(v_t, v_t, sgu_gb, b, "v_ready")
            lam4 = part(14728, 2, 2, HD)
            dve.tensor_tensor(lam4[:, :, 0, :], lam4[:, :, 0, :], lam4[:, :, 1, :], ALU.mult).then_inc(SEM["dve"], 1)
            dve.wait_ge(SEM["dve"], c.next("dve"))
            dve.tensor_reduce(lam_c[:, 0:2], lam4[:, :, 0, :], X, ALU.add).then_inc(SEM["lam_s"], 1)
            with c.loop(2, "dve qk") as i:
                for p in range(2):
                    dve.wait_ge(SEM[f"used{2 * p + 1}"], c.so_far(f"used{2 * p + 1}"))
                    for b in range(TB):
                        src = bank[2 * b + p][:, :].rearrange("p (h m d) -> p h m d", m=2, d=HD // 2)
                        r2 = rope2.rearrange("p (h m d) -> p h m d", m=2, d=HD // 2)
                        cos = cs[:, 0:1, b, :].broadcast_to([P, 8, HD])
                        sin = cs[:, 1:2, b, :].rearrange("p a (m d) -> p a m d", m=2)
                        dve.tensor_tensor(rope1.rearrange("p (h d) -> p h d", d=HD), src.rearrange("p h m d -> p h (m d)"),
                                          cos, ALU.mult)
                        for m in range(2):
                            ins = dve.tensor_tensor(r2[:, :, m, :], src[:, :, 1 - m, :],
                                                    sin[:, :, m, :].broadcast_to([P, 8, HD // 2]), ALU.mult)
                        if b == TB - 1:
                            ins.then_inc(SEM[f"gen{p}"], 1)
                            dve.wait_ge(SEM[f"gen{p}"], c.next(f"gen{p}"))
                        else:
                            ins.then_inc(SEM["dve"], 1)
                            dve.wait_ge(SEM["dve"], c.next("dve"))
                        dve.tensor_tensor(y[:, b, p * HALF:(p + 1) * HALF], rope1, rope2, ALU.add).then_inc(SEM["rope"], 1)
                        dve.wait_ge(SEM["rope"], c.next("rope"))
                    next_units(p)
            dve.wait_ge(SEM["lam_e"], c.next("lam_e"))
            dve.tensor_tensor(lam_c[:, 2:3], lam_c[:, 1:2], lam_c[:, 0:1], ALU.subtract).then_inc(SEM["dve"], 1)
            dve.wait_ge(SEM["dve"], c.next("dve"))
            dve.tensor_tensor(lam_c[:, 2:3], lam_c[:, 2:3], laminit[:, ds(l, 1), 0], ALU.subtract)\
               .then_inc(SEM["dve"], 1)
            dve.wait_ge(SEM["dve"], c.next("dve"))
            for r in range(2):
                dve.wait_ge(SEM["sgw_tr"], c.next("sgw_tr"))
                dve.tensor_tensor(sgu_wT[:, 4 * r:4 * r + 4, :], bank[6 + r][:, :].rearrange("p (g t) -> p g t", g=4),
                                  tri[:, :].rearrange("p (a t) -> p a t", a=1).broadcast_to([P, 4, P]), ALU.mult)\
                   .then_inc(SEM["sgw_ready"], 1)
            for b in range(TB):
                dve.wait_ge(SEM["sgu_mm"], c.next("sgu_mm"))
                for g in range(GROUPS):
                    at = slice(g * P, (g + 1) * P)
                    ins = dve.scalar_tensor_tensor(u_t[:, b, at], bank[4 + 2 * b + g // 4][:, (g % 4) * P:(g % 4 + 1) * P],
                                                   sgu_bT[:, g:g + 1], u_t[:, b, at], ALU.add, ALU.mult)
                ins.then_inc(SEM["ha_ready"], 1)
            for p in range(2):
                c.count(f"gen{p}")
                next_units(p)
            dve.wait_ge(SEM["gains_ld"], c.next("gains_ld", 32))
            def maxima(hh):
                dve.wait_ge(SEM[f"s_ready{hh % 2}"], c.next(f"s_ready{hh % 2}"))
                for j in range(4):
                    at = slice(0, P) if j < 2 else slice(P, P + T)
                    ins = dve.tensor_reduce(att[:, j:j + 1], bank[score_banks[hh % 2][j % 2]][:, at], X, ALU.max, negate=True)
                ins.then_inc(SEM["smax"], 1)

            def combine():
                dve.wait_ge(SEM["e_ready"], c.next("e_ready", 4))
                dve.reciprocal(att[:, 8:12], att[:, 4:8]).then_inc(SEM["dve"], 1)
                dve.wait_ge(SEM["dve"], c.next("dve"))
                dve.tensor_scalar(att[:, 9:12:2], att[:, 9:12:2], lam_c[:, 2:3], None, ALU.mult).then_inc(SEM["dve"], 1)
                dve.wait_ge(SEM["dve"], c.next("dve"))
                dve.tensor_scalar(e_t[:, 1, 0:P], e_t[:, 1, 0:P], att[:, 9:10], None, ALU.mult)
                dve.tensor_scalar(e_t[:, 1, P:P + T], e_t[:, 1, P:P + T], att[:, 11:12], None, ALU.mult)\
                   .then_inc(SEM["dve"], 1)
                dve.wait_ge(SEM["dve"], c.next("dve"))
                dve.wait_ge(SEM["a_tr"], c.so_far("a_tr"))
                c.count("a_tr")
                dve.scalar_tensor_tensor(a_t[:, 0:P], e_t[:, 0, 0:P], att[:, 8:9], e_t[:, 1, 0:P], ALU.mult, ALU.add)
                dve.scalar_tensor_tensor(a_t[:, P:P + T], e_t[:, 0, P:P + T], att[:, 10:11], e_t[:, 1, P:P + T],
                                         ALU.mult, ALU.add).then_inc(SEM["a_ready"], 1)

            def gate_panel(i, p):
                dve.wait_ge(SEM[f"used{2 * p + 1}"], c.so_far(f"used{2 * p + 1}"))
                for b in range(TB):
                    ins = dve.tensor_tensor(arena[:, ds(i * 8192 + 2048 + b * D + p * HALF, HALF)], bank[2 * b][:, :],
                                            gains[:, ds(i, 1), p * HALF:(p + 1) * HALF].rearrange("p a n -> p (a n)"), ALU.add)
                ins.then_inc(SEM["gen0"], 1)
                c.count("gen0")

            with c.loop(2, "dve att") as i:
                for hh in range(4):
                    maxima(hh)
                    if hh == 2:
                        low(0)
                    combine()
                    if hh == 1:
                        gate_panel(i, 0)
                    if hh == 2:
                        low(1)
                gate_panel(i, 1)
                low(2)
                low(3)
            transposed()
            dve.wait_ge(SEM["o_sq"], c.next("o_sq"))
            dve.tensor_reduce(oss, part(4096, 16, P), X, ALU.add).then_inc(SEM["dve"], 1)
            dve.wait_ge(SEM["dve"], c.next("dve"))
            dve.tensor_scalar(oss, oss, 1.0 / P, LN_EPS, ALU.mult, ALU.add).then_inc(SEM["o_var"], 1)
            dve.wait_ge(SEM["o_rstd"], c.next("o_rstd"))
            dve.tensor_scalar(orstd, orstd, laminit[:, ds(l, 1), 1], None, ALU.mult).then_inc(SEM["dve"], 1)
            dve.wait_ge(SEM["dve"], c.next("dve"))
            yh = y[:, :, :].rearrange("p b (h e) -> p (b h) e", e=P)
            for b in range(TB):
                hs = slice(8 * b, 8 * b + 8)
                dve.tensor_tensor(yh[:, hs, :], yh[:, hs, :],
                                  orstd[:, hs].rearrange("p (h a) -> p h a", a=1).broadcast_to([P, 8, P]), ALU.mult)\
                   .then_inc(SEM["dve"], 1)
                dve.wait_ge(SEM["dve"], c.next("dve"))
                dve.tensor_tensor(yh[:, hs, :], yh[:, hs, :], dgain.rearrange("p (a e) -> p a e", a=1).broadcast_to([P, 8, P]),
                                  ALU.mult).then_inc(SEM["hb_ready"], 1)
            dve.wait_ge(SEM["gate_on"], c.next("gate_on", 2))
            for br in range(2):
                for p in range(2):
                    dve.wait_ge(SEM[f"used{2 * p + 1}"], c.so_far(f"used{2 * p + 1}"))
                    for b in range(TB):
                        g = gate[br][:, b, p * HALF:(p + 1) * HALF]
                        ins = dve.tensor_tensor(g, g, bank[2 * b + p][:, :], ALU.mult)
                    ins.then_inc(SEM[f"gen{p}"], 1)
                    dve.wait_ge(SEM[f"gen{p}"], c.next(f"gen{p}"))
                    if p == 0:
                        next_units(0)
                for b in range(TB):
                    if br:
                        dve.tensor_tensor(gate[0][:, b, :], gate[0][:, b, :], gate[1][:, b, :], ALU.add)\
                           .then_inc(SEM["m_ready"], 1)
                    transposed(b)
                next_units(1)
            next_units(0)
            post_norm()
            ffn(0.5)
            next_units(0)
            post_norm(False)
        second_dve(c, dve, low, next_units, transposed, ffn, moments)

    @block.tensor
    def _(pe):
        c = Counts(pe, SEM["held"])

        def three(o, lh, ll, rh, rl, start, stop):
            pe.matmul(o, lh, rh, start=start, stop=False)
            pe.matmul(o, lh, rl, start=False, stop=False)
            return pe.matmul(o, ll, rh, start=False, stop=stop)

        def up_unit(s, h, out0, blocks=(0, 1), half=False):
            if 0 in blocks:
                pe.wait_ge(SEM[f"lo{s}"], c.next(f"lo{s}"))
            steps = [(b, q) for b in blocks for q in range(4)] if half else [(b, q) for q in range(4) for b in blocks]
            for b, q in steps:
                k = 4 * h + q
                r = slice(q * HALF, (q + 1) * HALF)
                t = slice(b * P, (b + 1) * P)
                ins = three(out0(b), xTh[:, k, t], xTl[:, k, t], wh[s][:, r], wl[s][:, r], k == 0, k == KT - 1)
                if half and (b, q) == (0, 3):
                    ins.then_inc(SEM["half"], 1)
            if TB - 1 in blocks:
                ins.then_inc(SEM[f"used{s}"], 1)

        def panel_unit(p, h, at=None, half=False):
            at = p if at is None else at
            if h == 0:
                pe.wait_ge(SEM[f"gen{at}"], c.so_far(f"gen{at}"))
                c.count(f"gen{at}")
            up_unit(2 * p + h, h, lambda b: bank[2 * b + at][:, :], half=half)

        def panel(p, half=False):
            panel_unit(p, 0)
            panel_unit(p, 1, half=half)

        def up():
            for h in range(2):
                up_unit(h, h, lambda b: bank[4 + b][:, :])

        def down(first, last):
            if first:
                for p in range(2):
                    pe.wait_ge(SEM[f"gen{p}"], c.so_far(f"gen{p}"))
                    c.count(f"gen{p}")
            pe.wait_ge(SEM["ht_ready"], c.next("ht_ready"))
            s = 3 if last else 2
            pe.wait_ge(SEM[f"lo{s}"], c.next(f"lo{s}"))
            for b in range(TB):
                t = slice(b * P, (b + 1) * P)
                for k in range(2):
                    for n in range(2):
                        r = slice(k * D + n * HALF, k * D + (n + 1) * HALF)
                        ins = three(bank[2 * b + n][:, :], hTh[:, k, t], hTl[:, k, t], wh[s][:, r], wl[s][:, r],
                                    first and k == 0, last and k == 1)
                if last and b == 0:
                    ins.then_inc(SEM["half"], 1)
            ins.then_inc(SEM[f"used{s}"], 1)

        def hidden():
            pe.wait_ge(SEM["h_ready"], c.next("h_ready"))
            for k in range(2):
                for b in range(TB):
                    ins = pe.transpose(bank[6][:, k * T + b * P:k * T + (b + 1) * P], hid[:, b, k * P:(k + 1) * P], ident[:, :])
            ins.then_inc(SEM["ht_tr"], 1)

        def ffn():
            hidden()
            up()
            down(True, False)
            hidden()
            with c.loop(STEPS - 2, "pe ffn"):
                up()
                down(False, False)
                hidden()
            down(False, True)

        def enter(src, ready, to_panel):
            for b in range(TB):
                if ready:
                    pe.wait_ge(SEM[ready], c.next(ready))
                for r in range(2):
                    for q in range(4):
                        k = 4 * r + q
                        ins = pe.transpose(bank[6 + r][:, q * P:(q + 1) * P],
                                           src(b, k) if callable(src) else src[:, b, k * P:(k + 1) * P], ident[:, :])
                    ins.then_inc(SEM["tr"], 1)
                pe.wait_ge(SEM["xt_ready"], c.next("xt_ready", 2))
                if to_panel and b == 0:
                    pe.wait_ge(SEM["gen0"], c.so_far("gen0"))
                    c.count("gen0")
                for h in range(2):
                    up_unit(h, h, lambda b: bank[2 * b if to_panel else 4 + b][:, :], (b,))

        pe.wait_ge(SEM["const_ld"], c.next("const_ld", 16 * 7))
        pe.wait_ge(SEM["x_ld"], c.next("x_ld", 16))
        c.seen["x_ready"] = 1

        with c.loop(DEPTH, "pe layer") as l:
            enter(x, "x_ready", False)
            ffn()
            enter(x, "x_ready", True)
            panel(1)
            panel(0)
            panel(1)
            with c.loop(2, "pe qk"):
                panel(0)
                panel(1)
                for r in range(4):
                    pe.wait_ge(SEM["rope"], c.next("rope"))
                    if r >= 2:
                        pe.wait_ge(SEM["qk_ready"], c.next("qk_ready"))
                    for q in range(4):
                        ins = pe.transpose(bank[6 + r % 2][:, q * P:(q + 1) * P],
                                           y[:, r % 2, (r // 2) * HALF + q * P:(r // 2) * HALF + (q + 1) * P], ident[:, :])
                    ins.then_inc(SEM["rope_tr"], 1)
                pe.wait_ge(SEM["qk_ready"], c.next("qk_ready", 2))
            pe.wait_ge(SEM["sgu_ld"], c.next("sgu_ld", 16 * 6))
            for r in range(2):
                for q in range(4):
                    ins = pe.transpose(bank[6 + r][:, q * P:(q + 1) * P], sgu_w[:, 4 * r + q, :], ident[:, :])
                ins.then_inc(SEM["sgw_tr"], 1)
            pe.wait_ge(SEM["sgw_ready"], c.next("sgw_ready", 2))
            for b in range(TB):
                pe.wait_ge(SEM["v_ready"], c.next("v_ready"))
                for g in range(GROUPS):
                    ins = pe.matmul(bank[4 + 2 * b + g // 4][:, (g % 4) * P:(g % 4 + 1) * P], sgu_wT[:, g, :],
                                    v_t[:, b, g * P:(g + 1) * P], start=True, stop=True)
                ins.then_inc(SEM["sgu_mm"], 1)
            panel(0)
            panel(1)
            pe.wait_ge(SEM["ha_ready"], c.next("ha_ready", 2))
            pe.wait_ge(SEM["gen0"], c.so_far("gen0"))
            pe.wait_ge(SEM["gen1"], c.so_far("gen1"))
            def scores(hh):
                q = hh % 2
                pe.wait_ge(SEM["qh_ready"], c.next("qh_ready"))
                for m in range(2):
                    f = slice(m * HD, (m + 1) * HD)
                    o = bank[score_banks[q][m]]
                    pe.matmul(o[:, 0:P], qh[q][f, 0:P], kh[q][f, 0:P], start=True, stop=False)
                    pe.matmul(o[:, 0:P], identb, negm, start=False, stop=True)
                    pe.matmul(o[:, P:P + T], qh[q][f, P:T], kh[q][f, 0:T], start=True, stop=False)
                    ins = pe.matmul(o[:, T:P + T], identb, negm, start=False, stop=True)
                ins.then_inc(SEM[f"s_ready{q}"], 1)

            def turn():
                pe.wait_ge(SEM["a_ready"], c.next("a_ready"))
                for j in range(3):
                    ins = pe.transpose(bank[6][:, j * P:(j + 1) * P], a_t[:, j * P:(j + 1) * P], ident[:, :])
                ins.then_inc(SEM["a_tr"], 1)

            def outputs(i, hh):
                pe.wait_ge(SEM["aT_ready"], c.next("aT_ready"))
                pe.wait_ge(SEM["o_out"], c.so_far("o_out"))
                c.count("o_out")
                ve_ = [val[:, b, ds(i * 512 + hh * P, P)] for b in range(TB)]
                pe.matmul(bank[7][:, 0:P], aT[:, 0, :], ve_[0], start=True, stop=True)
                pe.matmul(bank[7][:, P:T], aT[:, 1, :], ve_[0], start=True, stop=False)
                pe.matmul(bank[7][:, P:T], aT[:, 2, :], ve_[1], start=False, stop=True).then_inc(SEM["o_ready"], 1)

            with c.loop(2, "pe att") as i:
                for hh in range(4):
                    scores(hh)
                    if hh:
                        turn()
                    panel_unit(hh // 2, hh % 2, 0)
                    if hh:
                        outputs(i, hh - 1)
                turn()
                outputs(i, 3)
            pe.wait_ge(SEM["o_out"], c.so_far("o_out"))
            enter(u_t, None, True)
            panel(1)
            enter(y, "hb_ready", True)
            panel(1)
            enter(gate[0], "m_ready", True)
            panel(1, True)
            enter(x, "x_ready", False)
            ffn()
        c.count("x_ready", TB)
        second_pe(c, pe, three, panel, panel_unit, up_unit, enter, ffn)
    ctx.close()


def constants():
    f = np.float32

    def bf16(t):
        return (t.astype(f).view(np.uint32) >> 16).astype(np.uint16).view(f)

    pos = np.arange(T, dtype=f)
    inv = (f(ROPE_THETA) ** (-np.arange(0, HD, 2, dtype=f) / f(HD))).astype(f)
    ang = pos[:, None] * inv[None, :]
    cos, sin = np.cos(ang).astype(f), np.sin(ang).astype(f)
    rope = np.stack([np.concatenate([cos, cos], 1), np.concatenate([-sin, sin], 1)])
    r = np.arange(P)
    lam = np.array([0.8 - 0.6 * math.exp(-0.3 * l) for l in range(DEPTH)])
    tok, head = r // RH, r % RH
    same = head[:, None] == head[None, :]
    s_lt, s_le, s_gt = ((op(tok[:, None], tok[None, :]) & same).astype(f) for op in (np.less, np.less_equal, np.greater))
    masks = [s_lt, s_le, s_gt, -s_le, -s_lt, -s_gt, s_le, s_lt,
             (head[:, None] == np.arange(RH)[None, :]).astype(f), (r[:, None] // CH == np.arange(RH)[None, :]).astype(f)]
    return {
        "c_pairs": (head[None, None, :] == 2 * np.arange(4)[None, :, None] + (r // HD)[:, None, None]).astype(f),
        "c_masks": np.concatenate(masks, 1),
        "c_sel": np.broadcast_to(np.eye(FOX, dtype=f)[:, :, None], (FOX, FOX, P)).copy(),
        "c_ones": np.ones((P, P), f),
        "c_ident": np.eye(P, dtype=f),
        "c_mhalf": np.concatenate([np.full((P, P), -0.5, f), np.full((P, 1), HD ** -0.5, f)], 1),
        "c_rope": np.ascontiguousarray(rope.reshape(2, TB, P, HD).transpose(2, 0, 1, 3)),
        "c_tri": (r[:, None] <= r[None, :]).astype(f),
        "c_laminit": np.ascontiguousarray(np.broadcast_to(np.stack([lam, 1 - lam], 1).astype(f), (P, DEPTH, 2))),
        "c_negm": bf16(np.concatenate([np.zeros((P, P)), np.where(r[None, :] <= r[:, None], 0, NEG)], 1)),
        "c_identb": bf16(np.eye(P)),
    }


def kernel(**inputs):
    import concourse.bacc as bacc
    from concourse.bass_utils import run_bass_kernel_spmd

    nc = bacc.Bacc("TRN2", target_bir_lowering=False, num_devices=1)
    arrays = {n: np.ascontiguousarray(v) for n, v in inputs.items() if n in USED}
    arrays.update(constants())
    f32 = mybir.dt.float32
    a = {n: nc.dram_tensor(f"in_{n}", v.shape, f32, kind="ExternalInput").ap() for n, v in arrays.items()}
    out = nc.dram_tensor("out", (1, T, D), f32, kind="ExternalOutput").ap()
    program(nc, a, out)
    got = run_bass_kernel_spmd(nc, [{f"in_{n}": v for n, v in arrays.items()}], core_ids=[0])
    return got.results[0]["out"]
```

```python
import math
from contextlib import ExitStack, contextmanager

import numpy as np
import concourse.bass as bass
import concourse.mybir as mybir

P = 128
T = 256
TB = T // P
D = 1024
KT = D // P
FF = 2816
STEP = 256
STEPS = FF // STEP
DEPTH = 2
HALF = 512
SLOTS = 4
UNIT = 2048
LN_EPS = 1e-5
RMS_EPS = 1e-6
ALPHA = (2.0 * DEPTH) ** 0.25
GROUPS = 8
DHEADS = 8
HD = 64
ROPE_THETA = 10000.0
NEG = -1e30
IN1 = 7168
COL_U, COL_Q, COL_V, COL_G = 0, 2048, 4096, 5120
RH = 8
CH = 16
NCH = T // CH
LORA = 256
RW = 512
CONV = 31
GN_EPS = 1e-5 * HD
FOX = 16
DECAY = -math.exp(-0.5)

STARTED = [f"{n}{s}" for n in ("lo", "used") for s in range(SLOTS)] + [
    "gen0", "gen1", "x_ready", "s_ready0", "s_ready1", "a_ready", "a_tr", "o_out", "y_out", "sq_free"]


class Counts:

    def __init__(self, engine, held):
        self.engine, self.held, self.loops = engine, held, []
        self.seen = {n: 1 for n in STARTED} | {"x_ready": 1 + TB}

    def so_far(self, name):
        v = self.seen.get(name, 0)
        for i, per_pass in self.loops:
            if per_pass.get(name, 0):
                v = i * per_pass[name] + v
        return v

    def count(self, name, k=1):
        self.seen[name] = self.seen.get(name, 0) + k

    def next(self, name, k=1):
        self.count(name, k)
        return self.so_far(name)

    def hold(self):
        self.engine.sem_inc(self.held, 1)

    @contextmanager
    def loop(self, n, which):
        per_pass = PER_PASS.get(which, {})
        before = dict(self.seen)
        self.hold()
        with self.engine.Fori(0, n) as i:
            self.loops.append((i, per_pass))
            yield i
            self.loops.pop()
        grew = {k: v - before.get(k, 0) for k, v in self.seen.items() if v != before.get(k, 0)}
        assert grew == per_pass, (which, grew)
        for k, v in grew.items():
            self.seen[k] = before.get(k, 0) + n * v


PER_PASS = {
    "sp ffn": {"lo0": 1, "lo1": 1, "lo2": 1},
    "sp four": {"lo0": 1, "lo1": 1, "lo2": 1, "lo3": 1},
    "sp layer": {"lo0": 32, "lo1": 32, "lo2": 30, "lo3": 12},
    "pool att": {"s_ready0": 2, "s_ready1": 2},
    "pool layer": {"x_ready": 6, "s_ready0": 4, "s_ready1": 4, "var": 8, "qk_ready": 8, "o_var": 1, "m_ready": 2},
    "act ffn": {"ld0": 32, "used0": 1, "ld1": 32, "used1": 1, "ht_tr": 1, "ld2": 16, "used2": 1},
    "act uv": {"ld0": 16, "used0": 1, "ld1": 16, "used1": 1, "ld2": 16, "used2": 1, "gen0": 1, "gen1": 1, "ld3": 16,
        "used3": 1},
    "act att": {"used0": 1, "used1": 1, "used2": 1, "used3": 1, "gen0": 2, "a_ready": 4, "a_tr": 4, "o_out": 4,
        "ld0": 16, "ld1": 16, "ld2": 16, "ld3": 16, "smax": 4, "o_ready": 4},
    "act layer": {"used0": 32, "used1": 32, "used2": 30, "used3": 12, "gen0": 14, "gen1": 10, "a_ready": 8, "a_tr":
        8, "o_out": 8, "ld0": 864, "ld1": 864, "tr": 24, "ht_tr": 22, "ld2": 480, "ld3": 192, "lam_s": 1, "rope_tr":
        8, "smax": 8, "o_ready": 8},
    "dve ffn": {"hi0": 1, "used0": 1, "hi1": 1, "used1": 1, "h_silu": 2, "ht_hi": 1, "hi2": 1, "used2": 1},
    "dve uv": {"hi0": 1, "used0": 1, "hi1": 1, "used1": 1, "hi2": 1, "used2": 1, "hi3": 1, "used3": 1, "gen0": 1,
        "gen1": 1},
    "dve qk": {"hi0": 1, "used0": 1, "hi1": 1, "used1": 1, "hi2": 1, "used2": 1, "hi3": 1, "used3": 1, "dve": 2,
        "gen0": 1, "gen1": 1, "rope": 4},
    "dve att": {"used0": 1, "used1": 1, "used2": 1, "used3": 1, "gen0": 2, "s_ready0": 2, "s_ready1": 2, "a_tr": 4,
        "hi0": 1, "hi1": 1, "hi2": 1, "hi3": 1, "dve": 12, "e_ready": 16},
    "dve layer": {"used0": 32, "used1": 32, "used2": 30, "used3": 12, "gen0": 14, "gen1": 10, "x_ready": 6,
        "s_ready0": 4, "s_ready1": 4, "a_tr": 8, "hi0": 32, "hi1": 32, "xt_hi": 24, "h_silu": 44, "ht_hi": 22,
        "hi2": 30, "hi3": 12, "half": 3, "dve": 65, "gains_ld": 128, "rstd": 8, "sgu_ld": 96, "rope": 8, "lam_e": 1,
        "sgw_tr": 2, "sgu_mm": 2, "e_ready": 32, "o_sq": 1, "o_rstd": 1, "gate_on": 2},
    "pe ffn": {"lo0": 1, "lo1": 1, "h_ready": 1, "ht_ready": 1, "lo2": 1},
    "pe att": {"lo0": 1, "lo1": 1, "lo2": 1, "lo3": 1, "gen0": 2, "a_ready": 4, "o_out": 4, "qh_ready": 4,
        "aT_ready": 4},
    "pe layer": {"lo0": 32, "lo1": 32, "lo2": 30, "lo3": 12, "gen0": 14, "gen1": 10, "x_ready": 6, "a_ready": 8,
        "o_out": 8, "xt_ready": 24, "h_ready": 22, "ht_ready": 22, "rope": 8, "qk_ready": 8, "sgu_ld": 96,
        "sgw_ready": 2, "v_ready": 2, "ha_ready": 2, "qh_ready": 8, "aT_ready": 8, "hb_ready": 2, "m_ready": 2},
    "pool scan": {"rowsT_ready0": 1, "rowsT_ready1": 1, "rows_tr0": 1, "rows_tr1": 1, "m_mm": 2},
    "pool qk": {"fss_ready": 4},
    "pool fox": {"s_ready0": 2, "s_ready1": 2},
    "act scan": {"rows_tr0": 1, "rows_tr1": 1, "pw_mm0": 3, "pw_mm1": 3, "y_mm": 2},
    "act fox": {"used0": 1, "used1": 1, "gen0": 1, "ld0": 16, "ld1": 16, "smax": 4, "eT_tr": 4},
    "dve scan": {"dve": 20, "m_new": 2, "gram_mm0": 1, "gram_ready0": 1, "inv_ready0": 4, "gram_mm1": 1,
        "gram_ready1": 1, "inv_ready1": 4, "inv_mm0": 3, "inv_mm1": 3, "w_mm": 2, "u_mm": 2, "kv_mm": 2, "m_mm": 2,
        "y_mm": 2},
    "dve fqk": {"used0": 1, "used1": 1, "used2": 1, "used3": 1, "gen0": 1, "gen1": 1, "sq_free": 4, "hi0": 1, "hi1":
        1, "hi2": 1, "hi3": 1, "dve": 2, "rope": 4, "fsq": 4, "frs_ready": 4},
    "dve fox": {"used0": 1, "used1": 1, "gen0": 1, "s_ready0": 2, "s_ready1": 2, "o_out": 4, "hi0": 1, "hi1": 1,
        "e_ready": 16, "o_ready": 4, "eT1_tr": 4, "rinv": 4},
    "pe scan": {"y_out": 2, "rkab_ready0": 1, "rkab_ready1": 1, "rowsT_ready0": 1, "rowsT_ready1": 1, "gram_ready0":
        1, "gram_ready1": 1, "pw_ready0": 3, "inv_ready0": 4, "pw_ready1": 3, "inv_ready1": 4, "ra_ready0": 1,
        "m_new": 2, "exp_ready0": 1, "w_ready": 2, "u_ready": 2, "ra_ready1": 1, "exp_ready1": 1},
    "pe fox": {"lo0": 1, "lo1": 1, "gen0": 1, "o_out": 4, "qh_ready": 4, "aT_ready": 4, "e_ready": 16, "eT1_ready":
        4},
}

USED = ("x", "w_in", "gate_b", "sgu_ln_g", "sgu_ln_b", "sgu_w", "sgu_b", "lam", "diff_ln_g", "w_branch", "w_out",
        "ffn_w1", "ffn_w3", "ffn_w2", "ln_g", "ln_b",
        "norm_gains_2", "ffn_w_gate_2", "ffn_w_up_2", "ffn_w_down_2", "a_w_in_2", "a_shift_mu_2",
        "a_decay_up_2", "a_decay_base_2", "a_iclr_up_2", "a_iclr_base_2", "a_gate_up_2", "a_k_k_2", "a_k_a_2",
        "a_r_k_2", "a_lnx_g_2", "a_lnx_b_2", "b_conv_w_2", "b_conv_b_2", "b_ln_g_2", "b_ln_b_2", "ab_w_out_2",
        "c_w_in_2", "c_forget_bias_2", "c_q_norm_g_2", "c_k_norm_g_2", "c_w_out_2")


def program(nc, a, out):
    f32, f32r, bf16 = mybir.dt.float32, mybir.dt.float32r, mybir.dt.bfloat16
    ACT = mybir.ActivationFunctionType
    ALU = mybir.AluOpType
    X = mybir.AxisListType.X
    ds = bass.ds
    ctx = ExitStack()
    ctx.enter_context(nc.allow_non_contiguous_dma("small parameters"))

    def sb(name, shape, dt=f32):
        return ctx.enter_context(nc.sbuf_tensor(name, shape, dt))

    wf = [sb(f"wf{s}", [P, UNIT]) for s in range(SLOTS)]
    wh = [sb(f"wh{s}", [P, UNIT], f32r) for s in range(SLOTS)]
    wl = [sb(f"wl{s}", [P, UNIT], f32r) for s in range(SLOTS)]
    xTh = sb("xTh", [P, KT, T], f32r)
    xTl = sb("xTl", [P, KT, T], f32r)
    x = sb("x", [P, TB, D])
    y = sb("y", [P, TB, D])
    hTh = sb("hTh", [P, 2, T], f32r)
    hTl = sb("hTl", [P, 2, T], f32r)
    hid = sb("hid", [P, TB, STEP])
    sil = sb("sil", [P, TB, STEP])
    gains = sb("gains", [P, 2, D])
    ident = sb("ident", [P, P])
    mhalf = sb("mhalf", [P, P + 1])
    scale = mhalf[:, P:P + 1]
    stats = sb("stats", [P, 2, 6])
    mv = sb("mv", [P, TB, 2])
    ve = sb("ve", [P, TB])
    rstd = sb("rstd", [P, TB])
    ssq = sb("ssq", [P, 4])
    arena = sb("arena", [P, 15360])
    bank = [ctx.enter_context(nc.psum_tensor(f"bank{i}", [P, HALF], f32)) for i in range(8)]

    def part(at, *shape):
        n = int(np.prod(shape))
        assert at + n <= 15360
        v = arena[:, at:at + n]
        if len(shape) == 2:
            return v.rearrange("p (a b) -> p a b", a=shape[0])
        if len(shape) == 3:
            return v.rearrange("p (a b c) -> p a b c", a=shape[0], b=shape[1])
        if len(shape) == 4:
            return v.rearrange("p (a b c d) -> p a b c d", a=shape[0], b=shape[1], c=shape[2])
        return v

    u_t = part(0, TB, D)
    v_t = part(2048, TB, D)
    uv = part(0, 2, TB, D)
    qkT = part(4096, 2, DHEADS, T)
    val = part(8192, TB, D)
    sgu_gb = part(10240, 2, D)
    sgu_w = part(12288, GROUPS, P)
    sgu_wT = part(13312, GROUPS, P)
    rope1 = hid[:, :, :].rearrange("p b n -> p (b n)")
    rope2 = sil[:, :, :].rearrange("p b n -> p (b n)")
    qh, kh = ([t[:, w, :] for t in (hid, sil)] for w in range(2))
    score_banks = ((4, 5), (1, 3))
    osq = part(4096, TB, D)
    gate = (v_t, part(10240, TB, D))
    e_t = part(12288, 2, 384)
    a_t = part(13056, 384)
    aT = part(13440, 3, P)
    att = part(13824, 64)
    oss = part(13888, 16)
    orstd = part(13904, 16)
    sgu_bT = part(14336, GROUPS)
    cs = part(14344, 2, TB, HD)
    tri = part(14600, P)
    lam_t = part(14728, 4, HD)
    lam_c = part(14984, 4)
    laminit = part(14988, DEPTH, 2)
    dgain = part(14992, P)
    negm_f, identb_f = part(15120, P), part(15248, 64)
    negm_wide, identb = negm_f.bitcast(bf16), identb_f.bitcast(bf16)
    negm = negm_wide[:, P:T]

    names = []

    def new(*ns):
        names.extend(ns)

    new("held", "const_ld", "x_ld", "half", "pre_var", "pre_rstd")
    for s in range(SLOTS):
        new(f"ld{s}", f"hi{s}", f"lo{s}", f"used{s}")
    new("h_silu", "h_ready", "ht_tr", "ht_hi", "ht_ready")
    new("tr", "xt_hi", "xt_ready", "x_ready", "gen0", "gen1")
    new("var", "rstd", "gains_ld", "dve", "act", "pool")
    new("sgu_ld", "v_ready", "sgw_tr", "sgw_ready", "sgu_mm", "ha_ready")
    new("rope", "rope_tr", "qk_ready")
    new("s_ready0", "s_ready1", "smax", "e_ready", "a_ready", "a_tr", "aT_ready", "o_ready", "o_out")
    new("o_var", "o_rstd", "o_sq", "hb_ready", "gate_on", "m_ready", "lam_e", "lam_s", "qh_ready", "out_st")
    new("sq", "x_new", "done", "ab_ld", "z_st", "lp_ld", "rkv_ld", "glu_ready", "cgb_ld", "kk_var", "kk_rstd")
    new("mixed", "sag_ready", "sig_st0", "sig_st1", "sig_ld0", "sig_ld1", "iclr_st", "iclr_ld", "g_st", "g_ld", "bonus_done", "k_new", "made", "e_done", "m_new", "yr_ready", "y_st", "y_ld", "c_ld", "fss_ready")
    new("frs_ready", "cw_tr", "cw_ready", "glu_tr", "gluT_ready", "lmix", "lora_ready", "lora_tr", "loraT_ready")
    new("ups_ready", "sa_ready", "tot_ready", "pc_ready", "cum_ready", "e_exp", "conv_n", "yb_ready", "y_mm")
    new("y_out", "sq_free", "fsq", "fabs", "fln", "eT_tr", "convT", "u_mm", "u_ready", "m_mm", "flog_ready")
    new("cum_mm", "cumT_ready", "rinv", "eT1_tr", "eT1_ready", "w_mm", "w_ready", "kv_mm")
    for q in range(2):
        new(*(f"{n}{q}" for n in ("rkab_ready", "exp_ready", "rows_tr", "rowsT_ready", "ra_ready", "gram_mm", "gram_ready",
                                  "pw_mm", "pw_ready", "inv_mm", "inv_ready")))
    SEM = {n: ctx.enter_context(nc.semaphore(n)) for n in names}
    block = ctx.enter_context(nc.Block())

    def bcast_row(ap, n):
        return bass.AP(tensor=ap.tensor, offset=ap.offset, ap=[[0, P], [1, n]])


    rows_t = part(0, 9, NCH, HD)
    ROW_V, ROW_R, ROW_K, ROW_SIG, ROW_A, ROW_G, ROW_6, ROW_7, ROW_8 = range(9)
    st_rkv = part(6144, 3, TB, RW)
    st_sag = part(6144, 3, TB, RW)
    glu = part(9216, TB, RW)
    y_conv = part(9216, TB, RW)
    cgate = part(10240, TB, RW)
    conv_gb = part(10240, 2, RW)
    convw_rows = part(11264, RW)
    gluT = part(11264, 4, CONV - 1 + T)
    conv_o = part(12408, 4, T)
    sag_base = part(12408, 2, RW)
    lora = part(13432, TB, LORA)
    lora_prev = part(13944, TB, LORA)
    loraT = part(14456, 2, T)
    convw = part(14968, 4, 32)
    lora_up = hid[:, :, :].rearrange("p b n -> p (b n)")
    gate_up = sil[:, :, :].rearrange("p b n -> p (b n)")
    gflat = gains[:, :, :].rearrange("p a n -> p (a n)")
    cum_mask = gflat[:, 0:384].rearrange("p (a b) -> p a b", a=3)
    gram_mask = gflat[:, 384:1024].rearrange("p (a b) -> p a b", a=5)
    head_mask = gflat[:, 1024:1032]
    chunk_mask = gflat[:, 1032:1040]
    mu_rows = gflat[:, 1040:1232].rearrange("p (a b) -> p a b", a=3)
    row_par = gflat[:, 1232:1552].rearrange("p (a b) -> p a b", a=5)
    mu_lora = gflat[:, 1552:1808]
    small = gflat[:, 1808:1888].rearrange("p (a b) -> p a b", a=5)
    bonus = small[:, 0, :]
    pc = gflat[:, 1888:1952].rearrange("p (j c) -> p j c", j=4)
    yflat = y[:, :, :].rearrange("p b n -> p (b n)")
    kt_exp, bt_exp = ([yflat[:, (2 * q + i) * 512:(2 * q + i + 1) * 512] for q in range(2)] for i in range(2))
    xflat, lflat = wf[3], wf[2]
    ra_exp = [xflat[:, q * D:(q + 1) * D].rearrange("p (w j t) -> p w j t", w=2, j=4) for q in range(2)]
    gram = [lflat[:, q * 640:(q + 1) * 640].rearrange("p (a t) -> p a t", a=5) for q in range(2)]
    pw = [(lflat[:, 1280:1920] if q == 0 else part(13432, 640)).rearrange("p (a t) -> p a t", a=5) for q in range(2)]
    inv = [lflat[:, 1920:2048], part(14072, P)]
    rowsT = [part(14200 + q * 384, 3, P) for q in range(2)]
    rkab = [part(9216 + q * 384, 3, P) for q in range(2)]
    decays = [yflat[:, w * D:(w + 1) * D].rearrange("p (c n) -> p c n", c=NCH) for w in range(2)]
    state = part(9984, 4, HD)
    hflat = hid[:, :, :].rearrange("p b n -> p (b n)")
    sdec = hflat[:, 0:256].rearrange("p (j n) -> p j n", j=4)
    w_s, u_s = hflat[:, 256:320], hflat[:, 320:384]
    pair_mask = gate_up.rearrange("p (j t) -> p j t", j=4)
    y_rwkv = part(6144, TB, RW)
    fqkT = part(0, 2, 8, T)
    fval = part(4096, TB, D)
    fgate = part(6144, TB, D)
    sel = part(8192, FOX, P)
    fe_t = part(12288, 2, 384)
    feT = part(13056, 2, 3, P)
    fatt = [part(13824 + 16 * q, 16) for q in range(2)]
    cumh, cuml = hTh[0:FOX, 0, :], hTl[0:FOX, 0, :]
    fbias = part(14368, FOX)
    flog = part(14384, TB, FOX)
    fabs = part(14416, TB, FOX)
    qk_gain = part(14448, 2, HD)
    tri_c = part(14576, P)
    ones_c = part(14704, P)
    fss = part(14832, 8)
    frs = part(14840, 8)
    selh = [t[0:FOX, 1, :] for t in (hTh, hTl)]
    z_rows = nc.dram_tensor("z_rows", (3, (T + 1) * RH, HD), f32, kind="Internal").ap()
    lora_rows = nc.dram_tensor("lora_rows", (T + 1, LORA), f32, kind="Internal").ap()
    sag_rows = nc.dram_tensor("sag_rows", (3, T * RH, HD), f32, kind="Internal").ap()
    y_rows = nc.dram_tensor("y_rows", (T * RH, HD), f32, kind="Internal").ap()

    first_gain = part(0, D)
    y_add, y_gain = ([wf[0][:, w * D:(w + 1) * D].rearrange("p (c n) -> p c n", c=NCH) for w in range(2)])

    def par(j):
        return row_par[:, j:j + 1, :].broadcast_to([P, NCH, HD])

    def per_chunk(t):
        return t.rearrange("p (c a) -> p c a", a=1).broadcast_to([P, NCH, HD])

    def by_chunk(r):
        return r.rearrange("(c p) n -> p c n", p=P)

    def by_token(r):
        return r.rearrange("(b p h) n -> p b (h n)", b=TB, h=RH)

    def second_sp(c, sp, ffn, half_panel, load, rows):
        w1, w3, w2 = a["ffn_w_gate_2"], a["ffn_w_up_2"], a["ffn_w_down_2"]
        ffn(w1[0, 0], w3[0, 0], w2[0, 0])
        wa = a["a_w_in_2"][0]
        for s, col in ((0, 0), (1, 0), (2, 512), (3, 512), (0, 1024), (1, 1024), (2, 1536), (3, 1536), (0, 2048), (1, 2048)):
            half_panel(wa, col, s, s % 2)
        load(2, (wf[2][:, :].rearrange("p (k n) -> p k n", k=KT), rows(wa)[:, :, 2560:2816]))
        for s in range(4):
            half_panel(a["ab_w_out_2"][0], HALF * (s // 2), s, s % 2)
        for b in range(TB):
            sp.wait_ge(SEM["sag_ready"], c.next("sag_ready"))
            sp.dma_start(by_token(sag_rows[0])[:, b, :], st_sag[:, 0, b, :]).then_inc(SEM[f"sig_st{b}"], 16)
        for j, n in ((1, "iclr"), (2, "g")):
            sp.dma_start(by_token(sag_rows[j]), st_sag[:, j, :, :]).then_inc(SEM[f"{n}_st"], 16)
        sp.wait_ge(SEM["mixed"], c.next("mixed"))
        for b in range(TB):
            sp.wait_ge(SEM[f"sig_st{b}"], c.next(f"sig_st{b}", 16))
            half = slice(b * NCH // TB, (b + 1) * NCH // TB)
            sp.dma_start(rows_t[:, ROW_SIG, half, :], by_chunk(sag_rows[0])[:, half, :]).then_inc(SEM[f"sig_ld{b}"], 16)
        for row, j, n in ((ROW_A, 1, "iclr"), (ROW_G, 2, "g")):
            sp.wait_ge(SEM[f"{n}_st"], c.next(f"{n}_st", 16))
            sp.dma_start(rows_t[:, row, :, :], by_chunk(sag_rows[j])).then_inc(SEM[f"{n}_ld"], 16)
        sp.wait_ge(SEM["yr_ready"], c.next("yr_ready"))
        sp.dma_start(by_chunk(y_rows), rows_t[:, ROW_8, :, :]).then_inc(SEM["y_st"], 16)
        sp.wait_ge(SEM["y_st"], c.next("y_st", 16))
        sp.dma_start(y_rwkv, by_token(y_rows)).then_inc(SEM["y_ld"], 16)
        ffn(w1[0, 1], w3[0, 1], w2[0, 1])
        ffn(w1[1, 0], w3[1, 0], w2[1, 0])
        wc = a["c_w_in_2"][0]
        for s in range(4):
            half_panel(wc, HALF * (s // 2), s, s % 2)
        for s in range(4):
            half_panel(wc, D + HALF * (s // 2), s, s % 2)
        load(0, (wf[0][:, 0:KT * FOX].rearrange("p (k n) -> p k n", k=KT), rows(wc)[:, :, 4 * D:4 * D + FOX]))
        for s in (1, 2, 3, 0):
            half_panel(wc, 2 * D + HALF * (s // 2), s, s % 2)
        for i in range(2):
            for h in range(2):
                half_panel(wc, 3 * D + i * HALF, h, h)
        for s in range(4):
            half_panel(a["c_w_out_2"][0], HALF * (s // 2), s, s % 2)
        ffn(w1[1, 1], w3[1, 1], w2[1, 1])
        sp.wait_ge(SEM["done"], c.next("done", TB))
        sp.dma_start(out[0].rearrange("(b p) n -> p b n", p=P), x[:, :, :]).then_inc(SEM["out_st"], 16)
        sp.wait_ge(SEM["out_st"], c.next("out_st", 16))

    def second_pool(c, pool, gains_load, power, norm, pre_norm):
        g2 = a["norm_gains_2"]
        copy = pool.tensor_copy

        def two_norms(l, post, pre_l, pre):
            gains_load(g2[l, post:post + 1, :], g2[pre_l, pre:pre + 1, :])
            norm()
            pre_norm()
            pool.wait_ge(SEM["x_ready"], c.next("x_ready", TB))

        for p in range(2):
            c.count(f"gen{p}", (14, 10)[p] * DEPTH + 1)
        pre_norm()
        pool.wait_ge(SEM["x_ready"], c.next("x_ready", TB))
        two_norms(0, 1, 0, 2)
        def per_row(name, at):
            t = a[name]
            return bass.AP(tensor=t.tensor, offset=t.offset + at, ap=[[0, CH], [HD, RH], [1, HD]])
        loads = [(gflat[:, 0:1040], a["c_masks"]), (mu_lora, bcast_row(a["a_shift_mu_2"][0:1, 1536:1792], LORA)),
                 (lora_up[0:64, :], a["a_decay_up_2"][0]), (lora_up[64:128, :], a["a_iclr_up_2"][0]),
                 (gate_up, a["a_gate_up_2"][0]),
                 (sag_base[:, 0, :], bcast_row(a["a_decay_base_2"], RW)), (sag_base[:, 1, :], bcast_row(a["a_iclr_base_2"], RW)),
                 (convw_rows[0:31, :], a["b_conv_w_2"][0]), (convw_rows[31:32, :], a["b_conv_b_2"])]
        for j, col in enumerate((1024, 0, 512)):
            loads.append((mu_rows[:, j, :], per_row("a_shift_mu_2", col)))
        for j, n in enumerate(("a_k_k_2", "a_k_a_2", "a_r_k_2", "a_lnx_g_2", "a_lnx_b_2")):
            loads.append((row_par[:, j, :], per_row(n, 0)))
        for dst, src in loads:
            pool.dma_start(dst, src).then_inc(SEM["ab_ld"], 16)
        pool.memset(lora_prev[0:1, :, :], 0.0).then_inc(SEM["pool"], 1)
        pool.wait_ge(SEM["pool"], c.next("pool"))
        zero = lora_prev[0:1, :, :].rearrange("p b n -> p (b n)")
        for j in range(3):
            pool.dma_start(z_rows[j, 0:RH, :].rearrange("(o h) n -> o (h n)", o=1), zero).then_inc(SEM["z_st"], 16)
        pool.dma_start(lora_rows[0:1, :], zero[:, 0:LORA]).then_inc(SEM["z_st"], 16)
        for j, p in ((1, 0), (2, 1), (0, 0)):
            pool.wait_ge(SEM[f"gen{p}"], c.next(f"gen{p}"))
            pool.dma_start(by_token(z_rows[j, RH:, :]), st_rkv[:, j, :, :]).then_inc(SEM["z_st"], 16)
        pool.wait_ge(SEM["gen1"], c.next("gen1"))
        pool.dma_start(lora_rows[1:, :].rearrange("(b p) n -> p b n", p=P), lora).then_inc(SEM["z_st"], 16)
        pool.wait_ge(SEM["z_st"], c.next("z_st", 16 * 8))
        pool.dma_start(lora_prev, lora_rows[0:T, :].rearrange("(b p) n -> p b n", p=P)).then_inc(SEM["lp_ld"], 16)
        for j in range(3):
            pool.dma_start(rows_t[:, j, :, :], by_chunk(z_rows[j, RH:, :])).then_inc(SEM["rkv_ld"], 16)
            pool.dma_start(rows_t[:, 3 + j, :, :], by_chunk(z_rows[j, 0:T * RH, :])).then_inc(SEM["rkv_ld"], 16)
        pool.wait_ge(SEM["glu_ready"], c.next("glu_ready"))
        for i, n in enumerate(("b_ln_g_2", "b_ln_b_2")):
            pool.dma_start(conv_gb[:, i, :], bcast_row(a[n], RW)).then_inc(SEM["cgb_ld"], 16)
        pool.wait_ge(SEM["sag_ready"], c.next("sag_ready", 2))
        pool.dma_start(pair_mask, a["c_pairs"]).then_inc(SEM["cgb_ld"], 16)
        power(small[:, 1, :], small[:, 2, :], 16, "kk_var", "kk_rstd")
        def product(dst, s0, s1, to, op=ALU.mult):
            pool.tensor_tensor(dst, s0, s1, op).then_inc(SEM[to], 1)
            pool.wait_ge(SEM[to], c.next(to))
        pool.wait_ge(SEM["k_new"], c.next("k_new"))
        product(y_add, rows_t[:, ROW_R, :, :], rows_t[:, ROW_K, :, :], "made")
        product(y_gain, y_add, par(2), "made")
        pool.wait_ge(SEM["e_done"], c.next("e_done"))
        def rows_of(n, q):
            twice = rows_t[:, ROW_R:ROW_A:2, ds(n, 1), :].broadcast_to([P, 2, 2, HD])
            copy(rkab[q][:, 0:2, :].rearrange("p w (m n) -> p w m n", m=2), twice)
            copy(rkab[q][:, 2, :].rearrange("p (w n) -> p w n", w=2),
                 rows_t[:, ROW_K:ROW_G:2, ds(n, 1), :].rearrange("p w a n -> p w (a n)")).then_inc(SEM[f"rkab_ready{q}"], 1)

        def expand(n, q):
            for dst, j in ((kt_exp[q], ROW_6), (bt_exp[q], ROW_7)):
                ins = pool.tensor_tensor(dst.rearrange("p (h n) -> p h n", h=RH),
                                         rows_t[:, j, ds(n, 1), :].broadcast_to([P, RH, HD]),
                                         head_mask.rearrange("p (h a) -> p h a", a=1).broadcast_to([P, RH, HD]), ALU.mult)
            ins.then_inc(SEM[f"exp_ready{q}"], 1)

        def spread(q):
            pool.wait_ge(SEM[f"rowsT_ready{q}"], c.next(f"rowsT_ready{q}"))
            pool.tensor_tensor(ra_exp[q], rowsT[q][:, 0:2, :].rearrange("p w (a t) -> p w a t", a=1).broadcast_to([P, 2, 4, P]),
                               pair_mask.rearrange("p (a j) t -> p a j t", a=1).broadcast_to([P, 2, 4, P]), ALU.mult)\
                .then_inc(SEM[f"ra_ready{q}"], 1)

        for q in range(2):
            rows_of(q, q)
        pool.wait_ge(SEM["cgb_ld"], c.next("cgb_ld", 48))
        for q in range(2):
            spread(q)
            expand(q, q)
        with c.loop(NCH // 2 - 1, "pool scan") as i:
            for q in range(2):
                pool.wait_ge(SEM[f"rows_tr{q}"], c.next(f"rows_tr{q}"))
                rows_of(i * 2 + 2 + q, q)
            for q in range(2):
                pool.wait_ge(SEM["m_mm"], c.next("m_mm"))
                expand(i * 2 + 2 + q, q)
                spread(q)
        pool.wait_ge(SEM["bonus_done"], c.next("bonus_done"))
        pool.wait_ge(SEM["g_ld"], c.next("g_ld", 16))
        gate_rows = rows_t[:, ROW_G, :, :]
        product(y_gain, gate_rows, par(3), "made")
        product(y_add, rows_t[:, ROW_V, :, :], per_chunk(bonus), "made")
        product(y_add, y_add, par(4), "made", ALU.add)
        product(y_add, y_add, gate_rows, "made")
        power(small[:, 1, :], small[:, 2, :], 16, "kk_var", "kk_rstd")
        norm()
        two_norms(0, 3, 0, 4)
        two_norms(0, 5, 1, 0)
        two_norms(1, 1, 1, 2)
        for dst, src in ((sel[0:FOX, :, :], a["c_sel"]), (fbias, bcast_row(a["c_forget_bias_2"], FOX)),
                         (qk_gain[:, 0, :], bcast_row(a["c_q_norm_g_2"], HD)),
                         (qk_gain[:, 1, :], bcast_row(a["c_k_norm_g_2"], HD)),
                         (tri_c, a["c_tri"]), (ones_c, a["c_ones"])):
            pool.dma_start(dst, src).then_inc(SEM["c_ld"], 16)
        with c.loop(2, "pool qk") as i:
            for r in range(4):
                power(frs, fss, 8, "fss_ready", "frs_ready")
        pool.wait_ge(SEM["qk_ready"], c.next("qk_ready", 8))
        pool.wait_ge(SEM["c_ld"], c.next("c_ld", 16 * 6))
        with c.loop(2, "pool fox") as i:
            for hp in range(4):
                q = hp % 2
                pool.wait_ge(SEM[f"s_ready{q}"], c.so_far(f"s_ready{q}"))
                c.count(f"s_ready{q}")
                head = [fqkT[:, w, ds(i * 4 + hp, 1), :].rearrange("p a t -> p (a t)") for w in range(2)]
                pool.tensor_tensor(qh[q], head[0], scale.broadcast_to([P, T]), ALU.mult)
                copy(kh[q], head[1])
                copy(selh[q].rearrange("p (m t) -> p m t", m=2), sel[0:FOX, ds(i * 8 + hp * 2, 2), :])\
                    .then_inc(SEM["qh_ready"], 1)
        two_norms(1, 3, 1, 4)
        gains_load(g2[1, 5:6, :], g2[1, 5:6, :])
        norm()

    def second_act(c, act, prep, next_units, panel_evac, transposed, ffn):
        def square_sums():
            for b in range(TB):
                if b == 0:
                    act.wait_ge(SEM["half"], c.next("half"))
                else:
                    act.wait_ge(SEM["used3"], c.so_far("used3"))
                for h in range(2):
                    act.activation(y[:, b, h * HALF:(h + 1) * HALF], bank[2 * b + h][:, :], ACT.Square,
                                   accum_out=ssq[:, 2 * b + h:2 * b + h + 1]).then_inc(SEM["sq"], 1)

        def pre():
            for b in range(TB):
                act.wait_ge(SEM["x_new"], c.next("x_new"))
                act.activation(y[:, b, :], x[:, b, :], ACT.Square, accum_out=ssq[:, 2 * b:2 * b + 1]).then_inc(SEM["sq"], 1)
                transposed(b)

        def two_norms():
            square_sums()
            pre()

        c.count("half", 3 * DEPTH)
        c.count("x_ready", 6 * DEPTH - TB)
        act.dma_start(first_gain, bcast_row(a["norm_gains_2"][0, 0:1, :], D)).then_inc(SEM["const_ld"], 16)
        for b in range(TB):
            act.wait_ge(SEM["x_ready"], c.next("x_ready"))
            act.activation(y[:, b, :], x[:, b, :], ACT.Square, accum_out=ssq[:, 2 * b:2 * b + 1]).then_inc(SEM["sq"], 1)
        transposed()
        ffn([(0, 1), (1, 1), (2, 1)])
        two_norms()
        prep(3)
        def evac(p, fn, then):
            panel_evac(p, fn)
            for s in then:
                prep(s)
        def to_stage(j):
            def fn(b, t):
                return act.activation(st_rkv[:, j, b, :], t, ACT.Copy)
            return fn
        evac(0, to_stage(1), (0, 1))
        evac(1, to_stage(2), (2, 3))
        evac(0, to_stage(0), (0, 1))
        act.wait_ge(SEM["used3"], c.so_far("used3"))
        for b in range(TB):
            act.activation(glu[:, b, 0:256], bank[2 * b + 1][:, 256:512], ACT.Copy)
            ins = act.activation(lora[:, b, :], bank[2 * b + 1][:, 0:256], ACT.Copy)
        ins.then_inc(SEM["gen1"], 1)
        c.count("gen1")
        prep(2)
        act.wait_ge(SEM["used1"], c.so_far("used1"))
        for b in range(TB):
            act.activation(glu[:, b, 256:512], bank[2 * b][:, 0:256], ACT.Copy)
            ins = act.activation(cgate[:, b, 0:256], bank[2 * b][:, 256:512], ACT.Sigmoid)
        ins.then_inc(SEM["gen0"], 1)
        c.count("gen0")
        prep(0)
        prep(1)
        act.wait_ge(SEM["used2"], c.so_far("used2"))
        for b in range(TB):
            ins = act.activation(cgate[:, b, 256:512], bank[2 * b + 1][:, 0:256], ACT.Sigmoid)
        ins.then_inc(SEM["gen1"], 1)
        c.count("gen1")
        act.wait_ge(SEM["cw_tr"], c.next("cw_tr"))
        act.activation(convw, bank[4][:, 0:P].rearrange("p (c j) -> p c j", c=4), ACT.Copy).then_inc(SEM["cw_ready"], 1)
        for b in range(TB):
            act.wait_ge(SEM["glu_tr"], c.next("glu_tr"))
            act.activation(gluT[:, :, CONV - 1 + b * P:CONV - 1 + (b + 1) * P],
                           bank[6 + b][:, :].rearrange("p (c t) -> p c t", c=4), ACT.Copy).then_inc(SEM["gluT_ready"], 1)
        act.wait_ge(SEM["lmix"], c.next("lmix"))
        act.activation(lora[:, :, 0:64], lora[:, :, 0:64], ACT.Tanh).then_inc(SEM["lora_ready"], 1)
        act.activation(lora[:, :, 128:256], lora[:, :, 128:256], ACT.Sigmoid).then_inc(SEM["lora_ready"], 1)
        act.wait_ge(SEM["lora_tr"], c.next("lora_tr"))
        act.activation(loraT, bank[4][:, :].rearrange("p (w t) -> p w t", w=2), ACT.Copy).then_inc(SEM["loraT_ready"], 1)
        prep(2)
        prep(3)
        for b in range(TB):
            act.wait_ge(SEM["ups_ready"], c.next("ups_ready"))
            act.activation(st_sag[:, 2, b, :], bank[3 * b + 2][:, :], ACT.Copy)
            act.wait_ge(SEM["sa_ready"], c.next("sa_ready"))
            act.activation(st_sag[:, 0:2, b, :], st_sag[:, 0:2, b, :], ACT.Sigmoid).then_inc(SEM["sag_ready"], 1)
        act.wait_ge(SEM["tot_ready"], c.next("tot_ready"))
        act.activation(pc, bank[7][:, 0:64].rearrange("p (j c) -> p j c", j=4), ACT.Exp, scale=DECAY).then_inc(SEM["pc_ready"], 1)
        act.wait_ge(SEM["g_st"], c.next("g_st", 16))
        act.wait_ge(SEM["iclr_st"], c.next("iclr_st", 16))
        decays_to = (rows_t[:, ROW_6, :, :], decays[0], decays[1], rows_t[:, ROW_7, :, :])
        for n, (dst, bk, sgn) in enumerate(zip(decays_to, (0, 4, 2, 2), (1, 1, -1, 1))):
            if n < 3:
                act.wait_ge(SEM["cum_ready"], c.next("cum_ready"))
            else:
                act.wait_ge(SEM["k_new"], c.next("k_new"))
            for h in range(2):
                ins = act.activation(dst[:, 8 * h:8 * h + 8, :].rearrange("p c n -> p (c n)"), bank[bk + h][:, :],
                                     ACT.Exp, scale=sgn * DECAY)
            ins.then_inc(SEM["e_exp"], 1)

        def copy(dst, src, to):
            act.activation(dst, src, ACT.Copy).then_inc(SEM[to], 1)

        def take_rows(q):
            act.wait_ge(SEM[f"rows_tr{q}"], c.next(f"rows_tr{q}"))
            copy(rowsT[q], bank[2 * q][:, 0:384].rearrange("p (w t) -> p w t", w=3), f"rowsT_ready{q}")

        def take_powers(q, step):
            act.wait_ge(SEM[f"pw_mm{q}"], c.next(f"pw_mm{q}"))
            dst = pw[q][:, 4, :] if step == 2 else pw[q][:, 2 * step:2 * step + 2, :]
            src = bank[2 * q + step % 2][:, 0:P if step == 2 else 2 * P]
            copy(dst, src if step == 2 else src.rearrange("p (a t) -> p a t", a=2), f"pw_ready{q}")

        def take_y(n):
            act.wait_ge(SEM["y_mm"], c.next("y_mm"))
            copy(rows_t[:, ROW_8, ds(n, 1), :].rearrange("p a n -> p (a n)"), bank[6][:, 0:HD], "y_out")

        for q in range(2):
            take_rows(q)
        for q, step in ((0, 0), (1, 0), (0, 1), (1, 1), (0, 2)):
            take_powers(q, step)
        with c.loop(NCH // 2 - 1, "act scan") as i:
            take_powers(1, 2)
            take_rows(0)
            take_y(i * 2)
            take_rows(1)
            take_powers(0, 0)
            take_powers(0, 1)
            take_y(i * 2 + 1)
            take_powers(0, 2)
            take_powers(1, 0)
            take_powers(1, 1)
        take_powers(1, 2)
        for n in (NCH - 2, NCH - 1):
            take_y(n)
        for b in range(TB):
            act.wait_ge(SEM["conv_n"], c.next("conv_n"))
            act.activation(y_conv[:, b, :], y_conv[:, b, :], ACT.Silu).then_inc(SEM["yb_ready"], 1)
        transposed()
        next_units(0, 2)
        for p in range(2):
            c.count(f"gen{p}")
        two_norms()
        ffn([(0, 2), (1, 2)])
        two_norms()
        ffn([(0, 1), (1, 1), (2, 1)])
        two_norms()
        prep(3)
        def take_panel(n):
            for b in range(TB):
                act.wait_ge(SEM["rope_tr"], c.next("rope_tr"))
                act.activation(fqkT[:, n // 2, 4 * (n % 2):4 * (n % 2) + 4, b * P:(b + 1) * P],
                               bank[6 + b][:, :].rearrange("p (h t) -> p h t", h=4), ACT.Copy).then_inc(SEM["qk_ready"], 1)

        for n in range(4):
            p = n % 2
            act.wait_ge(SEM[f"used{2 * p + 1}"], c.so_far(f"used{2 * p + 1}"))
            for b in range(TB):
                act.wait_ge(SEM["sq_free"], c.so_far("sq_free"))
                c.count("sq_free")
                act.activation(rope2, bank[2 * b + p][:, :], ACT.Square).then_inc(SEM["fsq"], 1)
            c.count(f"gen{p}")
            next_units(p)
            if n:
                take_panel(n - 1)
        c.count("gen0")
        prep(0)
        act.wait_ge(SEM["fabs"], c.next("fabs"))
        act.activation(fabs, fabs, ACT.Exp, scale=-1.0).then_inc(SEM["act"], 1)
        act.wait_ge(SEM["act"], c.next("act"))
        act.activation(fabs, fabs, ACT.Ln, bias=1.0).then_inc(SEM["fln"], 1)
        panel_evac(1, lambda b, t: act.activation(fval[:, b, HALF:D], t, ACT.Copy))
        take_panel(3)
        panel_evac(0, lambda b, t: act.activation(fval[:, b, 0:HALF], t, ACT.Copy))
        prep(0)
        prep(1)

        def exps(hp):
            q = hp % 2
            act.wait_ge(SEM["smax"], c.next("smax"))
            for j in range(4):
                at = slice(0, P) if j < 2 else slice(P, P + T)
                act.activation(fe_t[:, j % 2, at], bank[score_banks[q][j % 2]][:, at], ACT.Exp, bias=fatt[q][:, j:j + 1],
                               accum_out=fatt[q][:, 4 + j:5 + j]).then_inc(SEM["e_ready"], 1)

        def take_turned():
            act.wait_ge(SEM["eT_tr"], c.next("eT_tr"))
            act.activation(feT[:, 0, :, :], bank[6][:, 0:384].rearrange("p (k t) -> p k t", k=3), ACT.Copy)\
               .then_inc(SEM["aT_ready"], 1)

        with c.loop(2, "act fox") as i:
            for hp in range(4):
                exps(hp)
                if hp == 2:
                    act.wait_ge(SEM["used1"], c.so_far("used1"))
                    for b in range(TB):
                        ins = act.activation(fgate[:, b, ds(i * HALF, HALF)], bank[2 * b][:, :], ACT.Copy)
                    ins.then_inc(SEM["gen0"], 1)
                    c.count("gen0")
                    prep(0)
                if hp == 3:
                    prep(1)
                take_turned()
        act.wait_ge(SEM["gen0"], c.so_far("gen0"))
        for b in range(TB):
            act.activation(fgate[:, b, :], fgate[:, b, :], ACT.Sigmoid).then_inc(SEM["gate_on"], 1)
        transposed()
        prep(2)
        prep(3)
        next_units(0, 2)
        for p in range(2):
            c.count(f"gen{p}")
        two_norms()
        ffn([])
        square_sums()

    def second_dve(c, dve, low, next_units, transposed, ffn, moments):
        def var_of(b, factor):
            dve.wait_ge(SEM["sq"], c.next("sq", 2))
            dve.tensor_tensor(ssq[:, 2 * b:2 * b + 1], ssq[:, 2 * b:2 * b + 1], ssq[:, 2 * b + 1:2 * b + 2], ALU.add)\
               .then_inc(SEM["dve"], 1)
            dve.wait_ge(SEM["dve"], c.next("dve"))
            dve.tensor_scalar(ve[:, b:b + 1], ssq[:, 2 * b:2 * b + 1], 1.0 / (D * factor ** 2), RMS_EPS / factor ** 2,
                              ALU.mult, ALU.add).then_inc(SEM["var"], 1)

        def post(b, to):
            dve.wait_ge(SEM["rstd"], c.next("rstd"))
            for h in range(2):
                at = slice(h * HALF, (h + 1) * HALF)
                ins = dve.scalar_tensor_tensor(y[:, b, at], bank[2 * b + h][:, :], rstd[:, b:b + 1], gains[:, 0, at],
                                               ALU.mult, ALU.mult)
                if b == TB - 1:
                    ins.then_inc(SEM[f"gen{h}"], 1)
                    dve.wait_ge(SEM[f"gen{h}"], c.next(f"gen{h}"))
                else:
                    ins.then_inc(SEM["dve"], 1)
                    dve.wait_ge(SEM["dve"], c.next("dve"))
            dve.tensor_tensor(x[:, b, :], x[:, b, :], y[:, b, :], ALU.add).then_inc(SEM[to], 1)

        def pre_var(b):
            dve.wait_ge(SEM["sq"], c.next("sq"))
            dve.tensor_scalar(ve[:, b:b + 1], ssq[:, 2 * b:2 * b + 1], 1.0 / D, RMS_EPS, ALU.mult, ALU.add)\
               .then_inc(SEM["pre_var"], 1)

        def pre(b, gain=gains[:, 1, :]):
            dve.wait_ge(SEM["pre_rstd"], c.next("pre_rstd"))
            dve.scalar_tensor_tensor(y[:, b, :], x[:, b, :], rstd[:, b:b + 1], gain, ALU.mult, ALU.mult)\
               .then_inc(SEM["x_ready"], 1)
            c.count("x_ready")

        def two_norms(factor):
            var_of(0, factor)
            dve.wait_ge(SEM["gains_ld"], c.next("gains_ld", 32))
            post(0, "x_new")
            var_of(1, factor)
            pre_var(0)
            pre(0)
            post(1, "x_new")
            transposed(0)
            pre_var(1)
            pre(1)
            transposed(1)

        c.count("o_out", 8 * DEPTH)
        c.count("o_ready", 8 * DEPTH)
        pre_var(0)
        dve.wait_ge(SEM["const_ld"], c.next("const_ld", 16))
        pre(0, first_gain)
        pre_var(1)
        pre(1, first_gain)
        transposed()
        ffn(1.0)
        for s in range(3):
            low(s)
        two_norms(0.5)
        low(3)
        for p, then in ((0, (0, 1)), (1, (2, 3)), (0, (0, 1)), (1, (2,)), (0, (0, 1)), (1, ())):
            c.count(f"gen{p}")
            for s in then:
                low(s)
        dve.wait_ge(SEM["gen0"], c.so_far("gen0"))
        dve.wait_ge(SEM["gen1"], c.so_far("gen1"))
        dve.tensor_tensor(glu, glu, cgate, ALU.mult).then_inc(SEM["glu_ready"], 1)
        dve.wait_ge(SEM["ab_ld"], c.next("ab_ld", 16 * 17))
        dve.wait_ge(SEM["lp_ld"], c.next("lp_ld", 16))
        dve.tensor_tensor(lora_prev, lora_prev, lora, ALU.subtract).then_inc(SEM["dve"], 1)
        dve.wait_ge(SEM["dve"], c.next("dve"))
        dve.tensor_tensor(lora_prev, lora_prev, mu_lora.rearrange("p (a n) -> p a n", a=1).broadcast_to([P, TB, LORA]), ALU.mult)\
           .then_inc(SEM["dve"], 1)
        dve.wait_ge(SEM["dve"], c.next("dve"))
        dve.tensor_tensor(lora, lora, lora_prev, ALU.add).then_inc(SEM["lmix"], 1)
        low(2)
        low(3)
        dve.wait_ge(SEM["rkv_ld"], c.next("rkv_ld", 16 * 6))
        for b in range(TB):
            dve.wait_ge(SEM["ups_ready"], c.next("ups_ready"))
            for j in range(2):
                ins = dve.tensor_tensor(st_sag[:, j, b, :], bank[3 * b + j][:, :], sag_base[:, j, :], ALU.add)
            ins.then_inc(SEM["sa_ready"], 1)
        dve.tensor_tensor(rows_t[:, 3:6, :, :], rows_t[:, 3:6, :, :], rows_t[:, 0:3, :, :], ALU.subtract)\
           .then_inc(SEM["dve"], 1)
        dve.wait_ge(SEM["dve"], c.next("dve"))
        for j in range(3):
            ins = dve.tensor_tensor(rows_t[:, 3 + j, :, :], rows_t[:, 3 + j, :, :],
                                    mu_rows[:, j:j + 1, :].broadcast_to([P, NCH, HD]), ALU.mult)
        ins.then_inc(SEM["dve"], 1)
        dve.wait_ge(SEM["dve"], c.next("dve"))
        dve.tensor_tensor(rows_t[:, 0:3, :, :], rows_t[:, 0:3, :, :], rows_t[:, 3:6, :, :], ALU.add).then_inc(SEM["mixed"], 1)
        dve.wait_ge(SEM["mixed"], c.next("mixed"))
        V, R_, K_, SIG, A_, G_, T6, T7, T8 = (rows_t[:, j, :, :] for j in range(9))
        dve.wait_ge(SEM["cw_ready"], c.next("cw_ready"))
        dve.memset(gluT[:, :, 0:CONV - 1], 0.0).then_inc(SEM["dve"], 1)
        dve.wait_ge(SEM["dve"], c.next("dve"))
        dve.wait_ge(SEM["gluT_ready"], c.next("gluT_ready", TB))

        def tap(j, first=False):
            for ct in range(4):
                if first:
                    ins = dve.tensor_scalar(conv_o[:, ct, :], gluT[:, ct, 0:T], convw[:, ct, 0:1], convw[:, ct, CONV:CONV + 1],
                                            ALU.mult, ALU.add)
                else:
                    ins = dve.scalar_tensor_tensor(conv_o[:, ct, :], gluT[:, ct, ds(j, T)], convw[:, ct, ds(j, 1)],
                                                   conv_o[:, ct, :], ALU.mult, ALU.add)
            ins.then_inc(SEM["dve"], 1)
            dve.wait_ge(SEM["dve"], c.next("dve"))

        tap(0, True)
        tap(1)
        tap(2)
        for b in range(TB):
            dve.wait_ge(SEM[f"sig_st{b}"], c.next(f"sig_st{b}", 16))
        for n in ("iclr_st", "g_st"):
            dve.wait_ge(SEM[n], c.next(n, 16))
        dve.wait_ge(SEM["pc_ready"], c.next("pc_ready"))
        dve.tensor_tensor(T8, K_, par(0), ALU.mult).then_inc(SEM["dve"], 1)
        dve.wait_ge(SEM["dve"], c.next("dve"))
        dve.tensor_tensor(T7, T8, T8, ALU.mult).then_inc(SEM["dve"], 1)
        dve.wait_ge(SEM["dve"], c.next("dve"))
        dve.tensor_reduce(small[:, 2, :], T7, X, ALU.add).then_inc(SEM["dve"], 1)
        dve.wait_ge(SEM["dve"], c.next("dve"))
        dve.tensor_scalar(small[:, 2, :], small[:, 2, :], 1e-24, None, ALU.max).then_inc(SEM["kk_var"], 1)
        dve.wait_ge(SEM["kk_rstd"], c.next("kk_rstd"))
        dve.tensor_tensor(T8, T8, per_chunk(small[:, 1, :]), ALU.mult)
        dve.wait_ge(SEM["iclr_ld"], c.next("iclr_ld", 16))
        dve.scalar_tensor_tensor(T7, A_, -1.0, par(1), ALU.add, ALU.mult).then_inc(SEM["dve"], 1)
        dve.wait_ge(SEM["dve"], c.next("dve"))
        dve.scalar_tensor_tensor(K_, T7, 1.0, K_, ALU.add, ALU.mult).then_inc(SEM["k_new"], 1)
        c.count("k_new")
        dve.tensor_tensor(A_, T8, A_, ALU.mult).then_inc(SEM["dve"], 1)
        dve.wait_ge(SEM["dve"], c.next("dve"))
        dve.wait_ge(SEM["k_new"], c.so_far("k_new"))
        dve.wait_ge(SEM["e_exp"], c.next("e_exp"))
        dve.wait_ge(SEM["cum_ready"], c.next("cum_ready", 3))
        dve.tensor_tensor(SIG, T8, T6, ALU.mult).then_inc(SEM["dve"], 1)
        dve.wait_ge(SEM["dve"], c.next("dve"))
        dve.wait_ge(SEM["e_exp"], c.next("e_exp"))
        dve.tensor_tensor(T6, K_, decays[0], ALU.mult).then_inc(SEM["dve"], 1)
        dve.wait_ge(SEM["dve"], c.next("dve"))
        dve.wait_ge(SEM["e_exp"], c.next("e_exp"))
        dve.wait_ge(SEM["made"], c.next("made"))
        dve.tensor_tensor(K_, K_, decays[1], ALU.mult)
        dve.wait_ge(SEM["e_exp"], c.next("e_exp"))
        dve.tensor_tensor(R_, R_, T7, ALU.mult).then_inc(SEM["dve"], 1)
        dve.wait_ge(SEM["dve"], c.next("dve"))
        dve.scalar_tensor_tensor(T7, A_, -1.0, decays[0], ALU.mult, ALU.mult).then_inc(SEM["dve"], 1)
        dve.wait_ge(SEM["dve"], c.next("dve"))
        dve.tensor_tensor(A_, A_, decays[1], ALU.mult).then_inc(SEM["e_done"], 1)
        dve.memset(state, 0.0).then_inc(SEM["m_new"], 1)
        dve.wait_ge(SEM["m_new"], c.next("m_new"))
        dve.wait_ge(SEM["made"], c.next("made"))
        dve.tensor_reduce(bonus, y_gain, X, ALU.add).then_inc(SEM["bonus_done"], 1)

        def masks(q):
            dve.wait_ge(SEM[f"gram_mm{q}"], c.next(f"gram_mm{q}"))
            dve.tensor_tensor(gram[q][:, 0:3, :], bank[2 * q + 1][:, 0:384].rearrange("p (a t) -> p a t", a=3),
                              gram_mask[:, 0:3, :], ALU.mult)
            dve.tensor_tensor(gram[q][:, 3:5, :], bank[2 * q][:, 0:256].rearrange("p (a t) -> p a t", a=2),
                              gram_mask[:, 3:5, :], ALU.mult).then_inc(SEM[f"gram_ready{q}"], 1)
            dve.wait_ge(SEM[f"gram_ready{q}"], c.next(f"gram_ready{q}"))
            dve.tensor_tensor(inv[q], gram[q][:, 1, :], ident[:, :], ALU.add).then_inc(SEM[f"inv_ready{q}"], 1)
            c.count(f"inv_ready{q}")

        def factor(q, step):
            dve.wait_ge(SEM[f"inv_mm{q}"], c.next(f"inv_mm{q}"))
            dve.wait_ge(SEM[f"inv_ready{q}"], c.so_far(f"inv_ready{q}"))
            dve.tensor_tensor(inv[q], inv[q], bank[2 * q + min(step - 1, 1)][:, 0:P], ALU.add).then_inc(SEM[f"inv_ready{q}"], 1)
            c.count(f"inv_ready{q}")

        def quarter(j, ct):
            dve.wait_ge(SEM["dve"], c.so_far("dve"))
            dve.scalar_tensor_tensor(conv_o[:, ct, :], gluT[:, ct, ds(j, T)], convw[:, ct, ds(j, 1)],
                                     conv_o[:, ct, :], ALU.mult, ALU.add).then_inc(SEM["dve"], 1)
            c.count("dve")

        def take_w(n):
            dve.wait_ge(SEM["w_mm"], c.next("w_mm"))
            dve.tensor_copy(w_s, bank[4][:, 0:HD]).then_inc(SEM["w_ready"], 1)
            dve.tensor_tensor(sdec, state, pc[:, :, ds(n, 1)].broadcast_to([P, 4, HD]), ALU.mult).then_inc(SEM["dve"], 1)
            c.count("dve")

        def take_u(between=lambda: None):
            dve.wait_ge(SEM["u_mm"], c.next("u_mm"))
            dve.tensor_copy(u_s, bank[4][:, HD:2 * HD]).then_inc(SEM["u_ready"], 1)
            between()
            dve.wait_ge(SEM["kv_mm"], c.next("kv_mm"))
            dve.wait_ge(SEM["dve"], c.so_far("dve"))
            dve.tensor_tensor(sdec, sdec, bank[5][:, 0:256].rearrange("p (j n) -> p j n", j=4), ALU.add).then_inc(SEM["dve"], 1)
            c.count("dve")

        def new_state():
            dve.wait_ge(SEM["m_mm"], c.next("m_mm"))
            dve.wait_ge(SEM["dve"], c.so_far("dve"))
            dve.tensor_tensor(state, sdec, bank[7][:, 0:256].rearrange("p (j n) -> p j n", j=4), ALU.add)\
               .then_inc(SEM["m_new"], 1)
            dve.wait_ge(SEM["m_new"], c.next("m_new"))

        masks(0)
        masks(1)
        for q, step in ((0, 1), (1, 1), (0, 2), (0, 3)):
            factor(q, step)
        with c.loop(NCH // 2 - 1, "dve scan") as i:
            quarters = iter([(i * 4 + 3 + j, ct) for j in range(4) for ct in range(4)])
            def taps(n):
                for _ in range(n):
                    quarter(*next(quarters))

            take_w(i * 2)
            factor(1, 2)
            taps(1)
            take_u(lambda: taps(1))
            factor(1, 3)
            taps(2)
            new_state()
            dve.wait_ge(SEM["y_mm"], c.next("y_mm"))
            masks(0)
            taps(2)
            take_w(i * 2 + 1)
            taps(1)
            take_u(lambda: taps(1))
            taps(2)
            factor(0, 1)
            taps(1)
            new_state()
            dve.wait_ge(SEM["y_mm"], c.next("y_mm"))
            masks(1)
            for (q, step), n in (((0, 2), 2), ((0, 3), 1), ((1, 1), 2)):
                factor(q, step)
                taps(n)
        take_w(NCH - 2)
        factor(1, 2)
        take_u()
        factor(1, 3)
        new_state()
        take_w(NCH - 1)
        dve.wait_ge(SEM["y_mm"], c.next("y_mm"))
        take_u()
        new_state()
        dve.wait_ge(SEM["cgb_ld"], c.next("cgb_ld", 48))
        dve.wait_ge(SEM["y_out"], c.next("y_out", NCH))
        dve.tensor_reduce(small[:, 2, :], T8, X, ALU.add).then_inc(SEM["dve"], 1)
        dve.wait_ge(SEM["dve"], c.next("dve"))
        dve.tensor_scalar(small[:, 2, :], small[:, 2, :], 1.0 / HD, None, ALU.mult).then_inc(SEM["dve"], 1)
        dve.wait_ge(SEM["dve"], c.next("dve"))
        dve.tensor_tensor(T8, T8, per_chunk(small[:, 2, :]), ALU.subtract).then_inc(SEM["dve"], 1)
        dve.wait_ge(SEM["dve"], c.next("dve"))
        dve.tensor_tensor(T7, T8, T8, ALU.mult).then_inc(SEM["dve"], 1)
        dve.wait_ge(SEM["dve"], c.next("dve"))
        dve.tensor_reduce(small[:, 2, :], T7, X, ALU.add).then_inc(SEM["dve"], 1)
        dve.wait_ge(SEM["dve"], c.next("dve"))
        dve.tensor_scalar(small[:, 2, :], small[:, 2, :], 1.0 / HD, GN_EPS, ALU.mult, ALU.add).then_inc(SEM["kk_var"], 1)
        dve.wait_ge(SEM["made"], c.next("made", 4))
        dve.tensor_tensor(T8, T8, y_gain, ALU.mult).then_inc(SEM["dve"], 1)
        dve.wait_ge(SEM["dve"], c.next("dve"))
        dve.wait_ge(SEM["kk_rstd"], c.next("kk_rstd"))
        dve.tensor_tensor(T8, T8, per_chunk(small[:, 1, :]), ALU.mult).then_inc(SEM["dve"], 1)
        dve.wait_ge(SEM["dve"], c.next("dve"))
        dve.tensor_tensor(T8, T8, y_add, ALU.add).then_inc(SEM["yr_ready"], 1)
        for b in range(TB):
            dve.wait_ge(SEM["convT"], c.next("convT"))
            dve.bn_stats(stats[:, 0, :], bank[b][:, :]).then_inc(SEM["dve"], 1)
            dve.wait_ge(SEM["dve"], c.next("dve"))
            c.hold()
            dve.bn_aggr(mv[:, b, :], stats[:, 0, :]).then_inc(SEM["dve"], 1)
            dve.wait_ge(SEM["dve"], c.next("dve"))
            dve.tensor_scalar(ve[:, b:b + 1], mv[:, b, 1:2], LN_EPS, None, ALU.add).then_inc(SEM["var"], 1)
            dve.scalar_tensor_tensor(y_conv[:, b, :], bank[b][:, :], mv[:, b, 0:1], conv_gb[:, 0, :], ALU.subtract, ALU.mult)\
               .then_inc(SEM["dve"], 1)
            dve.wait_ge(SEM["dve"], c.next("dve"))
        for b in range(TB):
            dve.wait_ge(SEM["rstd"], c.next("rstd"))
            dve.scalar_tensor_tensor(y_conv[:, b, :], y_conv[:, b, :], rstd[:, b:b + 1], conv_gb[:, 1, :], ALU.mult, ALU.add)\
               .then_inc(SEM["conv_n"], 1)
        transposed()
        next_units(0)
        two_norms(1.0)
        ffn(1.0)
        next_units(0)
        two_norms(0.5)
        ffn(1.0)
        for s in range(3):
            low(s)
        two_norms(0.5)
        low(3)
        dve.wait_ge(SEM["c_ld"], c.next("c_ld", 16 * 6))
        with c.loop(2, "dve fqk") as i:
            for p in range(2):
                dve.wait_ge(SEM[f"used{2 * p + 1}"], c.so_far(f"used{2 * p + 1}"))
                for b in range(TB):
                    dve.wait_ge(SEM["fsq"], c.next("fsq"))
                    dve.tensor_reduce(fss, rope2.rearrange("p (h d) -> p h d", d=HD), X, ALU.add).then_inc(SEM["sq_free"], 1)
                    dve.wait_ge(SEM["sq_free"], c.next("sq_free"))
                    dve.tensor_scalar(fss, fss, 1.0 / HD, RMS_EPS, ALU.mult, ALU.add).then_inc(SEM["fss_ready"], 1)
                    dve.wait_ge(SEM["frs_ready"], c.next("frs_ready"))
                    t = rope1.rearrange("p (h d) -> p h d", d=HD)
                    ins = dve.tensor_tensor(t, bank[2 * b + p][:, :].rearrange("p (h d) -> p h d", d=HD),
                                            frs.rearrange("p (h a) -> p h a", a=1).broadcast_to([P, 8, HD]), ALU.mult)
                    if b == TB - 1:
                        ins.then_inc(SEM[f"gen{p}"], 1)
                        dve.wait_ge(SEM[f"gen{p}"], c.next(f"gen{p}"))
                    else:
                        ins.then_inc(SEM["dve"], 1)
                        dve.wait_ge(SEM["dve"], c.next("dve"))
                    dve.tensor_tensor(y[:, b, p * HALF:(p + 1) * HALF].rearrange("p (h d) -> p h d", d=HD), t,
                                      qk_gain[:, ds(i, 1), :].broadcast_to([P, 8, HD]), ALU.mult).then_inc(SEM["rope"], 1)
                    dve.wait_ge(SEM["rope"], c.next("rope"))
                next_units(p)
        dve.wait_ge(SEM["used0"], c.so_far("used0"))
        for b in range(TB):
            ins = dve.tensor_tensor(flog[:, b, :], bank[2 * b][:, 0:FOX], fbias, ALU.add)
        ins.then_inc(SEM["gen0"], 1)
        dve.wait_ge(SEM["gen0"], c.next("gen0"))
        dve.scalar_tensor_tensor(fabs, flog, -1.0, flog, ALU.mult, ALU.max).then_inc(SEM["fabs"], 1)
        low(0)
        dve.wait_ge(SEM["fln"], c.next("fln"))
        dve.scalar_tensor_tensor(flog, flog, 0.0, fabs, ALU.min, ALU.subtract).then_inc(SEM["flog_ready"], 1)
        dve.wait_ge(SEM["cum_mm"], c.next("cum_mm"))
        dve.tensor_scalar(cumh, bank[1][0:FOX, 0:T], -1.0, None, ALU.mult).then_inc(SEM["dve"], 1)
        dve.wait_ge(SEM["dve"], c.next("dve"))
        dve.scalar_tensor_tensor(cuml, bank[1][0:FOX, 0:T], -1.0, cumh.bitcast(f32), ALU.mult, ALU.subtract)\
           .then_inc(SEM["cumT_ready"], 1)
        c.count("gen1")
        c.count("gen0")
        low(0)
        low(1)

        def maxima(hp):
            q = hp % 2
            dve.wait_ge(SEM[f"s_ready{q}"], c.next(f"s_ready{q}"))
            for j in range(4):
                at = slice(0, P) if j < 2 else slice(P, P + T)
                ins = dve.tensor_reduce(fatt[q][:, j:j + 1], bank[score_banks[q][j % 2]][:, at], X, ALU.max, negate=True)
            ins.then_inc(SEM["smax"], 1)

        def inverses(hp):
            q = hp % 2
            dve.wait_ge(SEM["e_ready"], c.next("e_ready", 4))
            dve.reciprocal(fatt[q][:, 8:12], fatt[q][:, 4:8]).then_inc(SEM["rinv"], 1)

        def take_turned():
            dve.wait_ge(SEM["eT1_tr"], c.next("eT1_tr"))
            dve.tensor_copy(feT[:, 1, :, :], bank[7][:, 0:384].rearrange("p (k t) -> p k t", k=3)).then_inc(SEM["eT1_ready"], 1)

        def take_output(i, hp):
            dve.wait_ge(SEM["rinv"], c.next("rinv"))
            dve.wait_ge(SEM["o_ready"], c.next("o_ready"))
            dve.tensor_tensor(y[:, :, ds(i * 512 + hp * P, P)].rearrange("p b (m e) -> p b m e", m=2),
                              bank[6][:, 0:T].rearrange("p (b m e) -> p b m e", b=TB, m=2),
                              fatt[hp % 2][:, 8:12].rearrange("p (b m a) -> p b m a", b=TB, a=1).broadcast_to([P, TB, 2, HD]),
                              ALU.mult).then_inc(SEM["o_out"], 1)
            c.count("o_out")

        with c.loop(2, "dve fox") as i:
            maxima(0)
            inverses(0)
            maxima(1)
            take_turned()
            inverses(1)
            take_output(i, 0)
            maxima(2)
            take_turned()
            inverses(2)
            maxima(3)
            take_output(i, 1)
            take_turned()
            c.count("gen0")
            low(0)
            inverses(3)
            take_output(i, 2)
            take_turned()
            low(1)
            take_output(i, 3)
        dve.wait_ge(SEM["o_out"], c.so_far("o_out"))
        for b in range(TB):
            dve.wait_ge(SEM["gate_on"], c.next("gate_on"))
            dve.tensor_tensor(y[:, b, :], y[:, b, :], fgate[:, b, :], ALU.mult).then_inc(SEM["hb_ready"], 1)
            transposed(b)
        low(2)
        low(3)
        next_units(0)
        two_norms(1.0)
        ffn(1.0)
        for b in range(TB):
            var_of(b, 0.5)
            if b == 0:
                dve.wait_ge(SEM["gains_ld"], c.next("gains_ld", 32))
            post(b, "done")

    def second_pe(c, pe, three, panel, panel_unit, enter, turn_panel, ffn):
        c.count("e_ready", 4 * 8 * DEPTH)
        enter(y, "x_ready", False)
        ffn()
        enter(y, "x_ready", True)
        for p in (1, 0, 1, 0):
            panel(p)
        pe.wait_ge(SEM["ab_ld"], c.next("ab_ld", 16 * 17))
        pe.wait_ge(SEM["gen1"], c.so_far("gen1"))
        c.count("gen1")
        pe.wait_ge(SEM["lo2"], c.next("lo2"))
        for k in range(KT):
            for b in range(TB):
                t = slice(b * P, (b + 1) * P)
                r = slice(k * 256, (k + 1) * 256)
                ins = three(bank[2 * b + 1][:, 0:256], xTh[:, k, t], xTl[:, k, t], wh[2][:, r], wl[2][:, r], k == 0, k == KT - 1)
        ins.then_inc(SEM["used2"], 1)
        for ct in range(4):
            ins = pe.transpose(bank[4][:, ct * 32:(ct + 1) * 32], convw_rows[0:32, ct * P:(ct + 1) * P], ident[0:32, 0:32])
        ins.then_inc(SEM["cw_tr"], 1)
        pe.wait_ge(SEM["glu_ready"], c.next("glu_ready"))
        for b in range(TB):
            for ct in range(4):
                ins = pe.transpose(bank[6 + b][:, ct * P:(ct + 1) * P], glu[:, b, ct * P:(ct + 1) * P], ident[:, :])
            ins.then_inc(SEM["glu_tr"], 1)
        pe.wait_ge(SEM["cw_ready"], c.next("cw_ready"))
        pe.wait_ge(SEM["lora_ready"], c.next("lora_ready", 2))
        for w in range(2):
            for b in range(TB):
                ins = pe.transpose(bank[4][:, w * T + b * P:w * T + (b + 1) * P], lora[:, b, w * P:(w + 1) * P], ident[:, :])
        ins.then_inc(SEM["lora_tr"], 1)
        pe.wait_ge(SEM["loraT_ready"], c.next("loraT_ready"))
        pe.wait_ge(SEM["gen0"], c.so_far("gen0"))
        pe.wait_ge(SEM["gen1"], c.so_far("gen1"))
        for b in range(TB):
            t = slice(b * P, (b + 1) * P)
            pe.matmul(bank[3 * b][:, :], loraT[0:64, 0, t], lora_up[0:64, :], start=True, stop=True)
            pe.matmul(bank[3 * b + 1][:, :], loraT[64:128, 0, t], lora_up[64:128, :], start=True, stop=True)
            pe.matmul(bank[3 * b + 2][:, :], loraT[:, 1, t], gate_up, start=True, stop=True).then_inc(SEM["ups_ready"], 1)
        pe.wait_ge(SEM["sag_ready"], c.next("sag_ready", 2))
        pe.wait_ge(SEM["gluT_ready"], c.next("gluT_ready", 2))
        for j in range(4):
            for b in range(TB):
                ins = pe.matmul(bank[7][:, j * NCH + b * 8:j * NCH + (b + 1) * 8], st_sag[:, 0, b, j * P:(j + 1) * P],
                                chunk_mask, start=True, stop=True)
        ins.then_inc(SEM["tot_ready"], 1)
        pe.wait_ge(SEM["pc_ready"], c.next("pc_ready"))
        for b in range(TB):
            pe.wait_ge(SEM[f"sig_ld{b}"], c.next(f"sig_ld{b}", 16))
        for m, bk in ((0, 0), (2, 4), (1, 2)):
            for h in range(2):
                ins = pe.matmul(bank[bk + h][:, :], cum_mask[:, m, :],
                                rows_t[:, ROW_SIG, 8 * h:8 * h + 8, :].rearrange("p c n -> p (c n)"), start=True, stop=True)
            ins.then_inc(SEM["cum_ready"], 1)
        pe.wait_ge(SEM["e_done"], c.next("e_done"))

        def transpose_rows(q):
            pe.wait_ge(SEM[f"rkab_ready{q}"], c.next(f"rkab_ready{q}"))
            for w in range(3):
                ins = pe.transpose(bank[2 * q][:, w * P:(w + 1) * P], rkab[q][:, w, :], ident[:, :])
            ins.then_inc(SEM[f"rows_tr{q}"], 1)

        def grams(q):
            pe.wait_ge(SEM[f"rowsT_ready{q}"], c.next(f"rowsT_ready{q}"))
            (r0, a0, k0), (r1, a1, b1) = ([rowsT[q][h * HD:(h + 1) * HD, w, :] for w in range(3)] for h in range(2))
            g0, g1 = bank[2 * q], bank[2 * q + 1]
            for o, lhs, rhs in ((g1[:, 0:P], b1, r1), (g1[:, P:2 * P], b1, a1), (g1[:, 2 * P:3 * P], a1, b1),
                                (g0[:, 0:P], k0, r0), (g0[:, P:2 * P], k0, a0)):
                ins = pe.matmul(o, lhs, rhs, start=True, stop=True)
            ins.then_inc(SEM[f"gram_mm{q}"], 1)

        def powers(q, step):
            if step == 0:
                pe.wait_ge(SEM[f"gram_ready{q}"], c.next(f"gram_ready{q}"))
            else:
                pe.wait_ge(SEM[f"pw_ready{q}"], c.next(f"pw_ready{q}"))
                pe.wait_ge(SEM[f"inv_ready{q}"], c.next(f"inv_ready{q}"))
            o = bank[2 * q + step % 2]
            if step == 0:
                xx, xt = gram[q][:, 1, :], gram[q][:, 2, :]
            else:
                xx, xt = pw[q][:, 2 * step - 2, :], pw[q][:, 2 * step - 1, :] if step < 3 else None
            if step < 2:
                pe.matmul(o[:, 0:P], xt, xx, start=True, stop=True)
                pe.matmul(o[:, P:2 * P], xx, xt, start=True, stop=True).then_inc(SEM[f"pw_mm{q}"], 1)
            elif step == 2:
                pe.matmul(o[:, 0:P], xx, xt, start=True, stop=True).then_inc(SEM[f"pw_mm{q}"], 1)
            if step:
                pe.matmul(bank[2 * q + min(step - 1, 1)][:, 0:P], xt if step < 3 else xx, inv[q], start=True, stop=True)\
                  .then_inc(SEM[f"inv_mm{q}"], 1)

        def before_u(n, q):
            v_c = rows_t[:, ROW_V, ds(n, 1), :].rearrange("p a n -> p (a n)")
            pe.wait_ge(SEM[f"ra_ready{q}"], c.next(f"ra_ready{q}"))
            pe.wait_ge(SEM["m_new"], c.next("m_new"))
            for j in range(4):
                pe.matmul(bank[4][:, 0:HD], ra_exp[q][:, 1, j, :], state[:, j, :], start=(j == 0), stop=False)
            pe.matmul(bank[4][:, 0:HD], gram[q][:, 4, :], v_c, start=False, stop=True).then_inc(SEM["w_mm"], 1)
            pe.wait_ge(SEM["y_out"], c.so_far("y_out"))
            c.count("y_out")
            for j in range(4):
                pe.matmul(bank[6][:, 0:HD], ra_exp[q][:, 0, j, :], state[:, j, :], start=(j == 0), stop=False)
            pe.matmul(bank[6][:, 0:HD], gram[q][:, 3, :], v_c, start=False, stop=False)

        def keys_values(n, q):
            v_c = rows_t[:, ROW_V, ds(n, 1), :].rearrange("p a n -> p (a n)")
            pe.wait_ge(SEM[f"exp_ready{q}"], c.next(f"exp_ready{q}"))
            for j in range(4):
                ins = pe.matmul(bank[5][:, j * HD:(j + 1) * HD], kt_exp[q][:, j * P:(j + 1) * P], v_c, start=True, stop=True)
            ins.then_inc(SEM["kv_mm"], 1)

        def u_of(q):
            pe.wait_ge(SEM["w_ready"], c.next("w_ready"))
            pe.wait_ge(SEM[f"inv_ready{q}"], c.next(f"inv_ready{q}"))
            pe.matmul(bank[4][:, HD:2 * HD], inv[q], w_s, start=True, stop=True).then_inc(SEM["u_mm"], 1)

        def after_u(q):
            pe.wait_ge(SEM["u_ready"], c.next("u_ready"))
            for j in range(4):
                ins = pe.matmul(bank[7][:, j * HD:(j + 1) * HD], bt_exp[q][:, j * P:(j + 1) * P], u_s, start=True, stop=True)
            ins.then_inc(SEM["m_mm"], 1)
            pe.matmul(bank[6][:, 0:HD], gram[q][:, 0, :], u_s, start=False, stop=True).then_inc(SEM["y_mm"], 1)

        for q in range(2):
            transpose_rows(q)
        for q in range(2):
            grams(q)
        for q, step in ((0, 0), (1, 0), (0, 1), (1, 1), (0, 2), (0, 3)):
            powers(q, step)
        with c.loop(NCH // 2 - 1, "pe scan") as i:
            before_u(i * 2, 0)
            powers(1, 2)
            u_of(0)
            keys_values(i * 2, 0)
            powers(1, 3)
            transpose_rows(0)
            after_u(0)
            transpose_rows(1)
            grams(0)
            before_u(i * 2 + 1, 1)
            u_of(1)
            powers(0, 0)
            keys_values(i * 2 + 1, 1)
            grams(1)
            powers(0, 1)
            after_u(1)
            powers(0, 2)
            powers(1, 0)
            powers(0, 3)
            powers(1, 1)
        before_u(NCH - 2, 0)
        powers(1, 2)
        u_of(0)
        keys_values(NCH - 2, 0)
        powers(1, 3)
        after_u(0)
        before_u(NCH - 1, 1)
        u_of(1)
        keys_values(NCH - 1, 1)
        after_u(1)
        for b in range(TB):
            for ct in range(4):
                ins = pe.transpose(bank[b][:, ct * P:(ct + 1) * P], conv_o[:, ct, b * P:(b + 1) * P], ident[:, :])
            ins.then_inc(SEM["convT"], 1)
        pe.wait_ge(SEM["yb_ready"], c.next("yb_ready", 2))
        pe.wait_ge(SEM["y_ld"], c.next("y_ld", 16))
        enter(lambda b, k: (y_rwkv if k < 4 else y_conv)[:, b, (k % 4) * P:(k % 4 + 1) * P], None, True)
        panel(1, True)
        enter(y, "x_ready", False)
        ffn()
        enter(y, "x_ready", False)
        ffn()
        enter(y, "x_ready", True)
        panel(1)
        turn_panel(0)
        for n in (2, 3):
            panel(n % 2)
            turn_panel(n - 1)
        pe.wait_ge(SEM["c_ld"], c.next("c_ld", 16 * 6))
        pe.wait_ge(SEM["gen0"], c.so_far("gen0"))
        c.count("gen0")
        pe.wait_ge(SEM["lo0"], c.next("lo0"))
        for k in range(KT):
            for b in range(TB):
                t = slice(b * P, (b + 1) * P)
                r = slice(k * FOX, (k + 1) * FOX)
                ins = three(bank[2 * b][:, 0:FOX], xTh[:, k, t], xTl[:, k, t], wh[0][:, r], wl[0][:, r], k == 0, k == KT - 1)
        ins.then_inc(SEM["used0"], 1)
        panel(1)
        pe.wait_ge(SEM["qk_ready"], c.next("qk_ready", 2))
        turn_panel(3)
        panel(0)
        pe.wait_ge(SEM["qk_ready"], c.next("qk_ready", 2))
        pe.wait_ge(SEM["gen0"], c.so_far("gen0"))
        pe.wait_ge(SEM["gen1"], c.so_far("gen1"))
        pe.wait_ge(SEM["flog_ready"], c.next("flog_ready"))
        pe.matmul(bank[1][0:FOX, 0:P], flog[:, 0, :], tri_c, start=True, stop=True)
        pe.matmul(bank[1][0:FOX, P:T], flog[:, 0, :], ones_c, start=True, stop=False)
        pe.matmul(bank[1][0:FOX, P:T], flog[:, 1, :], tri_c, start=False, stop=True).then_inc(SEM["cum_mm"], 1)
        pe.wait_ge(SEM["cumT_ready"], c.next("cumT_ready"))

        def scores(hp):
            q = hp % 2
            pe.wait_ge(SEM["qh_ready"], c.next("qh_ready"))
            for m in range(2):
                f = slice(m * HD, (m + 1) * HD)
                pair = selh[q][:, m * P:(m + 1) * P]
                for at, t, n in ((0, slice(0, P), P), (P, slice(P, T), T)):
                    o = bank[score_banks[q][m]][:, at:at + n]
                    pe.matmul(o, identb, negm_wide[:, T - n:T], start=True, stop=False)
                    pe.matmul(o, pair, cumh[:, 0:n], start=False, stop=False)
                    pe.matmul(o, pair, cuml[:, 0:n], start=False, stop=False)
                    ins = pe.matmul(o, qh[q][f, t], kh[q][f, 0:n], start=False, stop=True)
            ins.then_inc(SEM[f"s_ready{q}"], 1)

        def turn():
            pe.wait_ge(SEM["e_ready"], c.next("e_ready", 4))
            pe.wait_ge(SEM["o_out"], c.so_far("o_out"))
            c.count("o_out")
            for m, bk, to in ((1, 7, "eT1_tr"), (0, 6, "eT_tr")):
                for j in range(3):
                    ins = pe.transpose(bank[bk][:, j * P:(j + 1) * P], fe_t[:, m, j * P:(j + 1) * P], ident[:, :])
                ins.then_inc(SEM[to], 1)

        def outputs(i, hp):
            pe.wait_ge(SEM["aT_ready"], c.next("aT_ready"))
            pe.wait_ge(SEM["eT1_ready"], c.next("eT1_ready"))
            for b in range(TB):
                for m in range(2):
                    o = bank[6][:, (2 * b + m) * HD:(2 * b + m + 1) * HD]
                    for j in range(b + 1):
                        ins = pe.matmul(o, feT[:, m, b + j, :], fval[:, j, ds(i * 512 + hp * P + m * HD, HD)],
                                        start=(j == 0), stop=(j == b))
            ins.then_inc(SEM["o_ready"], 1)

        with c.loop(2, "pe fox") as i:
            scores(0)
            panel_unit(0, 0)
            scores(1)
            turn()
            panel_unit(0, 1)
            outputs(i, 0)
            scores(2)
            turn()
            scores(3)
            outputs(i, 1)
            turn()
            outputs(i, 2)
            turn()
            outputs(i, 3)
        enter(y, "hb_ready", True)
        panel(1, True)
        enter(y, "x_ready", False)
        ffn()


    @block.sync
    def _(sp):
        c = Counts(sp, SEM["held"])

        def load(s, *pieces):
            sp.wait_ge(SEM[f"lo{s}"], c.so_far(f"lo{s}"))
            c.count(f"lo{s}")
            for dst, src in pieces:
                sp.dma_start(dst, src).then_inc(SEM[f"ld{s}"], 16)

        def rows(w):
            return w.rearrange("(k p) n -> p k n", p=P)

        def up(w1, w3, j):
            for s in range(2):
                dst = wf[s][:, :].rearrange("p (k n) -> p k n", k=4)
                load(s, *((dst[:, :, m * STEP:(m + 1) * STEP],
                           rows(w)[:, 4 * s:4 * s + 4, ds(j * STEP, STEP)]) for m, w in enumerate((w1, w3))))

        def down(w2, j, s=2):
            load(s, (wf[s][:, :].rearrange("p (k n) -> p k n", k=2), rows(w2[ds(j * STEP, STEP), :])))

        def half_panel(w, col, s, h):
            load(s, (wf[s][:, :].rearrange("p (k n) -> p k n", k=4), rows(w)[:, 4 * h:4 * h + 4, ds(col, HALF)]))

        def ffn(w1, w3, w2):
            up(w1, w3, 0)
            with c.loop(STEPS - 1, "sp ffn") as j:
                up(w1, w3, j + 1)
                down(w2, j)
            down(w2, STEPS - 1, 3)

        def two_panels(w, col):
            for s in range(4):
                half_panel(w, col + HALF * (s // 2), s, s % 2)

        def layer_of(name, l):
            w = a[name][ds(l, 1)]
            return w.rearrange("a f k n -> (a f) k n") if len(w.shape) == 4 else w.rearrange("a k n -> (a k) n")

        for n in STARTED:
            sp.sem_inc(SEM[n], 1 + TB if n == "x_ready" else 1)
        sp.dma_start(ident[:, :], a["c_ident"]).then_inc(SEM["x_ld"], 16)
        sp.dma_start(x[:, :, :], a["x"][0].rearrange("(b p) n -> p b n", p=P)).then_inc(SEM["x_ld"], 16)
        with c.loop(DEPTH, "sp layer") as l:
            w1, w3, w2 = (layer_of(n, l) for n in ("ffn_w1", "ffn_w3", "ffn_w2"))
            w_in, w_br, w_out = (layer_of(n, l) for n in ("w_in", "w_branch", "w_out"))
            ffn(w1[0], w3[0], w2[0])
            two_panels(w_in, 0)
            two_panels(w_in, D)
            with c.loop(2, "sp four") as i:
                two_panels(w_in, i * D + 2 * D)
            two_panels(w_in, 4 * D)
            with c.loop(2, "sp four") as i:
                two_panels(w_in, i * D + 5 * D)
            two_panels(w_br[0], 0)
            two_panels(w_br[1], 0)
            two_panels(w_out, 0)
            ffn(w1[1], w3[1], w2[1])
        second_sp(c, sp, ffn, half_panel, load, rows)

    @block.gpsimd
    def _(pool):
        c = Counts(pool, SEM["held"])

        def gains_load(*rows_):
            for i, r in enumerate(rows_):
                pool.dma_start(gains[:, i, :], bcast_row(r, D)).then_inc(SEM["gains_ld"], 16)

        def power(dst, src, n, got, to):
            pool.wait_ge(SEM[got], c.next(got))
            pool.tensor_tensor(dst, src, mhalf[:, 0:n], ALU.pow).then_inc(SEM[to], 1)

        def norm():
            for b in range(TB):
                power(rstd[:, b:b + 1], ve[:, b:b + 1], 1, "var", "rstd")

        def pre_norm():
            for b in range(TB):
                power(rstd[:, b:b + 1], ve[:, b:b + 1], 1, "pre_var", "pre_rstd")

        def of_layer(name, l):
            return a[name][ds(l, 1)].rearrange("a k n -> (a k) n")

        def ln_rows(l, i):
            gains_load(of_layer("ln_g", l)[i:i + 1, :], of_layer("ln_b", l)[i:i + 1, :])

        pool.wait_ge(SEM["const_ld"], c.next("const_ld", 16 * 6))

        with c.loop(DEPTH, "pool layer") as l:
            pool.wait_ge(SEM["x_ready"], c.so_far("x_ready"))
            ln_rows(l, 0)
            norm()
            pool.wait_ge(SEM["x_ready"], c.next("x_ready", TB))
            gb = of_layer("gate_b", l)
            gains_load(gb[0:1, :], gb[1:2, :])
            for dst, src in ((sgu_gb[:, 0, :], bcast_row(a["sgu_ln_g"][ds(l, 1), :], D)),
                             (sgu_gb[:, 1, :], bcast_row(a["sgu_ln_b"][ds(l, 1), :], D)),
                             (sgu_w, a["sgu_w"][ds(l, 1)].rearrange("a g t r -> t (a g) r")),
                             (sgu_bT, a["sgu_b"][ds(l, 1)].rearrange("a g t -> t (a g)")),
                             (part(14728, 256), bcast_row(a["lam"][ds(l, 1)].rearrange("a k n -> a (k n)"), 256)),
                             (dgain, bcast_row(a["diff_ln_g"][ds(l, 1), :], P))):
                pool.dma_start(dst, src).then_inc(SEM["sgu_ld"], 16)
            for b in range(TB):
                power(rstd[:, b:b + 1], ve[:, b:b + 1], 1, "var", "rstd")
            pool.wait_ge(SEM["qk_ready"], c.next("qk_ready", 8))
            with c.loop(2, "pool att") as i:
                for hh in range(4):
                    q = hh % 2
                    pool.wait_ge(SEM[f"s_ready{q}"], c.so_far(f"s_ready{q}"))
                    c.count(f"s_ready{q}")
                    head = [qkT[:, w, ds(i * 4 + hh, 1), :].rearrange("p a t -> p (a t)") for w in range(2)]
                    pool.tensor_tensor(qh[q], head[0], scale.broadcast_to([P, T]), ALU.mult)
                    pool.tensor_copy(kh[q], head[1]).then_inc(SEM["qh_ready"], 1)
            power(orstd, oss, 16, "o_var", "o_rstd")
            pool.wait_ge(SEM["m_ready"], c.next("m_ready", TB))
            ln_rows(l, 1)
            norm()
            pool.wait_ge(SEM["x_ready"], c.next("x_ready", TB))
            ln_rows(l, 2)
            norm()
            c.count("x_ready", TB)
        second_pool(c, pool, gains_load, power, norm, pre_norm)

    @block.scalar
    def _(act):
        c = Counts(act, SEM["held"])

        def prep(s, dmas=1):
            act.wait_ge(SEM[f"ld{s}"], c.next(f"ld{s}", 16 * dmas))
            act.wait_ge(SEM[f"used{s}"], c.so_far(f"used{s}"))
            c.count(f"used{s}")
            act.activation(wh[s][:, :], wf[s][:, :], ACT.Copy).then_inc(SEM[f"hi{s}"], 1)

        def transposed(*blocks):
            for r in (2 * b + h for b in blocks or range(TB) for h in range(2)):
                act.wait_ge(SEM["tr"], c.next("tr"))
                act.activation(xTh[:, 4 * (r % 2):4 * (r % 2) + 4, (r // 2) * P:(r // 2 + 1) * P],
                               bank[6 + r % 2][:, :].rearrange("p (k t) -> p k t", k=4), ACT.Copy)\
                   .then_inc(SEM["xt_hi"], 1)

        def ffn_step(last):
            if last:
                prep(3)
            else:
                prep(0, 2)
            act.wait_ge(SEM["used1"], c.so_far("used1"))
            for b in range(TB):
                act.activation(sil[:, b, :], bank[4 + b][:, 0:STEP], ACT.Silu).then_inc(SEM["h_silu"], 1)
            if not last:
                prep(1, 2)
            act.wait_ge(SEM["ht_tr"], c.next("ht_tr"))
            act.activation(hTh[:, :, :], bank[6][:, :].rearrange("p (k t) -> p k t", k=2), ACT.Copy)\
               .then_inc(SEM["ht_hi"], 1)
            if not last:
                prep(2)

        def ffn(then):
            with c.loop(STEPS - 1, "act ffn"):
                ffn_step(False)
            ffn_step(True)
            for p in range(2):
                c.count(f"gen{p}")
            for s, dmas in then:
                prep(s, dmas)

        def panel_evac(p, fn):
            act.wait_ge(SEM[f"used{2 * p + 1}"], c.so_far(f"used{2 * p + 1}"))
            for b in range(TB):
                ins = fn(b, bank[2 * b + p][:, :])
            ins.then_inc(SEM[f"gen{p}"], 1)
            c.count(f"gen{p}")

        def next_units(p, dmas=1):
            prep(2 * p, dmas)
            prep(2 * p + 1, dmas)

        for dst, src in ((mhalf[:, :], a["c_mhalf"]), (cs, a["c_rope"]), (tri, a["c_tri"]), (laminit, a["c_laminit"]),
                         (negm_f, a["c_negm"]), (identb_f, a["c_identb"])):
            act.dma_start(dst, src).then_inc(SEM["const_ld"], 16)
        act.wait_ge(SEM["const_ld"], c.next("const_ld", 16 * 6))
        prep(0, 2)
        prep(1, 2)
        act.wait_ge(SEM["x_ld"], c.next("x_ld", 32))

        with c.loop(DEPTH, "act layer") as l:
            transposed()
            ffn([(0, 1), (1, 1), (2, 1)])
            transposed()
            prep(3)
            with c.loop(2, "act uv") as i:
                for p in range(2):
                    panel_evac(p, lambda b, t: act.activation(
                        uv[:, ds(i, 1), b, p * HALF:(p + 1) * HALF], t.rearrange("p (a n) -> p a n", a=1), ACT.Gelu))
                    next_units(p)
            act.wait_ge(SEM["lam_s"], c.next("lam_s"))
            act.activation(lam_c[:, 0:2], lam_c[:, 0:2], ACT.Exp).then_inc(SEM["lam_e"], 1)
            def take_panel(n):
                for b in range(TB):
                    act.wait_ge(SEM["rope_tr"], c.next("rope_tr"))
                    act.activation(qkT[:, n // 2, 4 * (n % 2):4 * (n % 2) + 4, b * P:(b + 1) * P],
                                   bank[6 + b][:, :].rearrange("p (h t) -> p h t", h=4), ACT.Copy).then_inc(SEM["qk_ready"], 1)

            for n in range(4):
                c.count(f"gen{n % 2}")
                next_units(n % 2)
                if n:
                    take_panel(n - 1)
            for p in range(2):
                panel_evac(p, lambda b, t: act.activation(val[:, b, p * HALF:(p + 1) * HALF], t, ACT.Copy))
                next_units(p)
                if p == 0:
                    take_panel(3)

            def exps(hh):
                act.wait_ge(SEM["smax"], c.next("smax"))
                act.wait_ge(SEM["a_ready"], c.so_far("a_ready"))
                c.count("a_ready")
                for j in range(4):
                    at = slice(0, P) if j < 2 else slice(P, P + T)
                    act.activation(e_t[:, j % 2, at], bank[score_banks[hh % 2][j % 2]][:, at], ACT.Exp, bias=att[:, j:j + 1],
                                   accum_out=att[:, 4 + j:5 + j]).then_inc(SEM["e_ready"], 1)

            def take_turned():
                act.wait_ge(SEM["a_tr"], c.next("a_tr"))
                act.activation(aT, bank[6][:, 0:384].rearrange("p (k t) -> p k t", k=3), ACT.Copy).then_inc(SEM["aT_ready"], 1)

            def take_output(i, hh):
                act.wait_ge(SEM["o_ready"], c.next("o_ready"))
                act.activation(y[:, :, ds(i * 512 + hh * P, P)], bank[7][:, 0:T].rearrange("p (b e) -> p b e", b=TB), ACT.Copy)\
                   .then_inc(SEM["o_out"], 1)
                c.count("o_out")

            with c.loop(2, "act att") as i:
                for hh in range(4):
                    exps(hh)
                    if hh:
                        take_output(i, hh - 1)
                    if hh == 1:
                        c.count("gen0")
                        next_units(0)
                    take_turned()
                c.count("gen0")
                next_units(1)
                take_output(i, 3)
            transposed()
            act.wait_ge(SEM["o_out"], c.so_far("o_out"))
            act.activation(osq, y[:, :, :], ACT.Square).then_inc(SEM["o_sq"], 1)
            act.wait_ge(SEM["gen0"], c.so_far("gen0"))
            act.wait_ge(SEM["gen1"], c.so_far("gen1"))
            for g in gate:
                act.activation(g, g, ACT.Sigmoid).then_inc(SEM["gate_on"], 1)
            for br in range(2):
                for p in range(2):
                    c.count(f"gen{p}")
                next_units(0)
                transposed()
                next_units(1)
            next_units(0, 2)
            for p in range(2):
                c.count(f"gen{p}")
            transposed()
            ffn([(0, 2), (1, 2)])
        second_act(c, act, prep, next_units, panel_evac, transposed, ffn)

    @block.vector
    def _(dve):
        c = Counts(dve, SEM["held"])


        def low(s):
            dve.wait_ge(SEM[f"hi{s}"], c.next(f"hi{s}"))
            c.count(f"used{s}")
            dve.tensor_tensor(wl[s][:, :], wf[s][:, :], wh[s][:, :].bitcast(f32), ALU.subtract).then_inc(SEM[f"lo{s}"], 1)

        def next_units(p):
            low(2 * p)
            low(2 * p + 1)

        def transposed(*blocks):
            for r in (2 * b + h for b in blocks or range(TB) for h in range(2)):
                dve.wait_ge(SEM["xt_hi"], c.next("xt_hi"))
                at = slice(4 * (r % 2), 4 * (r % 2) + 4), slice((r // 2) * P, (r // 2 + 1) * P)
                dve.tensor_tensor(xTl[:, at[0], at[1]], bank[6 + r % 2][:, :].rearrange("p (k t) -> p k t", k=4),
                                  xTh[:, at[0], at[1]].bitcast(f32), ALU.subtract).then_inc(SEM["xt_ready"], 1)

        def ffn_step(last, half):
            low(3 if last else 0)
            for b in range(TB):
                dve.wait_ge(SEM["h_silu"], c.next("h_silu"))
                ins = dve.scalar_tensor_tensor(hid[:, b, :], sil[:, b, :], half, bank[4 + b][:, STEP:2 * STEP],
                                               ALU.mult, ALU.mult)
            ins.then_inc(SEM["h_ready"], 1)
            if not last:
                low(1)
            dve.wait_ge(SEM["ht_hi"], c.next("ht_hi"))
            dve.tensor_tensor(hTl[:, :, :], bank[6][:, :].rearrange("p (k t) -> p k t", k=2),
                              hTh[:, :, :].bitcast(f32), ALU.subtract).then_inc(SEM["ht_ready"], 1)
            if not last:
                low(2)

        def ffn(half):
            with c.loop(STEPS - 1, "dve ffn"):
                ffn_step(False, half)
            ffn_step(True, half)

        def moments(src, b):
            for h in range(2):
                ins = dve.bn_stats(stats[:, h, :], src[:, b, h * HALF:(h + 1) * HALF])
            ins.then_inc(SEM["dve"], 1)
            dve.wait_ge(SEM["dve"], c.next("dve"))
            c.hold()
            dve.bn_aggr(mv[:, b, :], stats[:, :, :].rearrange("p a b -> p (a b)")).then_inc(SEM["dve"], 1)
            dve.wait_ge(SEM["dve"], c.next("dve"))
            dve.tensor_scalar(ve[:, b:b + 1], mv[:, b, 1:2], LN_EPS, None, ALU.add).then_inc(SEM["var"], 1)

        def normalise(dst, src, gb, b, to):
            dve.scalar_tensor_tensor(src[:, b, :], src[:, b, :], mv[:, b, 0:1], gb[:, 0, :], ALU.subtract, ALU.mult)\
               .then_inc(SEM["dve"], 1)
            dve.wait_ge(SEM["dve"], c.next("dve"))
            dve.wait_ge(SEM["rstd"], c.next("rstd"))
            dve.scalar_tensor_tensor(dst[:, b, :], src[:, b, :], rstd[:, b:b + 1], gb[:, 1, :], ALU.mult, ALU.add)\
               .then_inc(SEM[to], 1)

        def post_norm(and_transposed=True):
            for b in range(TB):
                if b == 0:
                    dve.wait_ge(SEM["half"], c.next("half"))
                else:
                    dve.wait_ge(SEM["used3"], c.so_far("used3"))
                for h in range(2):
                    ins = dve.scalar_tensor_tensor(y[:, b, h * HALF:(h + 1) * HALF], x[:, b, h * HALF:(h + 1) * HALF],
                                                   ALPHA, bank[2 * b + h][:, :], ALU.mult, ALU.add)
                    if b == TB - 1:
                        ins.then_inc(SEM[f"gen{h}"], 1)
                        dve.wait_ge(SEM[f"gen{h}"], c.next(f"gen{h}"))
                    else:
                        ins.then_inc(SEM["dve"], 1)
                        dve.wait_ge(SEM["dve"], c.next("dve"))
                moments(y, b)
                if b == 0:
                    dve.wait_ge(SEM["gains_ld"], c.next("gains_ld", 32))
                normalise(x, y, gains, b, "x_ready")
                c.count("x_ready")
                if and_transposed:
                    transposed(b)

        dve.wait_ge(SEM["const_ld"], c.next("const_ld", 16 * 6))
        low(0)
        low(1)

        with c.loop(DEPTH, "dve layer") as l:
            transposed()
            ffn(0.5)
            low(0)
            low(1)
            low(2)
            post_norm()
            low(3)
            with c.loop(2, "dve uv"):
                for p in range(2):
                    c.count(f"gen{p}")
                    next_units(p)
            dve.wait_ge(SEM["gen0"], c.so_far("gen0"))
            dve.wait_ge(SEM["gen1"], c.so_far("gen1"))
            dve.wait_ge(SEM["sgu_ld"], c.next("sgu_ld", 16 * 6))
            for b in range(TB):
                moments(v_t, b)
            for b in range(TB):
                normalise(v_t, v_t, sgu_gb, b, "v_ready")
            lam4 = part(14728, 2, 2, HD)
            dve.tensor_tensor(lam4[:, :, 0, :], lam4[:, :, 0, :], lam4[:, :, 1, :], ALU.mult).then_inc(SEM["dve"], 1)
            dve.wait_ge(SEM["dve"], c.next("dve"))
            dve.tensor_reduce(lam_c[:, 0:2], lam4[:, :, 0, :], X, ALU.add).then_inc(SEM["lam_s"], 1)
            with c.loop(2, "dve qk") as i:
                for p in range(2):
                    dve.wait_ge(SEM[f"used{2 * p + 1}"], c.so_far(f"used{2 * p + 1}"))
                    for b in range(TB):
                        src = bank[2 * b + p][:, :].rearrange("p (h m d) -> p h m d", m=2, d=HD // 2)
                        r2 = rope2.rearrange("p (h m d) -> p h m d", m=2, d=HD // 2)
                        cos = cs[:, 0:1, b, :].broadcast_to([P, 8, HD])
                        sin = cs[:, 1:2, b, :].rearrange("p a (m d) -> p a m d", m=2)
                        dve.tensor_tensor(rope1.rearrange("p (h d) -> p h d", d=HD), src.rearrange("p h m d -> p h (m d)"),
                                          cos, ALU.mult)
                        for m in range(2):
                            ins = dve.tensor_tensor(r2[:, :, m, :], src[:, :, 1 - m, :],
                                                    sin[:, :, m, :].broadcast_to([P, 8, HD // 2]), ALU.mult)
                        if b == TB - 1:
                            ins.then_inc(SEM[f"gen{p}"], 1)
                            dve.wait_ge(SEM[f"gen{p}"], c.next(f"gen{p}"))
                        else:
                            ins.then_inc(SEM["dve"], 1)
                            dve.wait_ge(SEM["dve"], c.next("dve"))
                        dve.tensor_tensor(y[:, b, p * HALF:(p + 1) * HALF], rope1, rope2, ALU.add).then_inc(SEM["rope"], 1)
                        dve.wait_ge(SEM["rope"], c.next("rope"))
                    next_units(p)
            dve.wait_ge(SEM["lam_e"], c.next("lam_e"))
            dve.tensor_tensor(lam_c[:, 2:3], lam_c[:, 1:2], lam_c[:, 0:1], ALU.subtract).then_inc(SEM["dve"], 1)
            dve.wait_ge(SEM["dve"], c.next("dve"))
            dve.tensor_tensor(lam_c[:, 2:3], lam_c[:, 2:3], laminit[:, ds(l, 1), 0], ALU.subtract)\
               .then_inc(SEM["dve"], 1)
            dve.wait_ge(SEM["dve"], c.next("dve"))
            for r in range(2):
                dve.wait_ge(SEM["sgw_tr"], c.next("sgw_tr"))
                dve.tensor_tensor(sgu_wT[:, 4 * r:4 * r + 4, :], bank[6 + r][:, :].rearrange("p (g t) -> p g t", g=4),
                                  tri[:, :].rearrange("p (a t) -> p a t", a=1).broadcast_to([P, 4, P]), ALU.mult)\
                   .then_inc(SEM["sgw_ready"], 1)
            c.count("gen0")
            next_units(0)
            for b in range(TB):
                dve.wait_ge(SEM["sgu_mm"], c.next("sgu_mm"))
                for g in range(GROUPS):
                    at = slice(g * P, (g + 1) * P)
                    ins = dve.scalar_tensor_tensor(u_t[:, b, at], bank[4 + 2 * b + g // 4][:, (g % 4) * P:(g % 4 + 1) * P],
                                                   sgu_bT[:, g:g + 1], u_t[:, b, at], ALU.add, ALU.mult)
                ins.then_inc(SEM["ha_ready"], 1)
            c.count("gen1")
            next_units(1)
            dve.wait_ge(SEM["gains_ld"], c.next("gains_ld", 32))
            def maxima(hh):
                dve.wait_ge(SEM[f"s_ready{hh % 2}"], c.next(f"s_ready{hh % 2}"))
                for j in range(4):
                    at = slice(0, P) if j < 2 else slice(P, P + T)
                    ins = dve.tensor_reduce(att[:, j:j + 1], bank[score_banks[hh % 2][j % 2]][:, at], X, ALU.max, negate=True)
                ins.then_inc(SEM["smax"], 1)

            def combine():
                dve.wait_ge(SEM["e_ready"], c.next("e_ready", 4))
                dve.reciprocal(att[:, 8:12], att[:, 4:8]).then_inc(SEM["dve"], 1)
                dve.wait_ge(SEM["dve"], c.next("dve"))
                dve.tensor_scalar(att[:, 9:12:2], att[:, 9:12:2], lam_c[:, 2:3], None, ALU.mult).then_inc(SEM["dve"], 1)
                dve.wait_ge(SEM["dve"], c.next("dve"))
                dve.tensor_scalar(e_t[:, 1, 0:P], e_t[:, 1, 0:P], att[:, 9:10], None, ALU.mult)
                dve.tensor_scalar(e_t[:, 1, P:P + T], e_t[:, 1, P:P + T], att[:, 11:12], None, ALU.mult)\
                   .then_inc(SEM["dve"], 1)
                dve.wait_ge(SEM["dve"], c.next("dve"))
                dve.wait_ge(SEM["a_tr"], c.so_far("a_tr"))
                c.count("a_tr")
                dve.scalar_tensor_tensor(a_t[:, 0:P], e_t[:, 0, 0:P], att[:, 8:9], e_t[:, 1, 0:P], ALU.mult, ALU.add)
                dve.scalar_tensor_tensor(a_t[:, P:P + T], e_t[:, 0, P:P + T], att[:, 10:11], e_t[:, 1, P:P + T],
                                         ALU.mult, ALU.add).then_inc(SEM["a_ready"], 1)

            def gate_panel(i, p):
                dve.wait_ge(SEM[f"used{2 * p + 1}"], c.so_far(f"used{2 * p + 1}"))
                for b in range(TB):
                    ins = dve.tensor_tensor(arena[:, ds(i * 8192 + 2048 + b * D + p * HALF, HALF)], bank[2 * b][:, :],
                                            gains[:, ds(i, 1), p * HALF:(p + 1) * HALF].rearrange("p a n -> p (a n)"), ALU.add)
                ins.then_inc(SEM["gen0"], 1)
                c.count("gen0")

            with c.loop(2, "dve att") as i:
                for hh in range(4):
                    maxima(hh)
                    if hh == 2:
                        low(0)
                    combine()
                    if hh == 1:
                        gate_panel(i, 0)
                    if hh == 2:
                        low(1)
                gate_panel(i, 1)
                low(2)
                low(3)
            transposed()
            dve.wait_ge(SEM["o_sq"], c.next("o_sq"))
            dve.tensor_reduce(oss, part(4096, 16, P), X, ALU.add).then_inc(SEM["dve"], 1)
            dve.wait_ge(SEM["dve"], c.next("dve"))
            dve.tensor_scalar(oss, oss, 1.0 / P, LN_EPS, ALU.mult, ALU.add).then_inc(SEM["o_var"], 1)
            dve.wait_ge(SEM["o_rstd"], c.next("o_rstd"))
            dve.tensor_scalar(orstd, orstd, laminit[:, ds(l, 1), 1], None, ALU.mult).then_inc(SEM["dve"], 1)
            dve.wait_ge(SEM["dve"], c.next("dve"))
            yh = y[:, :, :].rearrange("p b (h e) -> p (b h) e", e=P)
            for b in range(TB):
                hs = slice(8 * b, 8 * b + 8)
                dve.tensor_tensor(yh[:, hs, :], yh[:, hs, :],
                                  orstd[:, hs].rearrange("p (h a) -> p h a", a=1).broadcast_to([P, 8, P]), ALU.mult)\
                   .then_inc(SEM["dve"], 1)
                dve.wait_ge(SEM["dve"], c.next("dve"))
                dve.tensor_tensor(yh[:, hs, :], yh[:, hs, :], dgain.rearrange("p (a e) -> p a e", a=1).broadcast_to([P, 8, P]),
                                  ALU.mult).then_inc(SEM["hb_ready"], 1)
            dve.wait_ge(SEM["gate_on"], c.next("gate_on", 2))
            for br in range(2):
                for p in range(2):
                    dve.wait_ge(SEM[f"used{2 * p + 1}"], c.so_far(f"used{2 * p + 1}"))
                    for b in range(TB):
                        g = gate[br][:, b, p * HALF:(p + 1) * HALF]
                        ins = dve.tensor_tensor(g, g, bank[2 * b + p][:, :], ALU.mult)
                    ins.then_inc(SEM[f"gen{p}"], 1)
                    dve.wait_ge(SEM[f"gen{p}"], c.next(f"gen{p}"))
                    if p == 0:
                        next_units(0)
                for b in range(TB):
                    if br:
                        dve.tensor_tensor(gate[0][:, b, :], gate[0][:, b, :], gate[1][:, b, :], ALU.add)\
                           .then_inc(SEM["m_ready"], 1)
                    transposed(b)
                next_units(1)
            next_units(0)
            post_norm()
            ffn(0.5)
            next_units(0)
            post_norm(False)
        second_dve(c, dve, low, next_units, transposed, ffn, moments)

    @block.tensor
    def _(pe):
        c = Counts(pe, SEM["held"])

        def three(o, lh, ll, rh, rl, start, stop):
            pe.matmul(o, lh, rh, start=start, stop=False)
            pe.matmul(o, lh, rl, start=False, stop=False)
            return pe.matmul(o, ll, rh, start=False, stop=stop)

        def up_unit(s, h, out0, blocks=(0, 1), half=False, tiles=(0, 1, 2, 3)):
            if 0 in blocks and 0 in tiles:
                pe.wait_ge(SEM[f"lo{s}"], c.next(f"lo{s}"))
            steps = [(b, q) for b in blocks for q in tiles] if half else [(b, q) for q in tiles for b in blocks]
            for b, q in steps:
                k = 4 * h + q
                r = slice(q * HALF, (q + 1) * HALF)
                t = slice(b * P, (b + 1) * P)
                ins = three(out0(b), xTh[:, k, t], xTl[:, k, t], wh[s][:, r], wl[s][:, r], k == 0, k == KT - 1)
                if half and (b, q) == (0, 3):
                    ins.then_inc(SEM["half"], 1)
            if TB - 1 in blocks:
                ins.then_inc(SEM[f"used{s}"], 1)

        def panel_unit(p, h, at=None, half=False):
            at = p if at is None else at
            if h == 0:
                pe.wait_ge(SEM[f"gen{at}"], c.so_far(f"gen{at}"))
                c.count(f"gen{at}")
            up_unit(2 * p + h, h, lambda b: bank[2 * b + at][:, :], half=half)

        def panel(p, half=False):
            panel_unit(p, 0)
            panel_unit(p, 1, half=half)

        def up():
            for h in range(2):
                up_unit(h, h, lambda b: bank[4 + b][:, :])

        def down(first, last):
            if first:
                for p in range(2):
                    pe.wait_ge(SEM[f"gen{p}"], c.so_far(f"gen{p}"))
                    c.count(f"gen{p}")
            pe.wait_ge(SEM["ht_ready"], c.next("ht_ready"))
            s = 3 if last else 2
            pe.wait_ge(SEM[f"lo{s}"], c.next(f"lo{s}"))
            for b in range(TB):
                t = slice(b * P, (b + 1) * P)
                for k in range(2):
                    for n in range(2):
                        r = slice(k * D + n * HALF, k * D + (n + 1) * HALF)
                        ins = three(bank[2 * b + n][:, :], hTh[:, k, t], hTl[:, k, t], wh[s][:, r], wl[s][:, r],
                                    first and k == 0, last and k == 1)
                if last and b == 0:
                    ins.then_inc(SEM["half"], 1)
            ins.then_inc(SEM[f"used{s}"], 1)

        def hidden():
            pe.wait_ge(SEM["h_ready"], c.next("h_ready"))
            for k in range(2):
                for b in range(TB):
                    ins = pe.transpose(bank[6][:, k * T + b * P:k * T + (b + 1) * P], hid[:, b, k * P:(k + 1) * P], ident[:, :])
            ins.then_inc(SEM["ht_tr"], 1)

        def ffn():
            hidden()
            up()
            down(True, False)
            hidden()
            with c.loop(STEPS - 2, "pe ffn"):
                up()
                down(False, False)
                hidden()
            down(False, True)

        def enter(src, ready, to_panel):
            def turn(b):
                if ready:
                    pe.wait_ge(SEM[ready], c.next(ready))
                for r in range(2):
                    for q in range(4):
                        k = 4 * r + q
                        ins = pe.transpose(bank[6 + r][:, q * P:(q + 1) * P],
                                           src(b, k) if callable(src) else src[:, b, k * P:(k + 1) * P], ident[:, :])
                    ins.then_inc(SEM["tr"], 1)

            def products(b, h, *tiles):
                up_unit(h, h, lambda b: bank[2 * b if to_panel else 4 + b][:, :], (b,), tiles=tiles)

            turn(0)
            if to_panel:
                pe.wait_ge(SEM["gen0"], c.so_far("gen0"))
                c.count("gen0")
            pe.wait_ge(SEM["xt_ready"], c.next("xt_ready"))
            products(0, 0, 0, 1, 2, 3)
            pe.wait_ge(SEM["xt_ready"], c.next("xt_ready"))
            products(0, 1, 0, 1)
            turn(1)
            products(0, 1, 2, 3)
            for h in range(2):
                pe.wait_ge(SEM["xt_ready"], c.next("xt_ready"))
                products(1, h, 0, 1, 2, 3)

        def turn_panel(n):
            for b in range(TB):
                pe.wait_ge(SEM["rope"], c.next("rope"))
                if 0 < n < 3:
                    pe.wait_ge(SEM["qk_ready"], c.next("qk_ready"))
                for q in range(4):
                    ins = pe.transpose(bank[6 + b][:, q * P:(q + 1) * P],
                                       y[:, b, (n % 2) * HALF + q * P:(n % 2) * HALF + (q + 1) * P], ident[:, :])
                ins.then_inc(SEM["rope_tr"], 1)

        pe.wait_ge(SEM["const_ld"], c.next("const_ld", 16 * 6))
        pe.wait_ge(SEM["x_ld"], c.next("x_ld", 32))
        c.seen["x_ready"] = 1

        with c.loop(DEPTH, "pe layer") as l:
            enter(x, "x_ready", False)
            ffn()
            enter(x, "x_ready", True)
            panel(1)
            panel(0)
            panel(1)
            for n in range(4):
                panel(n % 2)
                if n:
                    turn_panel(n - 1)
            pe.wait_ge(SEM["qk_ready"], c.next("qk_ready", 2))
            pe.wait_ge(SEM["sgu_ld"], c.next("sgu_ld", 16 * 6))
            for r in range(2):
                for q in range(4):
                    ins = pe.transpose(bank[6 + r][:, q * P:(q + 1) * P], sgu_w[:, 4 * r + q, :], ident[:, :])
                ins.then_inc(SEM["sgw_tr"], 1)
            panel(0)
            pe.wait_ge(SEM["sgw_ready"], c.next("sgw_ready", 2))
            turn_panel(3)
            pe.wait_ge(SEM["qk_ready"], c.next("qk_ready", 2))
            for b in range(TB):
                pe.wait_ge(SEM["v_ready"], c.next("v_ready"))
                for g in range(GROUPS):
                    ins = pe.matmul(bank[4 + 2 * b + g // 4][:, (g % 4) * P:(g % 4 + 1) * P], sgu_wT[:, g, :],
                                    v_t[:, b, g * P:(g + 1) * P], start=True, stop=True)
                ins.then_inc(SEM["sgu_mm"], 1)
            panel(1)
            pe.wait_ge(SEM["ha_ready"], c.next("ha_ready", 2))
            pe.wait_ge(SEM["gen0"], c.so_far("gen0"))
            pe.wait_ge(SEM["gen1"], c.so_far("gen1"))
            def scores(hh):
                q = hh % 2
                pe.wait_ge(SEM["qh_ready"], c.next("qh_ready"))
                for m in range(2):
                    f = slice(m * HD, (m + 1) * HD)
                    o = bank[score_banks[q][m]]
                    pe.matmul(o[:, 0:P], qh[q][f, 0:P], kh[q][f, 0:P], start=True, stop=False)
                    pe.matmul(o[:, 0:P], identb, negm, start=False, stop=True)
                    pe.matmul(o[:, P:P + T], qh[q][f, P:T], kh[q][f, 0:T], start=True, stop=False)
                    ins = pe.matmul(o[:, T:P + T], identb, negm, start=False, stop=True)
                ins.then_inc(SEM[f"s_ready{q}"], 1)

            def turn():
                pe.wait_ge(SEM["a_ready"], c.next("a_ready"))
                for j in range(3):
                    ins = pe.transpose(bank[6][:, j * P:(j + 1) * P], a_t[:, j * P:(j + 1) * P], ident[:, :])
                ins.then_inc(SEM["a_tr"], 1)

            def outputs(i, hh):
                pe.wait_ge(SEM["aT_ready"], c.next("aT_ready"))
                pe.wait_ge(SEM["o_out"], c.so_far("o_out"))
                c.count("o_out")
                ve_ = [val[:, b, ds(i * 512 + hh * P, P)] for b in range(TB)]
                pe.matmul(bank[7][:, 0:P], aT[:, 0, :], ve_[0], start=True, stop=True)
                pe.matmul(bank[7][:, P:T], aT[:, 1, :], ve_[0], start=True, stop=False)
                pe.matmul(bank[7][:, P:T], aT[:, 2, :], ve_[1], start=False, stop=True).then_inc(SEM["o_ready"], 1)

            with c.loop(2, "pe att") as i:
                for hh in range(4):
                    scores(hh)
                    if hh:
                        turn()
                    panel_unit(hh // 2, hh % 2, 0)
                    if hh:
                        outputs(i, hh - 1)
                turn()
                outputs(i, 3)
            pe.wait_ge(SEM["o_out"], c.so_far("o_out"))
            enter(u_t, None, True)
            panel(1)
            enter(y, "hb_ready", True)
            panel(1)
            enter(gate[0], "m_ready", True)
            panel(1, True)
            enter(x, "x_ready", False)
            ffn()
        c.count("x_ready", TB)
        second_pe(c, pe, three, panel, panel_unit, enter, turn_panel, ffn)
    ctx.close()


def constants():
    f = np.float32

    def bf16(t):
        return (t.astype(f).view(np.uint32) >> 16).astype(np.uint16).view(f)

    pos = np.arange(T, dtype=f)
    inv = (f(ROPE_THETA) ** (-np.arange(0, HD, 2, dtype=f) / f(HD))).astype(f)
    ang = pos[:, None] * inv[None, :]
    cos, sin = np.cos(ang).astype(f), np.sin(ang).astype(f)
    rope = np.stack([np.concatenate([cos, cos], 1), np.concatenate([-sin, sin], 1)])
    r = np.arange(P)
    lam = np.array([0.8 - 0.6 * math.exp(-0.3 * l) for l in range(DEPTH)])
    tok, head = r // RH, r % RH
    same = head[:, None] == head[None, :]
    s_lt, s_le, s_gt = ((op(tok[:, None], tok[None, :]) & same).astype(f) for op in (np.less, np.less_equal, np.greater))
    masks = [s_lt, s_le, s_gt, -s_le, -s_lt, -s_gt, s_le, s_lt,
             (head[:, None] == np.arange(RH)[None, :]).astype(f), (r[:, None] // CH == np.arange(RH)[None, :]).astype(f)]
    return {
        "c_pairs": (head[None, None, :] == 2 * np.arange(4)[None, :, None] + (r // HD)[:, None, None]).astype(f),
        "c_masks": np.concatenate(masks, 1),
        "c_sel": np.broadcast_to(np.eye(FOX, dtype=f)[:, :, None], (FOX, FOX, P)).copy(),
        "c_ones": np.ones((P, P), f),
        "c_ident": np.eye(P, dtype=f),
        "c_mhalf": np.concatenate([np.full((P, P), -0.5, f), np.full((P, 1), HD ** -0.5, f)], 1),
        "c_rope": np.ascontiguousarray(rope.reshape(2, TB, P, HD).transpose(2, 0, 1, 3)),
        "c_tri": (r[:, None] <= r[None, :]).astype(f),
        "c_laminit": np.ascontiguousarray(np.broadcast_to(np.stack([lam, 1 - lam], 1).astype(f), (P, DEPTH, 2))),
        "c_negm": bf16(np.concatenate([np.zeros((P, P)), np.where(r[None, :] <= r[:, None], 0, NEG)], 1)),
        "c_identb": bf16(np.eye(P)),
    }


def kernel(**inputs):
    import concourse.bacc as bacc
    from concourse.bass_utils import run_bass_kernel_spmd

    nc = bacc.Bacc("TRN2", target_bir_lowering=False, num_devices=1)
    arrays = {n: np.ascontiguousarray(v) for n, v in inputs.items() if n in USED}
    arrays.update(constants())
    f32 = mybir.dt.float32
    a = {n: nc.dram_tensor(f"in_{n}", v.shape, f32, kind="ExternalInput").ap() for n, v in arrays.items()}
    out = nc.dram_tensor("out", (1, T, D), f32, kind="ExternalOutput").ap()
    program(nc, a, out)
    got = run_bass_kernel_spmd(nc, [{f"in_{n}": v for n, v in arrays.items()}], core_ids=[0])
    return got.results[0]["out"]
```
